# Optimizing a Trainium2 kernel written in Bass

```python
import jax, jax.numpy as jnp
from jax import lax
import numpy as np
import math

D_MODEL = 1024
BATCH = 1
SEQ = 1024
DEPTH = 1

N_META = 16
GRID_W = 64
HEAD_DIM = 64
N_Q_HEADS = 8
N_KV_HEADS = 2
GQA_GROUP = N_Q_HEADS // N_KV_HEADS
ATTN_WIDTH = N_Q_HEADS * HEAD_DIM
KV_WIDTH = N_KV_HEADS * HEAD_DIM
FOURIER_GROUPS = 8
FOURIER_GROUP_DIM = 64
FOURIER_WIDTH = FOURIER_GROUPS * FOURIER_GROUP_DIM
MIX_WIDTH = FOURIER_WIDTH + ATTN_WIDTH
IN_WIDTH = 2 * FOURIER_WIDTH + ATTN_WIDTH + 2 * KV_WIDTH + ATTN_WIDTH
SPLIT_POINTS = (FOURIER_WIDTH, 2 * FOURIER_WIDTH, 2 * FOURIER_WIDTH + ATTN_WIDTH,
                2 * FOURIER_WIDTH + ATTN_WIDTH + KV_WIDTH,
                2 * FOURIER_WIDTH + ATTN_WIDTH + 2 * KV_WIDTH)
Q_BLOCK = 128
ROPE_THETA = 10000.0
AXIS_ROT_DIM = HEAD_DIM // 2
AXIS_N_FREQ = AXIS_ROT_DIM // 2
EPS = 1e-6


def rmsnorm(x, g):
    xf = x.astype(jnp.float32)
    y = xf * lax.rsqrt(jnp.mean(xf * xf, axis=-1, keepdims=True) + EPS)
    return (y * g.astype(jnp.float32)).astype(x.dtype)

def axial_rope_tables(n_tok):
    rows = n_tok // GRID_W
    j = jnp.arange(n_tok, dtype=jnp.int32)
    row = (j // GRID_W - rows // 2).astype(jnp.float32)
    col = (j % GRID_W - GRID_W // 2).astype(jnp.float32)
    freqs = 1.0 / (ROPE_THETA ** (jnp.arange(AXIS_N_FREQ, dtype=jnp.float32) * 2.0 / AXIS_ROT_DIM))
    ang = jnp.concatenate([row[:, None] * freqs, col[:, None] * freqs], axis=-1)
    ang = jnp.concatenate([jnp.zeros((N_META, HEAD_DIM // 2), jnp.float32), ang], axis=0)
    return jnp.cos(ang), jnp.sin(ang)

def apply_rope(x, cos, sin):
    b, h, l, d = x.shape
    xf = x.astype(jnp.float32).reshape(b, h, l, d // 2, 2)
    x0, x1 = xf[..., 0], xf[..., 1]
    out = jnp.stack([x0 * cos - x1 * sin, x0 * sin + x1 * cos], axis=-1)
    return out.reshape(b, h, l, d).astype(x.dtype)

def gqa_block(q_blk, k, v):
    s = jnp.einsum('bkgqd,bksd->bkgqs', q_blk, k).astype(jnp.float32) * (HEAD_DIM ** -0.5)
    p = jax.nn.softmax(s, axis=-1)
    return jnp.einsum('bkgqs,bksd->bkgqd', p.astype(v.dtype), v)

def fourier_branch(f_in, w_fmix, b_fmix):
    b, l, _ = f_in.shape
    f = f_in.reshape(b, l, FOURIER_GROUPS, FOURIER_GROUP_DIM).astype(jnp.float32)
    fr = jnp.real(jnp.fft.fftn(f, axes=(1, 3), norm='ortho')).astype(f_in.dtype)
    out = jnp.einsum('blgc,gcd->blgd', fr, w_fmix) + b_fmix
    return out.reshape(b, l, FOURIER_WIDTH)

def attention_branch(q, k, v, q_g, k_g, cos, sin, n_tok):
    b, l, _ = q.shape
    q = q.reshape(b, l, N_Q_HEADS, HEAD_DIM).transpose(0, 2, 1, 3)
    k = k.reshape(b, l, N_KV_HEADS, HEAD_DIM).transpose(0, 2, 1, 3)
    v = v.reshape(b, l, N_KV_HEADS, HEAD_DIM).transpose(0, 2, 1, 3)
    q = apply_rope(rmsnorm(q, q_g), cos, sin)
    k = apply_rope(rmsnorm(k, k_g), cos, sin)
    q = q.reshape(b, N_KV_HEADS, GQA_GROUP, l, HEAD_DIM)
    out_meta = gqa_block(q[:, :, :, :N_META], k, v)
    n_blk = n_tok // Q_BLOCK
    q_real = q[:, :, :, N_META:].reshape(b, N_KV_HEADS, GQA_GROUP, n_blk, Q_BLOCK, HEAD_DIM)
    q_real = q_real.transpose(3, 0, 1, 2, 4, 5)
    out_real = lax.map(lambda qb: gqa_block(qb, k, v), q_real)
    out_real = out_real.transpose(1, 2, 3, 0, 4, 5).reshape(b, N_KV_HEADS, GQA_GROUP, n_tok, HEAD_DIM)
    out = jnp.concatenate([out_meta, out_real], axis=3).reshape(b, N_Q_HEADS, l, HEAD_DIM)
    return out.transpose(0, 2, 1, 3).reshape(b, l, ATTN_WIDTH)

def first_inputs(seed: int = 0) -> dict:
    key = jax.random.key(seed)
    ks = jax.random.split(key, 10)
    f32 = jnp.float32
    x = jax.random.normal(ks[0], (BATCH, SEQ, D_MODEL), f32)
    meta_tokens = jax.random.normal(ks[1], (N_META, D_MODEL), f32)
    norm_g = 1.0 + 0.05 * jax.random.normal(ks[2], (DEPTH, D_MODEL), f32)
    w_in = jax.random.normal(ks[3], (DEPTH, D_MODEL, IN_WIDTH), f32) * D_MODEL ** -0.5
    w_fmix = jax.random.normal(ks[4], (DEPTH, FOURIER_GROUPS, FOURIER_GROUP_DIM, FOURIER_GROUP_DIM), f32) * FOURIER_GROUP_DIM ** -0.5
    b_fmix = 0.02 * jax.random.normal(ks[5], (DEPTH, FOURIER_GROUPS, FOURIER_GROUP_DIM), f32)
    q_norm_g = 1.0 + 0.05 * jax.random.normal(ks[6], (DEPTH, HEAD_DIM), f32)
    k_norm_g = 1.0 + 0.05 * jax.random.normal(ks[7], (DEPTH, HEAD_DIM), f32)
    w_out = jax.random.normal(ks[8], (DEPTH, MIX_WIDTH, D_MODEL), f32) * MIX_WIDTH ** -0.5
    final_g = 1.0 + 0.05 * jax.random.normal(ks[9], (D_MODEL,), f32)
    return {"x": x, "meta_tokens": meta_tokens, "norm_g": norm_g, "w_in": w_in,
            "w_fmix": w_fmix, "b_fmix": b_fmix, "q_norm_g": q_norm_g, "k_norm_g": k_norm_g,
            "w_out": w_out, "final_g": final_g}

def first_block(x, meta_tokens, norm_g, w_in, w_fmix, b_fmix, q_norm_g, k_norm_g, w_out, final_g):
    b, n_tok, d = x.shape
    cos, sin = axial_rope_tables(n_tok)
    meta = jnp.broadcast_to(meta_tokens.astype(x.dtype)[None], (b, N_META, d))
    h = jnp.concatenate([meta, x], axis=1)
    for i in range(DEPTH):
        u = rmsnorm(h, norm_g[i])
        proj = jnp.einsum('bld,de->ble', u, w_in[i])
        f_in, f_gate, q, k, v, a_gate = jnp.split(proj, SPLIT_POINTS, axis=-1)
        f_out = fourier_branch(f_in, w_fmix[i], b_fmix[i]) * jax.nn.silu(f_gate)
        a_out = attention_branch(q, k, v, q_norm_g[i], k_norm_g[i], cos, sin, n_tok) * jax.nn.silu(a_gate)
        mixed = jnp.concatenate([f_out, a_out], axis=-1)
        h = h + jnp.einsum('ble,ed->bld', mixed, w_out[i])
    h = rmsnorm(h, final_g)
    return h[:, N_META:]


ATT_HEADS = 8
ATT_WIDTH = ATT_HEADS * HEAD_DIM
CONV_GROUPS = 8
CONV_WIDTH = D_MODEL - ATT_WIDTH
CONV_K = 3
FFN_CONV_K = 3
D_FF = 2816
RMS_EPS = 1e-6
IN_COLS = 3 * ATT_WIDTH + 3 * CONV_WIDTH + 2 * D_MODEL
IN_SPLITS = (ATT_WIDTH, 2 * ATT_WIDTH, 3 * ATT_WIDTH,
             3 * ATT_WIDTH + CONV_WIDTH, 3 * ATT_WIDTH + 2 * CONV_WIDTH,
             3 * ATT_WIDTH + 3 * CONV_WIDTH, 3 * ATT_WIDTH + 3 * CONV_WIDTH + D_MODEL)


def rms_norm(x, g):
    xf = x.astype(jnp.float32)
    var = jnp.mean(xf * xf, axis=-1, keepdims=True)
    return (xf * lax.rsqrt(var + RMS_EPS) * g.astype(jnp.float32)).astype(x.dtype)

def causal_dwconv(u, w):
    kw = w.shape[0]
    s = u.shape[1]
    up = jnp.pad(u, ((0, 0), (kw - 1, 0), (0, 0)))
    y = up[:, 0:s, :] * w[0]
    for i in range(1, kw):
        y = y + up[:, i:i + s, :] * w[i]
    return y

def stick_breaking_attention(q, k, v):
    _, _, s, dh = q.shape
    scale = 1.0 / math.sqrt(dh)
    outs = []
    for blk in range(s // Q_BLOCK):
        t0 = blk * Q_BLOCK
        t1 = t0 + Q_BLOCK
        qb = q[:, :, t0:t1]
        kb = k[:, :, :t1]
        vb = v[:, :, :t1]
        z = jnp.einsum("bhqd,bhkd->bhqk", qb, kb).astype(jnp.float32) * scale
        t_idx = t0 + jnp.arange(Q_BLOCK)[:, None]
        s_idx = jnp.arange(t1)[None, :]
        strict = s_idx < t_idx
        log_keep = jnp.where(strict, jax.nn.log_sigmoid(-z), 0.0)
        later = lax.cumsum(log_keep, axis=3, reverse=True) - log_keep
        w = jnp.where(strict, jnp.exp(jax.nn.log_sigmoid(z) + later), 0.0)
        outs.append(jnp.einsum("bhqk,bhkd->bhqd", w, vb.astype(jnp.float32)))
    return jnp.concatenate(outs, axis=2).astype(q.dtype)

def second_inputs(seed: int = 0) -> dict:
    key = jax.random.key(seed)
    ks = jax.random.split(key, 14)
    f32 = jnp.float32

    def nrm(k, shape, fan_in):
        return jax.random.normal(k, shape, f32) * (fan_in ** -0.5)

    def gain(k):
        return 1.0 + 0.05 * jax.random.normal(k, (DEPTH, D_MODEL), f32)

    return {
        "x": jax.random.normal(ks[0], (BATCH, SEQ, D_MODEL), f32),
        "norm_mix_pre": gain(ks[1]),
        "w_in": nrm(ks[2], (DEPTH, D_MODEL, IN_COLS), D_MODEL),
        "conv_mix_w": nrm(ks[3], (DEPTH, CONV_K, CONV_WIDTH), CONV_K),
        "w_att_branch": nrm(ks[4], (DEPTH, ATT_WIDTH, D_MODEL), ATT_WIDTH),
        "w_conv_branch": nrm(ks[5], (DEPTH, CONV_WIDTH, D_MODEL), CONV_WIDTH),
        "w_out": nrm(ks[6], (DEPTH, D_MODEL, D_MODEL), D_MODEL),
        "norm_mix_post": gain(ks[7]),
        "norm_ffn_pre": gain(ks[8]),
        "w_up": nrm(ks[9], (DEPTH, D_MODEL, 2 * D_FF), D_MODEL),
        "conv_ffn_w": nrm(ks[10], (DEPTH, FFN_CONV_K, 2 * D_FF), FFN_CONV_K),
        "w_down": nrm(ks[11], (DEPTH, D_FF, D_MODEL), D_FF),
        "norm_ffn_post": gain(ks[12]),
    }

def second_block(x, norm_mix_pre, w_in, conv_mix_w, w_att_branch, w_conv_branch, w_out,
              norm_mix_post, norm_ffn_pre, w_up, conv_ffn_w, w_down, norm_ffn_post):
    b, s, _ = x.shape
    for l in range(DEPTH):
        h = rms_norm(x, norm_mix_pre[l])
        proj = h @ w_in[l]
        q, k, v, cb, cc, cx, g_att, g_conv = jnp.split(proj, IN_SPLITS, axis=-1)

        def heads(t):
            return t.reshape(b, s, ATT_HEADS, HEAD_DIM).transpose(0, 2, 1, 3)

        o = stick_breaking_attention(heads(q), heads(k), heads(v))
        y_att = o.transpose(0, 2, 1, 3).reshape(b, s, ATT_WIDTH) @ w_att_branch[l]

        y_conv = (cb * causal_dwconv(cc * cx, conv_mix_w[l])) @ w_conv_branch[l]

        merged = jax.nn.sigmoid(g_att) * y_att + jax.nn.sigmoid(g_conv) * y_conv
        x = x + rms_norm(merged @ w_out[l], norm_mix_post[l])

        h = rms_norm(x, norm_ffn_pre[l])
        u = causal_dwconv(h @ w_up[l], conv_ffn_w[l])
        a, g = jnp.split(u, 2, axis=-1)
        f = (jax.nn.gelu(g, approximate=True) * a) @ w_down[l]
        x = x + rms_norm(f, norm_ffn_post[l])
    return x


def setup_inputs(seed=0):
    out = dict(first_inputs(seed))
    for name, value in second_inputs(seed + 1).items():
        if name != "x":
            out[name + "_2"] = value
    return out


def reference(
    x, meta_tokens, norm_g, w_in, w_fmix, b_fmix, q_norm_g, k_norm_g, w_out, final_g,
    norm_mix_pre_2, w_in_2, conv_mix_w_2, w_att_branch_2, w_conv_branch_2, w_out_2,
    norm_mix_post_2, norm_ffn_pre_2, w_up_2, conv_ffn_w_2, w_down_2, norm_ffn_post_2,
):
    x = first_block(
        x, meta_tokens, norm_g, w_in, w_fmix, b_fmix, q_norm_g, k_norm_g, w_out, final_g,
    )
    return second_block(
        x, norm_mix_pre_2, w_in_2, conv_mix_w_2, w_att_branch_2, w_conv_branch_2, w_out_2,
        norm_mix_post_2, norm_ffn_pre_2, w_up_2, conv_ffn_w_2, w_down_2, norm_ffn_post_2,
    )


_drawn_inputs = setup_inputs


def setup_inputs(seed=0):
    import zlib

    import numpy as np

    out = dict(_drawn_inputs(seed))
    spreads = {}
    factors = {'b_fmix': 4.271, 'q_norm_g': 8.0, 'k_norm_g': 8.0}
    for name, (base, spread) in spreads.items():
        noise = np.random.default_rng([zlib.crc32(name.encode()), seed]).standard_normal(out[name].shape)
        drawn = base * np.exp(spread * noise) if base else spread * noise
        out[name] = __import__('jax').numpy.asarray(drawn.astype(out[name].dtype))
    for name, factor in factors.items():
        out[name] = (out[name] * factor).astype(out[name].dtype)
    return out
```

```python
from contextlib import ExitStack

import concourse.bass as bass
import numpy as np
from concourse import mybir

F32 = mybir.dt.float32
F32R = mybir.dt.float32r
ALU = mybir.AluOpType
ACT = mybir.ActivationFunctionType
AX = mybir.AxisListType.X

P = 128
D = 1024
KT = D // P
N_TOK = 1024
TT = N_TOK // P
META = 16
POS = N_TOK + META
EPS = 1e-6
DH = 64
HEADS = 8
KV_HEADS = 2
GROUP = HEADS // KV_HEADS
FW = 512
FOLD = POS // 2
FOLDS = 522
NF = 5
REST = {0: FOLD + 1 - 4 * P, 1: FOLD - 1 - 4 * P}
HALF = FOLD // 2
SLOT = 4 * HALF
WCH = 1024
KEYS = 1044
KPART = KEYS // 3
KTILES = 9
FF = 2816
FT = FF // P
NEG = -1.0e30
VROWS = FT * 2 + 4 + 4
GATE1 = 1792

C_FIN = 0
C_DFT = C_FIN + 4
C_FGATE = C_DFT + 4
C_KV = C_FGATE + 4
C_Q = C_KV + 2
C_AGATE = C_Q + 4
C_OUT = C_AGATE + 4
C_V2 = C_OUT + 8
C_QK2 = C_V2 + 4
C_CONV = C_QK2 + 8
C_MRG = C_CONV + 12
C_OUT2 = C_MRG + 24
C_UP = C_OUT2 + 8
C_DOWN = C_UP + 2 * FT
C_END = C_DOWN + 2 * FT

T_FIN = 0
T_DFT = T_FIN + 2 * NF
T_KV = T_DFT + 32
T_Q = T_KV + KTILES
T_OUT = T_Q + TT
T_V2 = T_OUT + 2 * TT
T_OUT2 = T_V2 + TT
U_FGATE = 0
U_AGATE = 4
U_QK2 = 8
U_CONV = 16
U_MRG = 28
U_UP = U_MRG + 32

N_U = 0
N_A1 = N_U + KTILES
N_A2 = N_A1 + KTILES
N_A3 = N_A2 + TT
N_A4 = N_A3 + TT


def tm_signals():
    groups = [(2 * NF, C_FIN + 4)]
    for h in range(2):
        groups += [(4, C_DFT + 2 * h + 1), (4, C_DFT + 2 * h + 2), (8, None)]
    groups += [(KTILES, C_KV + 2), (TT, C_Q + 4), (TT, C_OUT + 4), (TT, C_OUT + 8), (TT, C_V2 + 4),
               (TT, C_OUT2 + 4), (TT, C_OUT2 + 8)]
    out, count = [], 0
    for units, used in groups:
        for u in range(units):
            if used is not None and u == units - 1:
                out.append(("w_used", used))
            else:
                count += 1
                out.append(("tm_mm", count))
    return out


SEMS = """
zero_set w_staged0 w_staged1 w_hi w_split w_used tm_mm tm_free fm_free nt_in0 nt_in1 nt_xn nt_mm nt_hi nt_free
v_chain a_chain rs_ss rs_y consts vec_zero vec_in vec_t vec_done rope_in cw_zero cw_in cw_mm cw_hi cw_done
fold_sum fold_hi fold_done fpad tm_hi tail_in tail_hi tail_done ch_a ch_out
gate_exp gate_out gate_stored vv_set
pr_sq pr_rope pr_t pr_hi pr_done kv_khh kv_kll kv_vhi kdup
sc_mm sc_max sc_exp pt_mm pt_zero pt_hi pt_lo av_mm ag_in0 ag_in1 o_out o_hi o_lo
mf_in mf_hi mf_done op_in0 op_in1 gains_in x1_out x1_stored
st_a st_v z_mm z_l z_e z_w wt_mm wt_hi wt_lo av2_mm at_out ones_set
at_hi at_done cv_pad cv_cc cv_out cv_hi cv_done mg_exp mg_out mg_st0 mg_st1 mr_in0 mr_in1 mr_hi mr_done
gains2_in xr_in0 xr_in1 x2_out x2_stored
up_c up_s up_g up_f dn_hi dn_lo dn_ya dn_yv gains3_in xf_in0 xf_in1 f_out f_stored
""".split()


def two_block_kernel(nc, a, const, scratch, out):
    ctx = ExitStack()
    with ctx:
        S = {name: ctx.enter_context(nc.semaphore(name)) for name in SEMS}
        TM = tm_signals()
        base = (nc.sbuf_base + 63) // 64 * 64

        def at(name, shape, first, dt=F32):
            size = int(np.prod(shape[1:]))
            assert first + size <= TOP, (name, first + size, TOP)
            return nc.alloc_sbuf_tensor_at(name, shape, dt, offset=base + 4 * first)

        TOP = (nc.sbuf_top - base) // 4

        WS = at("w_staging", [P, 2, SLOT], 0)
        WR = at("w_ring", [P, 4, 2, SLOT], 2 * SLOT, F32R)
        c0 = 10 * SLOT
        IDENT = at("ident", [P, P], c0)
        VEC = at("vectors", [P, 3, VROWS], c0 + 128)
        SS = at("sumsq", [P, 16], c0 + 288)
        LN = at("ln", [P, 16], c0 + 304)
        YY = at("rsqrt_guess", [P, 16], c0 + 320)
        MM = at("mean", [P, 16], c0 + 336)
        YA = at("newton_a", [P, 16], c0 + 352)
        YB = at("newton_b", [P, 16], c0 + 368)
        RSTD = at("rstd", [P, 16], c0 + 384)
        RX = at("rstd_x", [P, 16], c0 + 400)
        ZERO = at("zero", [P, 8], c0 + 688)
        MX = at("row_max", [P, 2], c0 + 416)
        NB = at("minus_max", [P, 2], c0 + 424)
        MASK = at("causal_masks", [P, 2, P], c0 + 432)
        c1 = c0 + 696
        ROPE = at("rope", [P, 4, KTILES, DH], c1)
        A0 = c1 + 4 * KTILES * DH
        R1 = A0
        R2 = A0 + 17408
        assert TOP - R2 >= 22400 - 64, TOP - R2

        XIN, XN, GB = {}, {}, {}
        for block_uses, first in (((N_U, N_A1), R2 + 10240), ((N_A2, N_A3, N_A4), R2 + 8192)):
            xin = at(f"xin{block_uses[0]}", [P, 2, D], first)
            xn = at(f"xn{block_uses[0]}", [P, 2, D], first + 2048)
            gain = at(f"gain{block_uses[0]}", [P, D], first + 4096)
            for use in block_uses:
                XIN[use], XN[use], GB[use] = xin, xn, gain

        UT = at("u_t", [P, KT, POS], R2)
        FSUM = at("fold_sum", [P, 2, FOLDS], R2 + 15360)
        AF = at("u_folded", [P, 2, KT, 2 * FOLDS - 2], R1, F32R)
        FC = at("f_in", [P, 2, 2, NF, FW], R2, F32R)
        DE = at("dft", [P, 2, 2, 4, HALF], R1, F32R)
        TAILR = at("dft_tail_raw", [P, 4, HALF], R2 + 10240)
        TAIL = at("dft_tail", [P, 2, 4, HALF], R2 + 11280, F32R)
        CWRAW = at("channel_raw", [P, 2, P], R2 + 19456)
        WBD = at("w_fmix_blocks", [P, 4, P], R2 + 19712)
        CW = at("channel_w", [P, 2, 2, 4, P], R2 + 20224, F32R)
        ROPER = at("rope_raw", [P, 2, KTILES, DH], R2 + 16416)
        GAINS = at("qk_gains", [P, 2, DH], R2 + 17568)
        VROW = at("vector_rows", [VROWS, 3, P], R2 + 17696)
        CHA = at("channel_a", [P, 2, HALF], R1 + 4160)
        FT1 = at("f_out", [P, 4, N_TOK], R2 + 15360)
        A1 = at("u", [P, 2, KT, POS], R1, F32R)
        GE = at("gate_e", [P, 2, N_TOK], R2 + 10240)
        QS = at("q_stack", [P, HEADS, N_TOK], R2, F32R)
        KHH = at("k_hi_hi", [P, KV_HEADS, KEYS], R2 + 8192, F32R)
        KLL = at("k_lo_lo", [P, KV_HEADS, KEYS], R2 + 10280, F32R)
        VV = at("v_hi_ones_lo", [P, KTILES, KV_HEADS, 3 * DH], R2 + 12368, F32R)
        T0 = R2 + 15824
        SQ = at("square", [P, 2, FW], T0)
        YN = at("normed", [P, FW], T0 + 1024)
        YC = at("times_cos", [P, FW], T0 + 1536)
        YS = at("times_sin", [P, FW], T0 + 2048)
        RQ = at("rotated", [P, 2, FW], T0 + 2560)
        GE2 = at("gate_e2", [P, 2, N_TOK], T0 + 3584)
        PR = at("probs", [P, 2, KEYS], T0)
        AG = at("a_gate", [P, 2, FW], T0 + 2088)
        RC = at("row_sum_inv", [DH, FW], T0 + 3112)
        OT = at("attended", [P, 2, FW], T0 + 3624)
        PT = at("probs_t", [P, 2, KTILES, 4 * P], R1, F32R)
        MIXA = at("mixed_a", [P, 2, 4, N_TOK], R1 + 9216, F32R)
        MFR = at("mixed_f_raw", [P, 4, N_TOK], R2)
        MIXF = at("mixed_f", [P, 2, 4, N_TOK], R1, F32R)
        H = at("h", [P, TT, D], R2)
        XR = at("x_again", [P, 2, FW], R2 + 13312)
        GF = at("final_gain", [P, D], R2 + 14336)
        JUNK = at("junk", [P, D], R2 + 15360)

        A2 = at("h2", [P, 2, KT, N_TOK], R1, F32R)
        V2 = at("v2", [P, 2, TT, FW], R2, F32R)
        QT = at("q2_t", [P, 4, N_TOK], R2 + 8192)
        KT2 = at("k2_t", [P, 4, N_TOK], R2 + 12288)
        AT = at("att_t", [P, 4, N_TOK], R2 + 16384)
        WT = at("stick_w_t", [P, 2, TT, 4 * P], R1, F32R)
        QS2 = at("q2_stack", [P, N_TOK], R1 + 8192, F32R)
        KHH2 = at("k2_hi_hi", [P, N_TOK], R1 + 9216, F32R)
        KLL2 = at("k2_lo_lo", [P, N_TOK], R1 + 10240, F32R)
        ZL = at("softplus_part", [P, 2, N_TOK], R1 + 11264)
        ZS = at("softplus", [P, 2, N_TOK], R1 + 13312)
        ONES = at("ones", [P, N_TOK], R1 + 15360)
        ATS = at("att_split", [P, 2, 4, N_TOK], R2, F32R)
        CTS = at("conv_split", [P, 2, 4, N_TOK], R2 + 8192, F32R)
        CCB = at("cc", [P, N_TOK], R2 + 16384)
        PROD = at("cc_cx", [P, N_TOK + 2], R2 + 17408)
        CY = at("conv_y", [P, N_TOK], R2 + 18440)
        CO = at("conv_out", [P, N_TOK], R2 + 19464)
        MGE = at("merge_gates", [P, 2, N_TOK], R2 + 16384)
        MGO = at("merged", [P, 2, N_TOK], R2 + 18432)
        MRR = at("merged_raw", [P, 2, N_TOK], R2 + 16384)
        MR = at("merged_split", [P, 2, KT, N_TOK], R1, F32R)
        Y = at("mix_out", [P, TT, D], R2)
        GP = at("post_gain", [P, D], R2 + 13312)
        JUNK2 = at("junk2", [P, D], R2 + 14336)
        XRR = at("x1_again", [P, 2, D], R2 + 15360)
        UB = at("up_buf", [P, 3, N_TOK], c1)
        A4 = at("ffn_in", [P, 2, KT, N_TOK], c1 + 3072, F32R)
        FFT = at("ffn_mid", [P, FT, N_TOK], TOP - FT * N_TOK)
        FS = at("ffn_split", [P, 2, 2, FW], c1 + 3072, F32R)
        Y2 = at("ffn_out", [P, 4, D], c1 + 5120)
        XF = at("x2_again", [P, 2, D], c1 + 9216)
        GL = at("last_gain", [P, D], c1 + 11264)
        JUNK3 = at("junk3", [P, D], c1 + 12288)

        PB = ctx.enter_context(nc.psum_tensor("psum", [P, 8, 512], F32))

        def pair(d):
            return PB[:, 2 * d:2 * d + 2, :].rearrange("p b n -> p (b n)")

        def pair_tiles(d):
            return PB[:, 2 * d:2 * d + 2, :].rearrange("p b (k n) -> p (b k) n", n=P)

        def tm_bank(n):
            return 4 + n % 4

        def slot(c):
            return WR[:, c % 4, 0, :], WR[:, c % 4, 1, :]

        def plain(r):
            return r.bitcast(F32)

        def tokens_of(u):
            return (META + P * u, P) if u < TT else (0, META)

        def folded(n):
            h, i = divmod(n, NF)
            return h, h * FOLDS + P * i, (P if i < 4 else REST[h])

        w_dram = weight_chunks(a, const)

        block = ctx.enter_context(nc.Block())

        @block.sync
        def _(sp):
            for c in range(C_UP):
                if c >= 2:
                    sp.wait_ge(S["w_split"], c - 1)
                width, parts = w_dram[c]
                for first, src in parts:
                    size = int(np.prod(src.shape[1:]))
                    dst = WS[:, c % 2, first:first + size]
                    if len(src.shape) == 3:
                        dst = dst.rearrange("p (k n) -> p k n", k=src.shape[1])
                    sp.dma_start(dst, src).then_inc(S[f"w_staged{c % 2}"], 16)
            up = a["w_up_2"][0].rearrange("(k p) n -> p k n", p=P)
            with sp.Fori(0, FT) as j:
                for s in range(2):
                    sp.wait_ge(S["w_split"], j * 2 + (C_UP + s - 1))
                    sp.dma_start(WS[:, s, 0:WCH].rearrange("p (k n) -> p k n", k=KT),
                                 up[:, :, bass.ds(j * P + s * FF, P)]).then_inc(S[f"w_staged{s}"], 16)
            down = a["w_down_2"][0].rearrange("(k p) n -> p k n", p=P)
            for half in range(2):
                with sp.Fori(0, FT // 2) as j:
                    for s in range(2):
                        sp.wait_ge(S["w_split"], j * 2 + (C_DOWN + FT * half + s - 1))
                        sp.dma_start(WS[:, s, 0:WCH].rearrange("p (k n) -> p k n", k=1),
                                     down[:, bass.ds(j * 2 + s, 1), :]).then_inc(S[f"w_staged{s}"], 16)

        @block.gpsimd
        def _(pool):
            def split(c, s, r, width, staged, free):
                pool.wait_ge(S[f"w_staged{s}"], staged)
                if free is not None:
                    pool.wait_ge(S["w_used"], free)
                w = width - 8
                pool.tensor_tensor(WR[:, r, 0, w:width], WS[:, s, w:width], ZERO[:, :], ALU.add)
                pool.tensor_scalar(WR[:, r, 0, 0:w], WS[:, s, 0:w], 1.0, 0.0, ALU.mult, ALU.add).then_inc(S["w_hi"], 1)
                pool.wait_ge(S["w_hi"], c + 1)
                pool.tensor_tensor(WR[:, r, 1, 0:width], WS[:, s, 0:width], plain(WR[:, r, 0, 0:width]),
                                   ALU.subtract).then_inc(S["w_split"], 1)

            pool.memset(ZERO[:, :], 0.0).then_inc(S["zero_set"], 1)
            pool.wait_ge(S["zero_set"], 1)
            peeled = C_FGATE + 2
            staged = [0, 0]
            for c in range(peeled):
                staged[c % 2] += 16 * len(w_dram[c][1])
                split(c, c % 2, c % 4, w_dram[c][0], staged[c % 2], c - 3 if c >= 4 else None)
            spans = [(peeled, C_MRG, 1), (C_MRG, C_OUT2, 3), (C_OUT2, C_END, 1)]
            for c_from, c_to, kind in spans:
                if kind == 3:
                    with pool.Fori(0, (c_to - c_from) // 12) as i:
                        loads = [0, 0]
                        for k in range(12):
                            c = c_from + k
                            loads[c % 2] += 32 if k % 3 == 2 else 16
                            split(i * 12 + c, c % 2, c % 4, WCH, i * 128 + (staged[c % 2] + loads[c % 2]),
                                  i * 12 + (c - 3))
                    staged = [staged[0] + 256, staged[1] + 256]
                else:
                    whole = (c_to - c_from) // 4 * 4
                    with pool.Fori(0, whole // 4) as i:
                        for k in range(4):
                            c = c_from + k
                            split(i * 4 + c, c % 2, c % 4, WCH, i * 32 + (staged[c % 2] + 16 * (k // 2 + 1)),
                                  i * 4 + (c - 3))
                    staged = [staged[0] + 8 * whole, staged[1] + 8 * whole]
                    for c in range(c_from + whole, c_to):
                        staged[c % 2] += 16
                        split(c, c % 2, c % 4, WCH, staged[c % 2], c - 3)

        @block.tensor
        def _(pe):
            n_nt, n_tm, n_fm = 0, 0, 0

            def settle(nt=0, tm=0, fm=0):
                for name, count in (("nt_free", nt), ("tm_free", tm), ("fm_free", fm)):
                    if count:
                        pe.wait_ge(S[name], count)

            def three(dst, sh, sl, mh, ml, first, last):
                pe.matmul(dst, sh, mh, start=first, stop=False)
                pe.matmul(dst, sh, ml, start=False, stop=False)
                return pe.matmul(dst, sl, mh, start=False, stop=last)

            def transpose_tile(n, n0, first_use, rows=P):
                pe.wait_ge(S["nt_xn"], n + 1)
                if n - first_use >= 2:
                    pe.wait_ge(S["nt_free"], n - 1)
                for k in range(KT):
                    ins = pe.transpose(pair_tiles(n % 2)[:, k, 0:rows], XN[first_use][0:rows, n % 2, P * k:P * k + P],
                                       IDENT[0:rows, 0:rows])
                ins.then_inc(S["nt_mm"], 1)

            def tm_units(t0, units, c0, chunks, ncols, stat, after=None):
                for u in range(units):
                    n = t0 + u
                    if u >= 4:
                        pe.wait_ge(S["tm_free"], n - 3)
                    d = None
                    for j in range(chunks):
                        if u == 0:
                            pe.wait_ge(S["w_split"], c0 + j + 1)
                        mh, ml = slot(c0 + j)
                        for q in range(WCH // ncols):
                            k = j * (WCH // ncols) + q
                            sh, sl = stat(u, k)
                            if d is None:
                                d = PB[0:sh.shape[1], tm_bank(n), 0:ncols]
                            ins = three(d, sh, sl, mh[:, q * ncols:(q + 1) * ncols],
                                        ml[:, q * ncols:(q + 1) * ncols], k == 0, k == KT - 1)
                        if u == units - 1:
                            ins.then_inc(S["w_used"], 1)
                    if u < units - 1:
                        ins.then_inc(S["tm_mm"], 1)
                    if after is not None:
                        after(u)

            def fm_unit(n, wait, c, mov):
                pe.wait_ge(S["w_split"], c + 1)
                if wait:
                    pe.wait_ge(S["fm_free"], n - 3)
                sh, sl = slot(c)
                for h in range(2):
                    for k in range(KT):
                        mh, ml = mov(k, h)
                        ins = three(PB[:, 2 * (n % 4) + h, :], sh[:, P * k:P * k + P], sl[:, P * k:P * k + P],
                                    mh, ml, k == 0, k == KT - 1)
                return ins

            pe.wait_ge(S["consts"], 16 * N_CONSTS)
            pe.wait_ge(S["vec_in"], 48)
            for i in range(3):
                ins = pe.transpose(PB[:, 7, VROWS * i:VROWS * (i + 1)], VROW[:, i, :], IDENT[0:VROWS, 0:VROWS])
            ins.then_inc(S["vec_t"], 1)

            for t in range(KTILES):
                transpose_tile(N_U + t, N_U, N_U, tokens_of(t)[1])
            settle(nt=KTILES)
            pe.wait_ge(S["cw_in"], 16 * 9)
            for i in range(2):
                ins = pe.matmul(PB[:, i, :], CWRAW[:, i, :], WBD[:, :, :].rearrange("p j n -> p (j n)"),
                                start=True, stop=True)
            ins.then_inc(S["cw_mm"], 1)
            pe.wait_ge(S["vec_done"], 1)
            pe.wait_ge(S["fold_done"], 2 * KT)

            def fold_stat(u, k):
                h, first, rows = folded(u)
                return AF[:, 0, k, first:first + rows], AF[:, 1, k, first:first + rows]

            tm_units(T_FIN, 2 * NF, C_FIN, 4, FW, fold_stat)

            pe.wait_ge(S["tail_done"], 1)
            pe.wait_ge(S["tm_free"], 2 * NF)
            for h in range(2):
                for kind in range(2):
                    c = C_DFT + 2 * h + kind
                    pe.wait_ge(S["w_split"], c + 1)
                    mh, ml = slot(c)
                    for ct in range(4):
                        n = T_DFT + 16 * h + 4 * kind + ct
                        pe.wait_ge(S["tm_free"], n - 3)
                        for i in range(NF):
                            sh, sl = (FC[:, x, kind, i, P * ct:P * ct + P] for x in range(2))
                            vh, vl = ((v[:, HALF * i:HALF * (i + 1)] for v in (mh, ml)) if i < 4 else
                                      (TAIL[:, x, 2 * h + kind, :] for x in range(2)))
                            ins = three(PB[:, tm_bank(n), 0:HALF], sh, sl, vh, vl, i == 0, i == NF - 1)
                        ins.then_inc(S["w_used"] if ct == 3 else S["tm_mm"], 1)
                pe.wait_ge(S["tm_free"], T_DFT + 16 * h + 8)
                pe.wait_ge(S["cw_done"], 2)
                for j in range(4):
                    for kind in range(2):
                        n = T_DFT + 16 * h + 8 + 2 * j + kind
                        pe.wait_ge(S["tm_free"], n - 3)
                        three(PB[:, tm_bank(n), 0:HALF], CW[:, 0, kind, j, :], CW[:, 1, kind, j, :],
                              DE[:, 0, kind, j, :], DE[:, 1, kind, j, :], True, True).then_inc(S["tm_mm"], 1)

            for t in range(KTILES):
                transpose_tile(N_A1 + t, N_A1, N_A1, tokens_of(t)[1])

            def a1_half(k, h):
                return (A1[:, x, k, META + FW * h:META + FW * (h + 1)] for x in range(2))

            def a1_stat(u, k):
                first, rows = tokens_of(u)
                return A1[:, 0, k, first:first + rows], A1[:, 1, k, first:first + rows]

            settle(nt=N_A1 + KTILES, tm=T_KV)
            for f in range(4):
                fm_unit(U_FGATE + f, False, C_FGATE + f, a1_half).then_inc(S["w_used"], 1)
            settle(fm=4)

            def turn_k(u):
                rows = tokens_of(u)[1]
                pe.wait_ge(S["pr_rope"], u + 1)
                if u >= 2:
                    pe.wait_ge(S["kv_kll"], 2 * (u - 1))
                for g in range(KV_HEADS):
                    ins = pe.transpose(pair_tiles(u % 2)[0:DH, g, 0:rows], RQ[0:rows, u % 2, DH * g:DH * g + DH],
                                       IDENT[0:rows, 0:rows])
                ins.then_inc(S["pr_t"], 1)

            def turn_q(u):
                pe.wait_ge(S["pr_rope"], KTILES + u + 1)
                if u >= 2:
                    pe.wait_ge(S["pr_done"], u - 1)
                for g in range(HEADS):
                    ins = pe.transpose(pair_tiles(u % 2)[0:DH, g, :], RQ[:, (KTILES + u) % 2, DH * g:DH * g + DH],
                                       IDENT[:, :])
                ins.then_inc(S["pr_t"], 1)

            tm_units(T_KV, KTILES, C_KV, 2, 256, a1_stat, lambda u: turn_k(u - 1) if u else None)
            turn_k(KTILES - 1)
            pe.wait_ge(S["kv_kll"], 2 * KTILES)
            tm_units(T_Q, TT, C_Q, 4, FW, a1_stat, lambda u: turn_q(u - 1) if u else None)
            turn_q(TT - 1)
            pe.wait_ge(S["pr_done"], TT)
            settle(tm=T_OUT)
            for f in range(4):
                fm_unit(U_AGATE + f, False, C_AGATE + f, a1_half).then_inc(S["w_used"], 1)
            settle(fm=8)

            def scores(i):
                h, t = divmod(i, TT)
                if i:
                    pe.wait_ge(S["sc_exp"], i)
                for x, k2 in enumerate((KHH, KLL)):
                    for b in range(3):
                        ins = pe.matmul(PB[:, b, 0:KPART], QS[:, h, P * t:P * t + P],
                                        k2[:, h // GROUP, KPART * b:KPART * (b + 1)], start=x == 0, stop=x == 1)
                ins.then_inc(S["sc_mm"], 1)

            def turn_probs(i):
                pe.wait_ge(S["sc_exp"], i + 1)
                for g in range(3):
                    if i:
                        pe.wait_ge(S["pt_lo"], 3 * (i - 1) + g + 1)
                    for kt in range(4 * g, min(4 * g + 4, KTILES)):
                        first, rows = tokens_of(kt)
                        ins = pe.transpose(PB[0:rows, 3 + g, P * (kt % 4):P * (kt % 4) + P],
                                           PR[:, i % 2, first:first + rows], IDENT[:, :])
                    ins.then_inc(S["pt_mm"], 1)

            def attend(b):
                g = b // 2 // GROUP
                pe.wait_ge(S["pt_lo"], 12 * (b + 1))
                if b >= 2:
                    pe.wait_ge(S["o_out"], b - 1)
                for kt in range(KTILES):
                    ph, pl = PT[:, 0, kt, :], PT[:, 1, kt, :]
                    pe.matmul(PB[:, 6 + b % 2, :], VV[:, kt, g, 0:P], ph, start=kt == 0, stop=False)
                    pe.matmul(PB[0:DH, 6 + b % 2, :], VV[:, kt, g, P:P + DH], ph, start=False, stop=False)
                    ins = pe.matmul(PB[:, 6 + b % 2, :], VV[:, kt, g, 0:P], pl, start=False, stop=kt == KTILES - 1)
                ins.then_inc(S["av_mm"], 1)

            pe.wait_ge(S["kdup"], 2)
            scores(0)
            for i in range(1, HEADS * TT):
                scores(i)
                turn_probs(i - 1)
                if i % 4 == 0:
                    attend(i // 4 - 1)
            turn_probs(HEADS * TT - 1)
            attend(2 * HEADS - 1)
            pe.wait_ge(S["o_out"], 2 * HEADS)
            pe.wait_ge(S["o_lo"], 2 * HEADS)
            pe.wait_ge(S["mf_done"], 4)

            def mix_stat(u, k):
                m = MIXF if k < 4 else MIXA
                return (m[:, x, k % 4, P * u:P * u + P] for x in range(2))

            for c in range(2):
                tm_units(T_OUT + TT * c, TT, C_OUT + 4 * c, 4, FW, mix_stat)
                settle(tm=T_OUT + TT * (c + 1))

            for t in range(TT):
                transpose_tile(N_A2 + t, N_A2, N_A2)
            settle(nt=N_A3)

            def a2_stat(u, k):
                return (A2[:, x, k, P * u:P * u + P] for x in range(2))

            def a2_half(k, h):
                return (A2[:, x, k, FW * h:FW * (h + 1)] for x in range(2))

            tm_units(T_V2, TT, C_V2, 4, FW, a2_stat)
            settle(tm=T_OUT2)
            for f in range(8):
                fm_unit(U_QK2 + f, f >= 4, C_QK2 + f, a2_half).then_inc(S["w_used"], 1)
            settle(fm=U_CONV)

            def stick_scores(i):
                h, t = divmod(i, TT)
                n = P * (t + 1)
                if t == 0:
                    pe.wait_ge(S["st_a"], 3 * (h + 1))
                    pe.wait_ge(S["st_v"], 3 * (h + 1))
                if i >= 2:
                    pe.wait_ge(S["z_e"], i - 1)
                for b in range((n + FW - 1) // FW):
                    lo, hi = FW * b, min(n, FW * (b + 1))
                    for x, k2 in enumerate((KHH2, KLL2)):
                        ins = pe.matmul(PB[:, 2 * (i % 2) + b, 0:hi - lo], QS2[:, P * t:P * t + P], k2[:, lo:hi],
                                        start=x == 0, stop=x == 1)
                ins.then_inc(S["z_mm"], 1)

            def turn_weights(i, n_before):
                t = i % TT
                pe.wait_ge(S["z_w"], i + 1)
                for g in range(t // 4 + 1):
                    n = n_before + g
                    if n >= 3:
                        pe.wait_ge(S["wt_lo"], n - 2)
                    for kt in range(4 * g, min(4 * g + 4, t + 1)):
                        ins = pe.transpose(PB[:, 4 + n % 3, P * (kt % 4):P * (kt % 4) + P],
                                           ZS[:, i % 2, P * kt:P * kt + P], IDENT[:, :])
                    ins.then_inc(S["wt_mm"], 1)
                return n_before + t // 4 + 1

            def stick_attend(b, groups):
                h, c = divmod(b, 2)
                pe.wait_ge(S["wt_lo"], groups)
                if b:
                    pe.wait_ge(S["at_out"], b)
                n = 4 * c + 4
                for kt in range(n):
                    q0 = P * max(0, kt - 4 * c)
                    vh, vl = (V2[:, x, kt, DH * h:DH * h + DH] for x in range(2))
                    ins = three(PB[0:DH, 7, q0:FW], vh, vl, WT[:, 0, kt, q0:FW], WT[:, 1, kt, q0:FW],
                                kt == 0, kt == n - 1)
                ins.then_inc(S["av2_mm"], 1)

            groups, before = 0, 0
            for i in range(HEADS * TT):
                stick_scores(i)
                if i >= 6 and i % 4 == 2:
                    stick_attend((i - 6) // 4, before)
                if i:
                    groups = turn_weights(i - 1, groups)
                    if i % 4 == 0:
                        before = groups
            groups = turn_weights(HEADS * TT - 1, groups)
            stick_attend(2 * HEADS - 1, groups)
            pe.wait_ge(S["at_out"], 2 * HEADS)

            for t in range(TT):
                transpose_tile(N_A3 + t, N_A3, N_A3)
            settle(nt=N_A4)
            for f in range(12):
                fm_unit(U_CONV + f, f >= 4, C_CONV + f, a2_half).then_inc(S["w_used"], 1)
            for f in range(KT):
                u, c = U_MRG + 4 * f, C_MRG + 3 * f
                fm_unit(u, True, c, a2_half).then_inc(S["w_used"], 1)
                fm_unit(u + 1, True, c + 1, a2_half).then_inc(S["w_used"], 1)
                pe.wait_ge(S["w_split"], c + 3)
                pe.wait_ge(S["at_done"], 4)
                pe.wait_ge(S["cv_done"], 4)
                sh, sl = slot(c + 2)
                for br, m in enumerate((ATS, CTS)):
                    pe.wait_ge(S["fm_free"], u + 2 + br - 3)
                    for h in range(2):
                        for k in range(4):
                            q = 4 * br + k
                            ins = three(PB[:, 2 * ((u + 2 + br) % 4) + h, :], sh[:, P * q:P * q + P],
                                        sl[:, P * q:P * q + P], m[:, 0, k, FW * h:FW * (h + 1)],
                                        m[:, 1, k, FW * h:FW * (h + 1)], k == 0, k == 3)
                ins.then_inc(S["w_used"], 1)
            settle(fm=U_UP)

            def mr_stat(u, k):
                return (MR[:, x, k, P * u:P * u + P] for x in range(2))

            pe.wait_ge(S["mr_done"], KT)
            for c in range(2):
                tm_units(T_OUT2 + TT * c, TT, C_OUT2 + 4 * c, 4, FW, mr_stat)
                settle(tm=T_OUT2 + TT * (c + 1))
            for t in range(TT):
                transpose_tile(N_A4 + t, N_A4, N_A4)
            settle(nt=N_A4 + TT)

            with pe.Fori(0, FT // 2) as i:
                for s in range(4):
                    pe.wait_ge(S["w_split"], i * 4 + (C_UP + s + 1))
                    pe.wait_ge(S["fm_free"], i * 4 + (U_UP + s - 3))
                    for h in range(2):
                        for k in range(KT):
                            ins = three(PB[:, 2 * s + h, :], WR[:, (C_UP + s) % 4, 0, P * k:P * k + P],
                                        WR[:, (C_UP + s) % 4, 1, P * k:P * k + P], A4[:, 0, k, FW * h:FW * (h + 1)],
                                        A4[:, 1, k, FW * h:FW * (h + 1)], k == 0, k == KT - 1)
                    ins.then_inc(S["w_used"], 1)
            pe.wait_ge(S["fm_free"], U_UP + 2 * FT)

            for half in range(2):
                if half:
                    pe.wait_ge(S["dn_ya"], 4)
                    pe.wait_ge(S["dn_yv"], 4)

                def down(j, s, first=False, last=False):
                    c = C_DOWN + FT * half
                    pe.wait_ge(S["w_split"], j + (c + 1))
                    pe.wait_ge(S["dn_lo"], j + (FT * half + 1))
                    r = (c + s) % 4
                    for t in range(4):
                        sh, sl = (FS[:, s % 2, x, P * t:P * t + P] for x in range(2))
                        for g in range(2):
                            ins = three(PB[:, 2 * t + g, :], sh, sl, WR[:, r, 0, FW * g:FW * (g + 1)],
                                        WR[:, r, 1, FW * g:FW * (g + 1)], first, last)
                    ins.then_inc(S["w_used"], 1)

                down(0, 0, first=True)
                down(1, 1)
                with pe.Fori(0, (FT - 4) // 4) as i:
                    for s in range(2, 6):
                        down(i * 4 + s, s)
                for s in range(FT - 4, FT):
                    down(s, s, last=s == FT - 1)

        @block.scalar
        def _(act):
            chain = [0]
            jobs = [0, 0]

            def link(ins):
                chain[0] += 1
                ins.then_inc(S["a_chain"], 1)
                act.wait_ge(S["a_chain"], chain[0])

            def guess(rows, col, n, scale, by_vector):
                if by_vector:
                    jobs[1] += 1
                    act.wait_ge(S["rs_ss"], jobs[1])
                link(act.activation(LN[0:rows, col:col + n], SS[0:rows, col:col + n], ACT.Ln, bias=EPS, scale=scale))
                jobs[0] += 1
                act.activation(YY[0:rows, col:col + n], LN[0:rows, col:col + n], ACT.Exp,
                               scale=-0.5).then_inc(S["rs_y"], 1)

            def ready(n):
                name, value = TM[n]
                act.wait_ge(S[name], value)

            def x_rows(t):
                return a["x"][0, P * t:P * t + P, :] if t < TT else a["meta_tokens"]

            def load_tile(use, t, src, wait=None):
                if wait is not None:
                    act.wait_ge(S["nt_xn"], wait)
                act.dma_start(XIN[use][0:src.shape[0], (use + t) % 2, :], src).then_inc(S[f"nt_in{(use + t) % 2}"], 16)

            load_tile(N_U, 0, x_rows(0))
            load_tile(N_U, 1, x_rows(1))
            act.dma_start(GB[N_U][:, :], a["norm_g"][0, :].partition_broadcast(P)).then_inc(S["consts"], 16)
            act.dma_start(IDENT[:, :], const["ident"]).then_inc(S["consts"], 16)
            act.dma_start(MASK[:, :, :], const["masks"]).then_inc(S["consts"], 16)
            act.dma_start(ROPER[:, :, :, :], const["rope"]).then_inc(S["rope_in"], 16)
            act.dma_start(GAINS[:, 0, :], a["q_norm_g"][0, :].partition_broadcast(P)).then_inc(S["rope_in"], 16)
            act.dma_start(GAINS[:, 1, :], a["k_norm_g"][0, :].partition_broadcast(P)).then_inc(S["rope_in"], 16)
            act.wait_ge(S["vec_zero"], 1)
            nf = 2 * FT
            act.dma_start(VROW[0:nf, :, :], a["conv_ffn_w_2"][0].rearrange("i (m p) -> m i p", p=P)).then_inc(S["vec_in"], 16)
            act.dma_start(VROW[nf:nf + 4, :, :], a["conv_mix_w_2"][0].rearrange("i (m p) -> m i p", p=P)).then_inc(S["vec_in"], 16)
            act.dma_start(VROW[nf + 4:nf + 8, 0, :], a["b_fmix"][0].rearrange("(m g) d -> m (g d)", g=2)).then_inc(S["vec_in"], 16)
            act.dma_start(CWRAW[:, :, :], const["channel"]).then_inc(S["cw_in"], 16)
            act.wait_ge(S["cw_zero"], 1)
            for g in range(8):
                r = DH * (g % 2)
                act.dma_start(WBD[r:r + DH, g // 2, r:r + DH], a["w_fmix"][0, g]).then_inc(S["cw_in"], 16)

            for t in range(KTILES + 1):
                if t < KTILES:
                    rows = tokens_of(t)[1]
                    act.wait_ge(S[f"nt_in{t % 2}"], 16 * (t // 2 + 1))
                    if t >= 2:
                        act.wait_ge(S["nt_mm"], t - 1)
                    link(act.activation(XN[N_U][0:rows, t % 2, :], XIN[N_U][0:rows, t % 2, :], ACT.Square,
                                        accum_out=SS[0:rows, t:t + 1]))
                    guess(rows, t, 1, 1.0 / D, False)
                if t:
                    first, rows = tokens_of(t - 1)
                    act.wait_ge(S["nt_mm"], t)
                    act.activation(UT[:, :, first:first + rows], pair_tiles((t - 1) % 2)[:, :, 0:rows],
                                   ACT.Copy).then_inc(S["nt_free"], 1)
                if t + 2 < KTILES:
                    load_tile(N_U, t + 2, x_rows(t + 2), t + 1)

            act.wait_ge(S["nt_xn"], KTILES)
            act.wait_ge(S["nt_mm"], KTILES)
            act.dma_start(TAILR[:, :, :], const["dft_tail"]).then_inc(S["tail_in"], 16)
            for j in range(2 * KT):
                k, h = divmod(j, 2)
                n = FOLD + 1 - 2 * h
                act.wait_ge(S["fold_sum"], j + 1)
                act.activation(AF[:, 0, k, FOLDS * h:FOLDS * h + n], FSUM[:, h, 0:n], ACT.Copy).then_inc(S["fold_hi"], 1)
            act.wait_ge(S["cw_mm"], 1)
            for i in range(2):
                act.activation(CW[:, 0, i, :, :], PB[:, i, :].rearrange("p (j n) -> p j n", j=4),
                               ACT.Copy).then_inc(S["cw_hi"], 1)
            act.wait_ge(S["tail_in"], 16)
            act.activation(TAIL[:, 0, :, :], TAILR[:, :, :], ACT.Copy).then_inc(S["tail_hi"], 1)

            act.wait_ge(S["fpad"], 1)
            for u in range(2 * NF):
                h, _, rows = folded(u)
                ready(T_FIN + u)
                act.activation(FC[0:rows, 0, h, u % NF, :], PB[0:rows, tm_bank(T_FIN + u), :],
                               ACT.Copy).then_inc(S["tm_hi"], 1)
            for h in range(2):
                for m in range(8):
                    n = T_DFT + 16 * h + m
                    if h and m == 0:
                        ready(T_DFT + 15)
                    ready(n)
                    act.activation(DE[:, 0, m // 4, m % 4, :], PB[:, tm_bank(n), 0:HALF], ACT.Copy).then_inc(S["tm_hi"], 1)
                for j in range(4):
                    n = T_DFT + 16 * h + 8 + 2 * j
                    ready(n)
                    if j >= 2 or h:
                        act.wait_ge(S["tm_free"], n - 2 if j >= 2 else T_DFT + 16)
                    act.activation(CHA[:, j % 2, :], PB[:, tm_bank(n), 0:HALF], ACT.Identity,
                                   bias=VEC[:, 0, nf + 4 + j:nf + 5 + j]).then_inc(S["ch_a"], 1)

            act.wait_ge(S["w_used"], C_DFT + 4)
            act.wait_ge(S["tm_free"], T_KV)
            load_tile(N_A1, 0, x_rows(0))
            load_tile(N_A1, 1, x_rows(1))
            for t in range(KTILES):
                n = N_A1 + t
                first, rows = tokens_of(t)
                if t + 2 < KTILES:
                    load_tile(N_A1, t + 2, x_rows(t + 2), n + 1)
                act.wait_ge(S["nt_mm"], n + 1)
                act.activation(A1[:, 0, :, first:first + rows], pair_tiles(n % 2)[:, :, 0:rows],
                               ACT.Copy).then_inc(S["nt_hi"], 1)

            for f in range(4):
                act.wait_ge(S["w_used"], C_FGATE + f + 1)
                if f >= 2:
                    act.wait_ge(S["gate_out"], f - 1)
                act.activation(GE[:, f % 2, :], pair(f), ACT.Exp, scale=-1.0).then_inc(S["gate_exp"], 1)
                if f:
                    act.wait_ge(S["gate_out"], f)
                    act.dma_start(scratch["mixed_f"][P * (f - 1):P * f, :], FT1[:, f - 1, :]).then_inc(S["gate_stored"], 16)
            act.wait_ge(S["gate_out"], 4)
            act.dma_start(scratch["mixed_f"][3 * P:4 * P, :], FT1[:, 3, :]).then_inc(S["gate_stored"], 16)

            act.wait_ge(S["gate_stored"], 64)
            act.wait_ge(S["vv_set"], 3)
            for u in range(KTILES + 1):
                if u < KTILES:
                    rows = tokens_of(u)[1]
                    n = T_KV + u
                    col = 8 * (u % 2)
                    ready(n)
                    act.activation(SQ[0:rows, u % 2, 0:P], PB[0:rows, tm_bank(n), 0:P], ACT.Square).then_inc(S["pr_sq"], 1)
                    act.activation(VV[0:rows, u, :, 0:DH],
                                   PB[0:rows, tm_bank(n), P:2 * P].rearrange("p (g d) -> p g d", g=KV_HEADS),
                                   ACT.Copy).then_inc(S["kv_vhi"], 1)
                    guess(rows, col, KV_HEADS, 1.0 / DH, True)
                if u:
                    first, rows = tokens_of(u - 1)
                    act.wait_ge(S["pr_t"], u)
                    for x in range(2):
                        act.activation(KHH[DH * x:DH * x + DH, :, first:first + rows],
                                       pair_tiles((u - 1) % 2)[0:DH, 0:KV_HEADS, 0:rows], ACT.Copy).then_inc(S["kv_khh"], 1)
            for u in range(TT + 1):
                if u < TT:
                    n = T_Q + u
                    ready(n)
                    act.activation(SQ[:, (KTILES + u) % 2, :], PB[:, tm_bank(n), :], ACT.Square).then_inc(S["pr_sq"], 1)
                    guess(P, 8 * ((KTILES + u) % 2), HEADS, 1.0 / DH, True)
                if u:
                    act.wait_ge(S["pr_t"], KTILES + u)
                    act.activation(QS[0:DH, :, P * (u - 1):P * u], pair_tiles((u - 1) % 2)[0:DH, :, :],
                                   ACT.Copy).then_inc(S["pr_hi"], 1)
            for f in range(4):
                act.wait_ge(S["w_used"], C_AGATE + f + 1)
                if f >= 2:
                    act.wait_ge(S["gate_stored"], 64 + 16 * (f - 1))
                act.activation(GE2[:, f % 2, :], pair(f), ACT.Exp, scale=-1.0).then_inc(S["gate_exp"], 1)
                if f:
                    act.wait_ge(S["gate_out"], 4 + f)
                    act.dma_start(scratch["a_gate"][P * (f - 1):P * f, :], GE2[:, (f - 1) % 2, :]).then_inc(S["gate_stored"], 16)
            act.wait_ge(S["gate_out"], 8)
            act.dma_start(scratch["a_gate"][3 * P:4 * P, :], GE2[:, 1, :]).then_inc(S["gate_stored"], 16)

            def load_a_gate(b):
                h, c = divmod(b, 2)
                r = DH * (h % 2)
                act.dma_start(AG[r:r + DH, b % 2, :], scratch["a_gate"][DH * h:DH * h + DH, FW * c:FW * c + FW])\
                   .then_inc(S[f"ag_in{b % 2}"], 16)

            def probs_hi(i):
                t = i % 4
                if t == 0 and i:
                    act.wait_ge(S["av_mm"], i // 4)
                for g in range(3):
                    n = 3 * i + g
                    act.wait_ge(S["pt_mm"], n + 1)
                    rows = P if g < 2 else META
                    kts = slice(4 * g, min(4 * g + 4, KTILES))
                    act.activation(PT[0:rows, 0, kts, P * t:P * t + P],
                                   PB[0:rows, 3 + g, 0:P * (4 if g < 2 else 1)].rearrange("p (k n) -> p k n", n=P),
                                   ACT.Copy).then_inc(S["pt_hi"], 1)

            def attended_hi(b):
                h, c = divmod(b, 2)
                r = DH * (h % 2)
                act.wait_ge(S["o_out"], b + 1)
                act.activation(MIXA[r:r + DH, 0, h // 2, FW * c:FW * c + FW], OT[r:r + DH, b % 2, :],
                               ACT.Copy).then_inc(S["o_hi"], 1)
                if b + 2 < 2 * HEADS:
                    load_a_gate(b + 2)

            act.wait_ge(S["gate_stored"], 128)
            load_a_gate(0)
            load_a_gate(1)
            act.wait_ge(S["pt_zero"], 1)
            for i in range(HEADS * TT):
                if i:
                    probs_hi(i - 1)
                act.wait_ge(S["sc_max"], i + 1)
                act.activation(PR[:, i % 2, :].rearrange("p (b n) -> p b n", b=3), PB[:, 0:3, 0:KPART], ACT.Exp,
                               bias=NB[:, i % 2:i % 2 + 1], scale=DH ** -0.5).then_inc(S["sc_exp"], 1)
                if i >= 6 and i % 4 == 2:
                    attended_hi((i - 6) // 4)
            probs_hi(HEADS * TT - 1)
            attended_hi(2 * HEADS - 1)
            act.dma_start(MFR[:, :, :], scratch["mixed_f"].rearrange("(k p) n -> p k n", p=P)).then_inc(S["mf_in"], 16)
            act.dma_start(GF[:, :], a["final_g"].partition_broadcast(P)).then_inc(S["gains_in"], 16)
            act.dma_start(GB[N_A2][:, :], a["norm_mix_pre_2"][0, :].partition_broadcast(P)).then_inc(S["gains_in"], 16)
            act.wait_ge(S["mf_in"], 16)
            act.wait_ge(S["av_mm"], 2 * HEADS)
            for f in range(4):
                act.activation(MIXF[:, 0, f, :], MFR[:, f, :], ACT.Copy).then_inc(S["mf_hi"], 1)

            def load_residual(m):
                c, u = divmod(m, TT)
                act.dma_start(XR[:, m % 2, :], a["x"][0, P * u:P * u + P, FW * c:FW * c + FW]).then_inc(S[f"op_in{m % 2}"], 16)

            load_residual(0)
            load_residual(1)
            for m in range(2, 2 * TT):
                act.wait_ge(S["tm_free"], T_OUT + m - 1)
                load_residual(m)

            def hi_of_tile(n, dst, t):
                act.wait_ge(S["nt_mm"], n + 1)
                act.activation(dst[:, 0, :, P * t:P * t + P], pair_tiles(n % 2), ACT.Copy).then_inc(S["nt_hi"], 1)

            act.wait_ge(S["tm_free"], T_V2)
            for s in range(TT + 2):
                if s < TT:
                    link(act.activation(JUNK[:, :], H[:, s, :], ACT.Square, accum_out=SS[:, s:s + 1]))
                    guess(P, s, 1, 1.0 / D, False)
                if 1 <= s <= TT:
                    t = s - 1
                    act.wait_ge(S["x1_out"], t + 1)
                    act.dma_start(scratch["x1"][P * t:P * t + P, :], H[:, t, :]).then_inc(S["x1_stored"], 16)
                    link(act.activation(JUNK[:, :], H[:, t, :], ACT.Square, accum_out=SS[:, 8 + t:9 + t]))
                    guess(P, 8 + t, 1, 1.0 / D, False)
                if s >= 2:
                    hi_of_tile(N_A2 + s - 2, A2, s - 2)

            act.wait_ge(S["x1_stored"], 16 * TT)
            act.wait_ge(S["nt_free"], N_A3)
            for u in range(TT):
                n = T_V2 + u
                ready(n)
                act.activation(V2[:, 0, u, :], PB[:, tm_bank(n), :], ACT.Copy).then_inc(S["tm_hi"], 1)
            for f in range(8):
                act.wait_ge(S["w_used"], C_QK2 + f + 1)
                act.activation((QT if f < 4 else KT2)[:, f % 4, :], pair((U_QK2 + f) % 4), ACT.Copy,
                               scale=DH ** -0.5 if f < 4 else 1.0).then_inc(S["fm_free"], 1)

            def stacks(h):
                r = DH * (h % 2)
                act.wait_ge(S["fm_free"], U_CONV)
                if h:
                    act.wait_ge(S["z_mm"], TT * h)
                act.activation(QS2[r:r + DH, :], QT[r:r + DH, h // 2, :], ACT.Copy).then_inc(S["st_a"], 1)
                for q in (r, DH - r):
                    act.activation(KHH2[q:q + DH, :], KT2[r:r + DH, h // 2, :], ACT.Copy).then_inc(S["st_a"], 1)

            def soft_part(i):
                t = i % TT
                n = P * (t + 1)
                b = ZL[:, i % 2, 0:n]
                act.wait_ge(S["z_mm"], i + 1)
                if i >= 2:
                    act.wait_ge(S["z_e"], i - 1)
                link(act.activation(b, pair(i % 2)[:, 0:n], ACT.Abs))
                link(act.activation(b, b, ACT.Exp, scale=-1.0))
                act.activation(b, b, ACT.Ln, bias=1.0).then_inc(S["z_l"], 1)

            def weights(i):
                n = P * (i % TT + 1)
                act.wait_ge(S["z_e"], i + 1)
                act.activation(ZS[:, i % 2, 0:n], ZS[:, i % 2, 0:n], ACT.Exp).then_inc(S["z_w"], 1)

            def weights_hi(i, n):
                t, c = i % TT, i % 4
                if c == 0 and i:
                    act.wait_ge(S["av2_mm"], i // 4)
                for g in range(t // 4 + 1):
                    w = min(4, t + 1 - 4 * g)
                    act.wait_ge(S["wt_mm"], n + g + 1)
                    act.activation(WT[:, 0, 4 * g:4 * g + w, P * c:P * c + P],
                                   PB[:, 4 + (n + g) % 3, 0:P * w].rearrange("p (k n) -> p k n", n=P),
                                   ACT.Copy).then_inc(S["wt_hi"], 1)
                return n + t // 4 + 1

            groups = 0
            act.wait_ge(S["w_used"], C_CONV)
            for i in range(HEADS * TT + 2):
                if i < HEADS * TT:
                    if i % TT == 0:
                        stacks(i // TT)
                    soft_part(i)
                if i >= 2:
                    groups = weights_hi(i - 2, groups)
                if 1 <= i <= HEADS * TT:
                    weights(i - 1)

            def x1_rows(t):
                return scratch["x1"][P * t:P * t + P, :]

            act.wait_ge(S["at_out"], 2 * HEADS)
            act.dma_start(GB[N_A3][:, :], a["norm_mix_pre_2"][0, :].partition_broadcast(P)).then_inc(S["gains_in"], 16)
            load_tile(N_A3, 0, x1_rows(0))
            load_tile(N_A3, 1, x1_rows(1))
            for f in range(4):
                act.activation(ATS[:, 0, f, :], AT[:, f, :], ACT.Copy).then_inc(S["at_hi"], 1)
            for t in range(TT):
                if t + 2 < TT:
                    load_tile(N_A3, t + 2, x1_rows(t + 2), N_A3 + t + 1)
                hi_of_tile(N_A3 + t, A2, t)

            act.wait_ge(S["at_done"], 4)
            act.wait_ge(S["nt_free"], N_A4)
            for f in range(5):
                if f < 4:
                    act.wait_ge(S["w_used"], C_CONV + 3 * f + 1)
                    if f:
                        act.wait_ge(S["fm_free"], U_CONV + 3 * f - 2)
                    act.activation(CCB[:, :], pair((U_CONV + 3 * f) % 4), ACT.Copy).then_inc(S["cv_cc"], 1)
                if f:
                    act.wait_ge(S["fm_free"], U_CONV + 3 * f)
                    act.activation(CTS[:, 0, f - 1, :], CO[:, :], ACT.Copy).then_inc(S["cv_hi"], 1)

            act.wait_ge(S["cv_done"], 4)
            for f in range(KT):
                if f:
                    act.wait_ge(S["mg_out"], f)
                for g in range(2):
                    act.wait_ge(S["w_used"], C_MRG + 3 * f + g + 1)
                    act.activation(MGE[:, g, :], pair((U_MRG + 4 * f + g) % 4), ACT.Exp, scale=-1.0)\
                       .then_inc(S["mg_exp"], 1)
                if f:
                    act.dma_start(scratch["merged"][P * (f - 1):P * f, :], MGO[:, (f - 1) % 2, :])\
                       .then_inc(S[f"mg_st{(f - 1) % 2}"], 16)
            act.wait_ge(S["mg_out"], KT)
            act.dma_start(scratch["merged"][P * (KT - 1):P * KT, :], MGO[:, 1, :]).then_inc(S["mg_st1"], 16)
            act.dma_start(GP[:, :], a["norm_mix_post_2"][0, :].partition_broadcast(P)).then_inc(S["gains2_in"], 16)
            act.dma_start(GB[N_A4][:, :], a["norm_ffn_pre_2"][0, :].partition_broadcast(P)).then_inc(S["gains2_in"], 16)
            act.wait_ge(S["mg_st0"], 64)
            act.wait_ge(S["mg_st1"], 64)
            act.wait_ge(S["w_used"], C_OUT2)
            for f in range(KT + 2):
                if f >= 2:
                    act.wait_ge(S[f"mr_in{f % 2}"], 16 * (f // 2))
                    act.activation(MR[:, 0, f - 2, :], MRR[:, f % 2, :], ACT.Copy).then_inc(S["mr_hi"], 1)
                    act.wait_ge(S["mr_done"], f - 1)
                if f < KT:
                    act.dma_start(MRR[:, f % 2, :], scratch["merged"][P * f:P * f + P, :]).then_inc(S[f"mr_in{f % 2}"], 16)
            for m in range(2 * TT):
                c, u = divmod(m, TT)
                n = T_OUT2 + m
                ready(n)
                act.activation(Y[:, u, FW * c:FW * c + FW], PB[:, tm_bank(n), :], ACT.Copy).then_inc(S["tm_free"], 1)

            def load_x1(t):
                act.dma_start(XRR[:, t % 2, :], x1_rows(t)).then_inc(S[f"xr_in{t % 2}"], 16)

            load_x1(0)
            load_x1(1)
            act.wait_ge(S["tm_free"], T_OUT2 + 2 * TT)
            for s in range(TT + 2):
                if s < TT:
                    link(act.activation(JUNK2[:, :], Y[:, s, :], ACT.Square, accum_out=SS[:, s:s + 1]))
                    guess(P, s, 1, 1.0 / D, False)
                if 1 <= s <= TT:
                    t = s - 1
                    act.wait_ge(S["x2_out"], t + 1)
                    act.dma_start(scratch["x2"][P * t:P * t + P, :], Y[:, t, :]).then_inc(S["x2_stored"], 16)
                    if t + 2 < TT:
                        load_x1(t + 2)
                    link(act.activation(JUNK2[:, :], Y[:, t, :], ACT.Square, accum_out=SS[:, 8 + t:9 + t]))
                    guess(P, 8 + t, 1, 1.0 / D, False)
                if s >= 2:
                    hi_of_tile(N_A4 + s - 2, A4, s - 2)

            act.wait_ge(S["x2_stored"], 16 * TT)
            act.wait_ge(S["nt_free"], N_A4 + TT)
            with act.Fori(0, FT // 2) as i:
                for s in range(4):
                    q, g = divmod(s, 2)
                    act.wait_ge(S["w_used"], i * 4 + (C_UP + s + 1))
                    act.wait_ge(S["up_f"], i * 2 + (q + 1))
                    act.activation(UB[:, g, :], pair(s), ACT.Copy,
                                   scale=VEC[:, 2, bass.ds(i * 2 + (q + FT * g), 1)]).then_inc(S["up_c"], 1)
                    if g:
                        act.wait_ge(S["fm_free"], i * 4 + (U_UP + s + 1))
                        act.activation(UB[:, 1, :], UB[:, 1, :], ACT.Gelu_apprx_tanh).then_inc(S["up_g"], 1)

            def load_x2(m):
                act.dma_start(XF[:, m % 2, :], scratch["x2"][P * m:P * m + P, :]).then_inc(S[f"xf_in{m % 2}"], 16)

            def mid_hi(half, j, s):
                act.wait_ge(S["w_used"], j + (C_DOWN + FT * half - 1))
                act.activation(FS[:, s, 0, :], FFT[:, bass.ds(j, 1), FW * half:FW * half + FW].rearrange("p a n -> p (a n)")
                               if not isinstance(j, int) else FFT[:, j, FW * half:FW * half + FW],
                               ACT.Copy).then_inc(S["dn_hi"], 1)

            def finish(half):
                for s in range(5):
                    if s < 4:
                        link(act.activation(JUNK3[:, :], Y2[:, s, :], ACT.Square, accum_out=SS[:, s:s + 1]))
                        guess(P, s, 1, 1.0 / D, False)
                    if s:
                        m = 4 * half + s - 1
                        act.wait_ge(S["f_out"], m + 1)
                        act.dma_start(out[0, P * m:P * m + P, :], Y2[:, s - 1, :]).then_inc(S["f_stored"], 16)
                        if m + 2 < TT:
                            load_x2(m + 2)

            act.wait_ge(S["w_used"], C_DOWN)
            act.wait_ge(S["up_f"], FT + 1)
            act.dma_start(GL[:, :], a["norm_ffn_post_2"][0, :].partition_broadcast(P)).then_inc(S["gains3_in"], 16)
            load_x2(0)
            load_x2(1)
            for half in range(2):
                mid_hi(half, 0, 0)
                mid_hi(half, 1, 1)
                if half:
                    finish(0)
                with act.Fori(1, FT // 2) as i:
                    for s in range(2):
                        mid_hi(half, i * 2 + s, s)
                act.wait_ge(S["w_used"], C_DOWN + FT * (half + 1))
                if half:
                    act.wait_ge(S["f_stored"], 64)
                for t in range(4):
                    act.activation(Y2[:, t, 0:FW], PB[:, 2 * t, :], ACT.Copy).then_inc(S["dn_ya"], 1)
                act.wait_ge(S["dn_ya"], 4 * half + 4)
                act.wait_ge(S["dn_yv"], 4 * half + 4)
            finish(1)
            act.wait_ge(S["f_stored"], 16 * TT)

        @block.vector
        def _(v):
            chain = [0]
            jobs = [0]

            def mark(ins):
                chain[0] += 1
                ins.then_inc(S["v_chain"], 1)
                return chain[0]

            def link(ins):
                v.wait_ge(S["v_chain"], mark(ins))

            def refine(rows, col, n, scale, dst):
                jobs[0] += 1
                m, y, ya, yb = (b[0:rows, col:col + n] for b in (MM, YY, YA, YB))
                v.wait_ge(S["rs_y"], jobs[0])
                mark(v.tensor_scalar(m, SS[0:rows, col:col + n], scale, EPS, ALU.mult, ALU.add))
                link(v.scalar_tensor_tensor(out=ya, in0=y, scalar=-0.5, in1=y, op0=ALU.mult, op1=ALU.mult))
                link(v.tensor_tensor(yb, ya, m, ALU.mult))
                link(v.scalar_tensor_tensor(out=dst, in0=yb, scalar=1.5, in1=y, op0=ALU.add, op1=ALU.mult))

            def ready(n):
                name, value = TM[n]
                v.wait_ge(S[name], value)

            def normalise(use, t, src, rstd, rows=P):
                n = use + t
                if t >= 2:
                    v.wait_ge(S["nt_mm"], n - 1)
                v.scalar_tensor_tensor(out=XN[use][0:rows, n % 2, :], in0=src, scalar=rstd, in1=GB[use][0:rows, :],
                                       op0=ALU.mult, op1=ALU.mult).then_inc(S["nt_xn"], 1)

            def lo_of_tile(n, dst, first, rows=P):
                v.wait_ge(S["nt_hi"], n - N_A1 + 1)
                v.tensor_tensor(dst[:, 1, :, first:first + rows], pair_tiles(n % 2)[:, :, 0:rows],
                                plain(dst[:, 0, :, first:first + rows]), ALU.subtract).then_inc(S["nt_free"], 1)

            v.memset(VROW[:, :, :], 0.0).then_inc(S["vec_zero"], 1)
            v.memset(WBD[:, :, :], 0.0).then_inc(S["cw_zero"], 1)
            v.wait_ge(S["consts"], 16 * N_CONSTS)
            for t in range(KTILES):
                rows = tokens_of(t)[1]
                refine(rows, t, 1, 1.0 / D, RX[0:rows, t:t + 1])
                normalise(N_U, t, XIN[N_U][0:rows, t % 2, :], RX[0:rows, t:t + 1], rows)
            v.wait_ge(S["rope_in"], 48)
            for q in range(2):
                gain = GAINS[:, q, :].unsqueeze(1).broadcast_to([P, KTILES, DH])
                swapped = GAINS[:, q, :].rearrange("p (f e) -> p f e", e=2)[:, :, ::-1].unsqueeze(1)\
                    .broadcast_to([P, KTILES, DH // 2, 2])
                v.tensor_tensor(ROPE[:, 2 * q, :, :], ROPER[:, 0, :, :], gain, ALU.mult)
                mark(v.tensor_tensor(ROPE[:, 2 * q + 1, :, :].rearrange("p t (f e) -> p t f e", e=2),
                                     ROPER[:, 1, :, :].rearrange("p t (f e) -> p t f e", e=2), swapped, ALU.mult))
            v.wait_ge(S["vec_t"], 1)
            v.tensor_copy(VEC[:, :, :], PB[:, 7, 0:3 * VROWS].rearrange("p (i m) -> p i m", i=3)).then_inc(S["vec_done"], 1)

            v.wait_ge(S["nt_free"], KTILES)

            def fold_lo(j):
                k, h = divmod(j, 2)
                n = FOLD + 1 - 2 * h
                v.wait_ge(S["fold_hi"], j + 1)
                v.tensor_tensor(AF[:, 1, k, FOLDS * h:FOLDS * h + n], FSUM[:, h, 0:n],
                                plain(AF[:, 0, k, FOLDS * h:FOLDS * h + n]), ALU.subtract).then_inc(S["fold_done"], 1)

            for j in range(2 * KT):
                k, h = divmod(j, 2)
                if j >= 2:
                    v.wait_ge(S["fold_done"], j - 1)
                if h == 0:
                    link(v.tensor_copy(FSUM[:, 0, 0:FOLD + 1:FOLD], UT[:, k, 0:FOLD + 1:FOLD]))
                v.tensor_tensor(FSUM[:, h, 1 - h:FOLD - h], UT[:, k, 1:FOLD], UT[:, k, POS - 1:FOLD:-1],
                                ALU.subtract if h else ALU.add).then_inc(S["fold_sum"], 1)
                if j:
                    fold_lo(j - 1)
            fold_lo(2 * KT - 1)
            v.wait_ge(S["fold_done"], 2 * KT)
            v.memset(plain(FC[:, :, :, NF - 1, :]), 0.0).then_inc(S["fpad"], 1)
            for i in range(2):
                v.wait_ge(S["cw_hi"], i + 1)
                v.tensor_tensor(CW[:, 1, i, :, :], PB[:, i, :].rearrange("p (j n) -> p j n", j=4),
                                plain(CW[:, 0, i, :, :]), ALU.subtract).then_inc(S["cw_done"], 1)
            v.wait_ge(S["tail_hi"], 1)
            v.tensor_tensor(TAIL[:, 1, :, :], TAILR[:, :, :], plain(TAIL[:, 0, :, :]), ALU.subtract).then_inc(S["tail_done"], 1)
            v.wait_ge(S["fpad"], 1)
            for u in range(2 * NF):
                h, _, rows = folded(u)
                v.wait_ge(S["tm_hi"], u + 1)
                v.tensor_tensor(FC[0:rows, 1, h, u % NF, :], PB[0:rows, tm_bank(T_FIN + u), :],
                                plain(FC[0:rows, 0, h, u % NF, :]), ALU.subtract).then_inc(S["tm_free"], 1)
            for h in range(2):
                for m in range(8):
                    n = T_DFT + 16 * h + m
                    v.wait_ge(S["tm_hi"], 2 * NF + 8 * h + m + 1)
                    v.tensor_tensor(DE[:, 1, m // 4, m % 4, :], PB[:, tm_bank(n), 0:HALF],
                                    plain(DE[:, 0, m // 4, m % 4, :]), ALU.subtract).then_inc(S["tm_free"], 1)
                skip = META - 1 if h == 0 else 0
                drop = 0 if h == 0 else 1
                for j in range(4):
                    n = T_DFT + 16 * h + 8 + 2 * j
                    ready(n + 1)
                    v.wait_ge(S["ch_a"], 4 * h + j + 1)
                    k0 = 1 + HALF * h
                    v.tensor_tensor(FT1[:, j, k0 + skip - META:k0 + HALF - META], CHA[:, j % 2, skip:HALF],
                                    PB[:, tm_bank(n + 1), skip:HALF], ALU.subtract).then_inc(S["tm_free"], 1)
                    last = POS - k0 - META
                    v.tensor_tensor(FT1[:, j, last:last - (HALF - drop):-1], CHA[:, j % 2, 0:HALF - drop],
                                    PB[:, tm_bank(n + 1), 0:HALF - drop], ALU.add).then_inc(S["tm_free"], 1)
            for t in range(KTILES + 1):
                if t < KTILES:
                    rows = tokens_of(t)[1]
                    n = N_A1 + t
                    v.wait_ge(S[f"nt_in{n % 2}"], 16 * (5 - n % 2 + t // 2 + 1))
                    normalise(N_A1, t, XIN[N_A1][0:rows, n % 2, :], RX[0:rows, t:t + 1], rows)
                if t:
                    lo_of_tile(N_A1 + t - 1, A1, *tokens_of(t - 1))

            def gate(z, e, count):
                v.wait_ge(S["gate_exp"], count)
                link(v.tensor_scalar(e, e, 1.0, None, ALU.add))
                link(v.reciprocal(e, e))

            for f in range(4):
                e = GE[:, f % 2, :]
                gate(pair(f), e, f + 1)
                v.tensor_tensor(e, pair(f), e, ALU.mult).then_inc(S["fm_free"], 1)
                v.wait_ge(S["fm_free"], f + 1)
                v.tensor_tensor(FT1[:, f, :], FT1[:, f, :], e, ALU.mult).then_inc(S["gate_out"], 1)

            v.wait_ge(S["gate_stored"], 64)
            v.memset(plain(VV[:, TT, :, :]), 0.0).then_inc(S["vv_set"], 1)
            v.memset(plain(VV[:, 0:TT, :, DH:2 * DH]), 1.0).then_inc(S["vv_set"], 1)
            v.wait_ge(S["vv_set"], 1)
            v.memset(plain(VV[0:META, TT, :, DH:2 * DH]), 1.0).then_inc(S["vv_set"], 1)

            def rotate(n, m, q, t, rows, nh):
                w, col = nh * DH, 8 * (m % 2)
                heads = lambda b: b.rearrange("p (g d) -> p g d", d=DH)
                v.wait_ge(S["pr_sq"], m + 1)
                v.reduce_sum(SS[0:rows, col:col + nh], heads(SQ[0:rows, m % 2, 0:w]), AX).then_inc(S["rs_ss"], 1)
                return w, col, heads

            def rotate_rest(n, m, q, t, rows, nh):
                w, col = nh * DH, 8 * (m % 2)
                heads = lambda b: b.rearrange("p (g d) -> p g d", d=DH)
                pairs = lambda b: b.rearrange("p (g f e) -> p g f e", f=DH // 2, e=2)
                refine(rows, col, nh, 1.0 / DH, RSTD[0:rows, col:col + nh])
                v.tensor_tensor(heads(YN[0:rows, 0:w]), heads(PB[0:rows, tm_bank(n), 0:w]),
                                RSTD[0:rows, col:col + nh].unsqueeze(2).broadcast_to([rows, nh, DH]),
                                ALU.mult).then_inc(S["tm_free"], 1)
                v.wait_ge(S["tm_free"], n + 1)
                mark(v.tensor_tensor(heads(YC[0:rows, 0:w]), heads(YN[0:rows, 0:w]),
                                     ROPE[0:rows, 2 * q, t, :].unsqueeze(1).broadcast_to([rows, nh, DH]), ALU.mult))
                link(v.tensor_tensor(pairs(YS[0:rows, 0:w]), pairs(YN[0:rows, 0:w])[:, :, :, ::-1],
                                     ROPE[0:rows, 2 * q + 1, t, :].rearrange("p (f e) -> p f e", e=2).unsqueeze(1)
                                     .broadcast_to([rows, nh, DH // 2, 2]), ALU.mult))
                if m >= 2:
                    v.wait_ge(S["pr_t"], m - 1)
                v.tensor_tensor(RQ[0:rows, m % 2, 0:w], YC[0:rows, 0:w], YS[0:rows, 0:w], ALU.add).then_inc(S["pr_rope"], 1)

            for u in range(KTILES + 1):
                if u < KTILES:
                    rows = tokens_of(u)[1]
                    rotate(T_KV + u, u, 1, u, rows, KV_HEADS)
                    v.wait_ge(S["kv_vhi"], u + 1)
                    mark(v.tensor_tensor(VV[0:rows, u, :, 2 * DH:3 * DH],
                                         PB[0:rows, tm_bank(T_KV + u), P:2 * P].rearrange("p (g d) -> p g d", g=KV_HEADS),
                                         plain(VV[0:rows, u, :, 0:DH]), ALU.subtract))
                    rotate_rest(T_KV + u, u, 1, u, rows, KV_HEADS)
                if u:
                    first, rows = tokens_of(u - 1)
                    v.wait_ge(S["kv_khh"], 2 * u)
                    for x in range(2):
                        v.tensor_tensor(KLL[DH * x:DH * x + DH, :, first:first + rows],
                                        pair_tiles((u - 1) % 2)[0:DH, 0:KV_HEADS, 0:rows],
                                        plain(KHH[0:DH, :, first:first + rows]), ALU.subtract).then_inc(S["kv_kll"], 1)
            v.wait_ge(S["kv_kll"], 2 * KTILES)
            for b in (KHH, KLL):
                v.tensor_copy(b[:, :, POS:KEYS], plain(b[:, :, 0:KEYS - POS])).then_inc(S["kdup"], 1)
            for u in range(TT + 1):
                if u < TT:
                    rotate(T_Q + u, KTILES + u, 0, u, P, HEADS)
                    rotate_rest(T_Q + u, KTILES + u, 0, u, P, HEADS)
                if u:
                    cols = slice(P * (u - 1), P * u)
                    v.wait_ge(S["pr_hi"], u)
                    v.tensor_tensor(QS[DH:P, :, cols], pair_tiles((u - 1) % 2)[0:DH, :, :], plain(QS[0:DH, :, cols]),
                                    ALU.subtract).then_inc(S["pr_done"], 1)
            for f in range(4):
                e = GE2[:, f % 2, :]
                gate(pair(f), e, 4 + f + 1)
                v.tensor_tensor(e, pair(f), e, ALU.mult).then_inc(S["fm_free"], 1)
                v.wait_ge(S["fm_free"], 4 + f + 1)
                v.tensor_scalar(e, e, 1.0, None, ALU.mult).then_inc(S["gate_out"], 1)

            def probs_lo(i):
                t = i % 4
                for g in range(3):
                    rows = P if g < 2 else META
                    kts = slice(4 * g, min(4 * g + 4, KTILES))
                    v.wait_ge(S["pt_hi"], 3 * i + g + 1)
                    v.tensor_tensor(PT[0:rows, 1, kts, P * t:P * t + P],
                                    PB[0:rows, 3 + g, 0:P * (4 if g < 2 else 1)].rearrange("p (k n) -> p k n", n=P),
                                    plain(PT[0:rows, 0, kts, P * t:P * t + P]), ALU.subtract).then_inc(S["pt_lo"], 1)

            def attended(b):
                h, c = divmod(b, 2)
                r = DH * (h % 2)
                bank = 6 + b % 2
                v.wait_ge(S["av_mm"], b + 1)
                link(v.reciprocal(RC[:, :], PB[DH:P, bank, :]))
                if b >= 2:
                    v.wait_ge(S["o_lo"], b - 1)
                link(v.tensor_tensor(OT[r:r + DH, b % 2, :], PB[0:DH, bank, :], RC[:, :], ALU.mult))
                v.wait_ge(S[f"ag_in{b % 2}"], 16 * (b // 2 + 1))
                v.tensor_tensor(OT[r:r + DH, b % 2, :], OT[r:r + DH, b % 2, :], AG[r:r + DH, b % 2, :],
                                ALU.mult).then_inc(S["o_out"], 1)

            def attended_lo(b):
                h, c = divmod(b, 2)
                r = DH * (h % 2)
                v.wait_ge(S["o_hi"], b + 1)
                v.tensor_tensor(MIXA[r:r + DH, 1, h // 2, FW * c:FW * c + FW], OT[r:r + DH, b % 2, :],
                                plain(MIXA[r:r + DH, 0, h // 2, FW * c:FW * c + FW]), ALU.subtract).then_inc(S["o_lo"], 1)

            v.wait_ge(S["gate_stored"], 128)
            v.wait_ge(S["w_used"], C_OUT)
            v.memset(plain(PT[:, :, KTILES - 1, :]), 0.0).then_inc(S["pt_zero"], 1)
            v.wait_ge(S["pt_zero"], 1)
            for i in range(HEADS * TT):
                v.wait_ge(S["sc_mm"], i + 1)
                link(v.reduce_max(MX[:, i % 2:i % 2 + 1], PB[:, 0:3, 0:KPART], mybir.AxisListType.XY))
                v.tensor_scalar(NB[:, i % 2:i % 2 + 1], MX[:, i % 2:i % 2 + 1], -DH ** -0.5, None,
                                ALU.mult).then_inc(S["sc_max"], 1)
                if i:
                    probs_lo(i - 1)
                if i >= 5 and i % 4 == 1:
                    attended((i - 5) // 4)
                if i >= 7 and i % 4 == 3:
                    attended_lo((i - 7) // 4)
            probs_lo(HEADS * TT - 1)
            attended(2 * HEADS - 1)
            attended_lo(2 * HEADS - 1)
            for f in range(4):
                v.wait_ge(S["mf_hi"], f + 1)
                v.tensor_tensor(MIXF[:, 1, f, :], MFR[:, f, :], plain(MIXF[:, 0, f, :]), ALU.subtract).then_inc(S["mf_done"], 1)
            v.wait_ge(S["mf_done"], 4)
            for m in range(2 * TT):
                c, u = divmod(m, TT)
                ready(T_OUT + m)
                v.wait_ge(S[f"op_in{m % 2}"], 16 * (m // 2 + 1))
                v.tensor_tensor(H[:, u, FW * c:FW * c + FW], PB[:, tm_bank(T_OUT + m), :], XR[:, m % 2, :],
                                ALU.add).then_inc(S["tm_free"], 1)
            v.wait_ge(S["gains_in"], 32)
            v.wait_ge(S["tm_free"], T_V2)
            for s in range(TT + 2):
                if s < TT:
                    refine(P, s, 1, 1.0 / D, RSTD[:, s:s + 1])
                    v.scalar_tensor_tensor(out=H[:, s, :], in0=H[:, s, :], scalar=RSTD[:, s:s + 1], in1=GF[:, :],
                                           op0=ALU.mult, op1=ALU.mult).then_inc(S["x1_out"], 1)
                if 1 <= s <= TT:
                    t = s - 1
                    refine(P, 8 + t, 1, 1.0 / D, RX[:, t:t + 1])
                    normalise(N_A2, t, H[:, t, :], RX[:, t:t + 1])
                if s >= 2:
                    lo_of_tile(N_A2 + s - 2, A2, P * (s - 2))
            v.wait_ge(S["x1_stored"], 16 * TT)
            for u in range(TT):
                n = T_V2 + u
                v.wait_ge(S["tm_hi"], 2 * NF + 16 + u + 1)
                v.tensor_tensor(V2[:, 1, u, :], PB[:, tm_bank(n), :], plain(V2[:, 0, u, :]), ALU.subtract)\
                 .then_inc(S["tm_free"], 1)

            def stacks_lo(h):
                r = DH * (h % 2)
                v.wait_ge(S["st_a"], 3 * h + 3)
                src, khh = KT2[r:r + DH, h // 2, :], plain(KHH2[r:r + DH, :])
                v.tensor_tensor(QS2[DH - r:P - r, :], QT[r:r + DH, h // 2, :], plain(QS2[r:r + DH, :]),
                                ALU.subtract).then_inc(S["st_v"], 1)
                for q in (r, DH - r):
                    v.tensor_tensor(KLL2[q:q + DH, :], src, khh, ALU.subtract).then_inc(S["st_v"], 1)

            def exponent(i):
                t = i % TT
                n = P * (t + 1)
                z, l, s = pair(i % 2)[:, 0:n], ZL[:, i % 2, 0:n], ZS[:, i % 2, 0:n]
                v.wait_ge(S["z_l"], i + 1)
                if i >= 2:
                    v.wait_ge(S["wt_mm"], turned[i - 2])
                link(v.scalar_tensor_tensor(out=s, in0=z, scalar=0.0, in1=l, op0=ALU.max, op1=ALU.add))
                diag = ZS[:, i % 2, P * t:P * t + P]
                link(v.tensor_tensor(diag, diag, MASK[:, 0, :], ALU.mult))
                link(v.tensor_tensor_scan(ZL[:, i % 2, n - 1::-1] if n == N_TOK else ZL[:, i % 2, n - 1::-1],
                                          ONES[:, 0:n], ZS[:, i % 2, n - 1::-1], 0.0, ALU.mult, ALU.add))
                link(v.tensor_tensor(s, z, l, ALU.subtract))
                v.tensor_tensor(diag, diag, MASK[:, 1, :], ALU.add).then_inc(S["z_e"], 1)

            def weights_lo(i, n):
                t, c = i % TT, i % 4
                for g in range(t // 4 + 1):
                    w = min(4, t + 1 - 4 * g)
                    v.wait_ge(S["wt_hi"], n + g + 1)
                    v.tensor_tensor(WT[:, 1, 4 * g:4 * g + w, P * c:P * c + P],
                                    PB[:, 4 + (n + g) % 3, 0:P * w].rearrange("p (k n) -> p k n", n=P),
                                    plain(WT[:, 0, 4 * g:4 * g + w, P * c:P * c + P]), ALU.subtract).then_inc(S["wt_lo"], 1)
                return n + t // 4 + 1

            turned, groups = [], 0
            for i in range(HEADS * TT):
                groups += i % TT // 4 + 1
                turned.append(groups)
            v.wait_ge(S["w_used"], C_CONV)
            v.memset(ONES[:, :], 1.0).then_inc(S["ones_set"], 1)
            v.wait_ge(S["ones_set"], 1)
            groups = 0

            def attended2(b):
                h, c = divmod(b, 2)
                r = DH * (h % 2)
                v.wait_ge(S["av2_mm"], b + 1)
                v.tensor_copy(AT[r:r + DH, h // 2, FW * c:FW * c + FW], PB[0:DH, 7, :]).then_inc(S["at_out"], 1)

            for i in range(HEADS * TT + 2):
                if i < HEADS * TT:
                    if i % TT == 0:
                        stacks_lo(i // TT)
                    exponent(i)
                if i >= 2:
                    groups = weights_lo(i - 2, groups)
                if i >= 6 and i % 4 == 2 and i < HEADS * TT:
                    attended2((i - 6) // 4)
            attended2(2 * HEADS - 1)

            for f in range(4):
                v.wait_ge(S["at_hi"], f + 1)
                v.tensor_tensor(ATS[:, 1, f, :], AT[:, f, :], plain(ATS[:, 0, f, :]), ALU.subtract).then_inc(S["at_done"], 1)
            v.wait_ge(S["gains_in"], 48)
            for t in range(TT + 1):
                if t < TT:
                    n = N_A3 + t
                    v.wait_ge(S[f"nt_in{n % 2}"], 16 * (9 + t // 2 + 1))
                    normalise(N_A3, t, XIN[N_A3][:, n % 2, :], RX[:, t:t + 1])
                if t:
                    lo_of_tile(N_A3 + t - 1, A2, P * (t - 1))

            v.wait_ge(S["at_done"], 4)
            v.memset(PROD[:, 0:2], 0.0).then_inc(S["cv_pad"], 1)
            v.wait_ge(S["cv_pad"], 1)
            nf = 2 * FT
            for f in range(5):
                if f < 4:
                    u = U_CONV + 3 * f
                    v.wait_ge(S["w_used"], C_CONV + 3 * f + 2)
                    v.wait_ge(S["cv_cc"], f + 1)
                    v.tensor_tensor(PROD[:, 2:N_TOK + 2], pair((u + 1) % 4), CCB[:, :], ALU.mult).then_inc(S["fm_free"], 1)
                    v.wait_ge(S["fm_free"], u + 1)
                    v.tensor_scalar(CY[:, :], PROD[:, 2:N_TOK + 2], VEC[:, 2, nf + f:nf + f + 1], None,
                                    ALU.mult).then_inc(S["fm_free"], 1)
                    v.wait_ge(S["fm_free"], u + 2)
                    for i in (1, 0):
                        link(v.scalar_tensor_tensor(out=CY[:, :], in0=PROD[:, i:N_TOK + i], scalar=VEC[:, i, nf + f:nf + f + 1],
                                                    in1=CY[:, :], op0=ALU.mult, op1=ALU.add))
                if f:
                    v.wait_ge(S["cv_hi"], f)
                    v.tensor_tensor(CTS[:, 1, f - 1, :], CO[:, :], plain(CTS[:, 0, f - 1, :]), ALU.subtract).then_inc(S["cv_done"], 1)
                    v.wait_ge(S["cv_done"], f)
                if f < 4:
                    v.wait_ge(S["w_used"], C_CONV + 3 * f + 3)
                    v.tensor_tensor(CO[:, :], pair((u + 2) % 4), CY[:, :], ALU.mult).then_inc(S["fm_free"], 1)
                    v.wait_ge(S["fm_free"], u + 3)

            for f in range(KT):
                u = U_MRG + 4 * f
                for g in range(2):
                    v.wait_ge(S["mg_exp"], 2 * f + g + 1)
                    v.tensor_scalar(MGE[:, g, :], MGE[:, g, :], 1.0, None, ALU.add).then_inc(S["fm_free"], 1)
                v.wait_ge(S["fm_free"], u + 2)
                link(v.reciprocal(MGE[:, :, :], MGE[:, :, :]))
                v.wait_ge(S["w_used"], C_MRG + 3 * f + 3)
                for g in range(2):
                    v.tensor_tensor(MGE[:, g, :], pair((u + 2 + g) % 4), MGE[:, g, :], ALU.mult).then_inc(S["fm_free"], 1)
                v.wait_ge(S["fm_free"], u + 4)
                if f >= 2:
                    v.wait_ge(S[f"mg_st{f % 2}"], 16 * (f // 2))
                v.tensor_tensor(MGO[:, f % 2, :], MGE[:, 0, :], MGE[:, 1, :], ALU.add).then_inc(S["mg_out"], 1)
            for f in range(KT):
                v.wait_ge(S["mr_hi"], f + 1)
                v.tensor_tensor(MR[:, 1, f, :], MRR[:, f % 2, :], plain(MR[:, 0, f, :]), ALU.subtract).then_inc(S["mr_done"], 1)

            v.wait_ge(S["gains2_in"], 32)
            for s in range(TT + 2):
                if s < TT:
                    refine(P, s, 1, 1.0 / D, RSTD[:, s:s + 1])
                    link(v.scalar_tensor_tensor(out=Y[:, s, :], in0=Y[:, s, :], scalar=RSTD[:, s:s + 1], in1=GP[:, :],
                                                op0=ALU.mult, op1=ALU.mult))
                    v.wait_ge(S[f"xr_in{s % 2}"], 16 * (s // 2 + 1))
                    v.tensor_tensor(Y[:, s, :], Y[:, s, :], XRR[:, s % 2, :], ALU.add).then_inc(S["x2_out"], 1)
                if 1 <= s <= TT:
                    t = s - 1
                    refine(P, 8 + t, 1, 1.0 / D, RX[:, t:t + 1])
                    normalise(N_A4, t, Y[:, t, :], RX[:, t:t + 1])
                if s >= 2:
                    lo_of_tile(N_A4 + s - 2, A4, P * (s - 2))

            v.sem_inc(S["up_f"], 1)
            with v.Fori(0, FT // 2) as i:
                for s in range(4):
                    q, g = divmod(s, 2)
                    up = pair(s)
                    w1, w0 = (VEC[:, x, bass.ds(i * 2 + (q + FT * g), 1)] for x in (1, 0))
                    v.wait_ge(S["up_c"], i * 4 + (s + 1))
                    v.scalar_tensor_tensor(out=UB[:, g, 1:N_TOK], in0=up[:, 0:N_TOK - 1], scalar=w1,
                                           in1=UB[:, g, 1:N_TOK], op0=ALU.mult, op1=ALU.add).then_inc(S["up_s"], 1)
                    v.wait_ge(S["up_s"], i * 4 + (s + 1))
                    v.scalar_tensor_tensor(out=UB[:, g, 2:N_TOK], in0=up[:, 0:N_TOK - 2], scalar=w0,
                                           in1=UB[:, g, 2:N_TOK], op0=ALU.mult, op1=ALU.add).then_inc(S["fm_free"], 1)
                    if g:
                        v.wait_ge(S["up_g"], i * 2 + (q + 1))
                        v.tensor_tensor(FFT[:, bass.ds(i * 2 + q, 1), :].rearrange("p a n -> p (a n)"), UB[:, 0, :],
                                        UB[:, 1, :], ALU.mult).then_inc(S["up_f"], 1)

            def mid_lo(half, j, s):
                v.wait_ge(S["dn_hi"], j + (FT * half + 1))
                src = FFT[:, j, FW * half:FW * half + FW] if isinstance(j, int) else \
                    FFT[:, bass.ds(j, 1), FW * half:FW * half + FW].rearrange("p a n -> p (a n)")
                v.tensor_tensor(FS[:, s, 1, :], src, plain(FS[:, s, 0, :]), ALU.subtract).then_inc(S["dn_lo"], 1)

            def finish(half):
                for s in range(4):
                    m = 4 * half + s
                    refine(P, s, 1, 1.0 / D, RSTD[:, s:s + 1])
                    link(v.scalar_tensor_tensor(out=Y2[:, s, :], in0=Y2[:, s, :], scalar=RSTD[:, s:s + 1],
                                                in1=GL[:, :], op0=ALU.mult, op1=ALU.mult))
                    v.wait_ge(S[f"xf_in{m % 2}"], 16 * (m // 2 + 1))
                    v.tensor_tensor(Y2[:, s, :], Y2[:, s, :], XF[:, m % 2, :], ALU.add).then_inc(S["f_out"], 1)

            v.wait_ge(S["gains3_in"], 16)
            v.wait_ge(S["up_f"], FT + 1)
            for half in range(2):
                mid_lo(half, 0, 0)
                mid_lo(half, 1, 1)
                if half:
                    finish(0)
                with v.Fori(1, FT // 2) as i:
                    for s in range(2):
                        mid_lo(half, i * 2 + s, s)
                v.wait_ge(S["w_used"], C_DOWN + FT * (half + 1))
                if half:
                    v.wait_ge(S["f_stored"], 64)
                for t in range(4):
                    v.tensor_copy(Y2[:, t, FW:D], PB[:, 2 * t + 1, :]).then_inc(S["dn_yv"], 1)
            finish(1)


N_CONSTS = 3


def weight_chunks(a, const):
    def token_major(w, first, n):
        per = WCH // n
        v = w.rearrange("(k p) n -> p k n", p=P)
        return [(WCH, [(0, v[:, per * j:per * j + per, first:first + n])]) for j in range(KT // per)]

    def feature_tile(w, first):
        return (WCH, [(0, w.rearrange("(k p) n -> p k n", p=P)[:, :, first:first + P])])

    w1, w2 = a["w_in"][0], a["w_in_2"][0]
    out = token_major(w1, 0, FW)
    out += [(SLOT, [(0, const["dft_main"][i])]) for i in range(4)]
    out += [feature_tile(w1, FW + P * f) for f in range(4)]
    out += token_major(w1, 1536, 256) + token_major(w1, 1024, FW)
    out += [feature_tile(w1, GATE1 + P * f) for f in range(4)]
    out += token_major(a["w_out"][0], 0, FW) + token_major(a["w_out"][0], FW, FW)
    out += token_major(w2, 1024, FW)
    out += [feature_tile(w2, P * f) for f in range(8)]
    for f in range(4):
        out += [feature_tile(w2, c + P * f) for c in (2048, 2560, 1536)]
    branches = [a[k][0].rearrange("(k p) n -> p k n", p=P) for k in ("w_att_branch_2", "w_conv_branch_2")]
    for f in range(KT):
        out += [feature_tile(w2, 3072 + P * f), feature_tile(w2, 4096 + P * f)]
        out.append((WCH, [(FW * i, b[:, :, P * f:P * f + P]) for i, b in enumerate(branches)]))
    out += token_major(a["w_out_2"][0], 0, FW) + token_major(a["w_out_2"][0], FW, FW)
    assert len(out) == C_UP
    return out


def constants():
    ident = np.eye(P, dtype=np.float32)
    masks = np.zeros((P, 2, P), np.float32)
    q, k = np.arange(P)[:, None], np.arange(P)[None, :]
    masks[:, 0] = k < q
    masks[:, 1] = np.where(k < q, 0.0, NEG)
    grid, axis = 64, 16
    j = np.arange(N_TOK)
    row, col = j // grid - (N_TOK // grid) // 2, j % grid - grid // 2
    freqs = 1.0 / (10000.0 ** (np.arange(axis) * 2.0 / (2 * axis)))
    ang = np.concatenate([row[:, None] * freqs, col[:, None] * freqs], axis=-1)
    cos, sin = np.repeat(np.cos(ang), 2, axis=1), np.repeat(np.sin(ang), 2, axis=1)
    sin[:, 0::2] *= -1.0
    rope = np.zeros((P, 2, KTILES, DH), np.float32)
    rope[:, 0, TT] = 1.0
    for t in range(TT):
        rope[:, 0, t], rope[:, 1, t] = cos[P * t:P * t + P], sin[P * t:P * t + P]
    c = np.arange(DH)
    ang = 2 * np.pi * (np.outer(c, c) % DH) / DH
    channel = np.zeros((P, 2, P), np.float32)
    for g in range(2):
        s = slice(DH * g, DH * g + DH)
        channel[s, 0, s], channel[s, 1, s] = np.cos(ang), np.sin(ang)
    main = np.zeros((4, P, 4, HALF), np.float64)
    tail = np.zeros((P, 4, HALF), np.float64)
    for h in range(2):
        freq = 1 + HALF * h + np.arange(HALF)
        for kind in range(2):
            n = np.arange(FOLD + 1) if kind == 0 else np.arange(1, FOLD)
            ang = 2 * np.pi * (np.outer(n, freq) % POS) / POS
            table = (np.sin(ang) if kind else np.cos(ang)) / np.sqrt(POS * DH)
            main[2 * h + kind] = table[:4 * P].reshape(4, P, HALF).transpose(1, 0, 2)
            tail[:len(n) - 4 * P, 2 * h + kind] = table[4 * P:]
    return {"ident": ident, "masks": masks, "rope": rope, "channel": channel,
            "dft_main": main.reshape(4, P, SLOT).astype(np.float32), "dft_tail": tail.astype(np.float32)}


_INS = ["x", "meta_tokens", "norm_g", "w_in", "w_fmix", "b_fmix", "q_norm_g", "k_norm_g", "w_out", "final_g",
        "norm_mix_pre_2", "w_in_2", "conv_mix_w_2", "w_att_branch_2", "w_conv_branch_2", "w_out_2",
        "norm_mix_post_2", "norm_ffn_pre_2", "w_up_2", "conv_ffn_w_2", "w_down_2", "norm_ffn_post_2"]
_SCRATCH = {"mixed_f": (512, N_TOK), "a_gate": (512, N_TOK), "x1": (N_TOK, D), "merged": (D, N_TOK), "x2": (N_TOK, D)}


def kernel(**inputs):
    import concourse.bacc as bacc
    from concourse.bass_utils import run_bass_kernel_spmd

    nc = bacc.Bacc("TRN2", target_bir_lowering=False, num_devices=1)
    arrays, a, const = {}, {}, {}
    for name in _INS:
        array = np.ascontiguousarray(inputs[name])
        arrays[f"in_{name}"] = array
        a[name] = nc.dram_tensor(f"in_{name}", array.shape, mybir.dt.from_np(array.dtype), kind="ExternalInput").ap()
    for name, array in constants().items():
        arrays[f"const_{name}"] = array
        const[name] = nc.dram_tensor(f"const_{name}", array.shape, F32, kind="ExternalInput").ap()
    scratch = {name: nc.dram_tensor(f"scratch_{name}", shape, F32, kind="Internal").ap()
               for name, shape in _SCRATCH.items()}
    out = nc.dram_tensor("out_0", (1, N_TOK, D), F32, kind="ExternalOutput").ap()
    two_block_kernel(nc, a, const, scratch, out)
    r = run_bass_kernel_spmd(nc, [arrays], core_ids=[0])
    return r.results[0]["out_0"]
```

```python
from contextlib import ExitStack

import concourse.bass as bass
import numpy as np
from concourse import mybir

F32 = mybir.dt.float32
F32R = mybir.dt.float32r
ALU = mybir.AluOpType
ACT = mybir.ActivationFunctionType
AX = mybir.AxisListType.X

P = 128
D = 1024
KT = D // P
N_TOK = 1024
TT = N_TOK // P
META = 16
POS = N_TOK + META
EPS = 1e-6
DH = 64
HEADS = 8
KV_HEADS = 2
GROUP = HEADS // KV_HEADS
FW = 512
FOLD = POS // 2
FOLDS = 522
NF = 5
REST = {0: FOLD + 1 - 4 * P, 1: FOLD - 1 - 4 * P}
HALF = FOLD // 2
SLOT = 4 * HALF
WCH = 1024
KEYS = 1044
KPART = KEYS // 3
KTILES = 9
FF = 2816
FT = FF // P
PAIR = 2 * P
PAIRS = HEADS * TT // 2
NEG = -2.0 ** 100
VROWS = FT * 2 + 4 + 4
EXP_AND_LN = 6
GATE1 = 1792

C_FIN = 0
C_DFT = C_FIN + 4
C_FGATE = C_DFT + 4
C_KV = C_FGATE + 4
C_Q = C_KV + 2
C_AGATE = C_Q + 4
C_OUT = C_AGATE + 4
C_V2 = C_OUT + 8
C_QK2 = C_V2 + 4
C_CONV = C_QK2 + 8
C_MRG = C_CONV + 12
C_OUT2 = C_MRG + 24
C_UP = C_OUT2 + 8
C_DOWN = C_UP + 2 * FT
C_END = C_DOWN + 2 * FT

T_FIN = 0
T_DFT = T_FIN + 2 * NF
T_KV = T_DFT + 32
T_Q = T_KV + KTILES
T_OUT = T_Q + TT
T_V2 = T_OUT + 2 * TT
T_OUT2 = T_V2 + TT
U_FGATE = 0
U_AGATE = 4
U_QK2 = 8
U_CONV = 16
U_MRG = 28
U_UP = U_MRG + 32

N_U = 0
N_A1 = N_U + KTILES
N_A2 = N_A1 + KTILES
N_A3 = N_A2 + TT
N_A4 = N_A3 + TT


def tm_signals():
    groups = [(2 * NF, C_FIN + 4)]
    for h in range(2):
        groups += [(4, C_DFT + 2 * h + 1), (4, C_DFT + 2 * h + 2), (8, None)]
    groups += [(KTILES, C_KV + 2), (TT, C_Q + 4), (TT, C_OUT + 4), (TT, C_OUT + 8), (TT, C_V2 + 4),
               (TT, C_OUT2 + 4), (TT, C_OUT2 + 8)]
    out, count = [], 0
    for units, used in groups:
        for u in range(units):
            if used is not None and u == units - 1:
                out.append(("w_used", used))
            else:
                count += 1
                out.append(("tm_mm", count))
    return out


SEMS = """
zero_set w_staged0 w_staged1 w_hi w_split w_used tm_mm tm_free fm_free nt_in0 nt_in1 nt_xn nt_mm nt_hi nt_free
v_chain a_chain rs_ss rs_y consts vec_zero vec_in vec_t vec_done rope_in cw_zero cw_in cw_mm cw_hi cw_done
fold_sum fold_hi fold_done fpad tm_hi tail_in tail_hi tail_done ch_a ch_out
gate_sig gate_out gate_stored vv_set
pr_sq pr_rope pr_t pr_hi pr_done kv_khh kv_kll kv_vhi kdup
sc_mm sc_max sc_exp pt_mm pt_zero pt_hi pt_lo av_mm ag_in0 ag_in1 o_inv o_out o_hi o_lo
mf_in mf_hi mf_done op_in0 op_in1 gains_in x1_out x1_stored
causal_in st_a st_v z_mm z_l z_e z_w wt_mm wt_hi wt_lo av2_mm at_out ones_set
at_hi at_done cv_pad cv_cc cv_out cv_hi cv_done mg_out mg_st0 mg_st1 mr_in0 mr_in1 mr_hi mr_done
gains2_in xr_in0 xr_in1 x2_out x2_stored
up_c up_s up_g up_f dn_hi dn_lo dn_ya dn_yv gains3_in xf_in0 xf_in1 f_out f_stored
""".split()


def two_block_kernel(nc, a, const, scratch, out):
    ctx = ExitStack()
    with ctx:
        S = {name: ctx.enter_context(nc.semaphore(name)) for name in SEMS}
        TM = tm_signals()
        base = (nc.sbuf_base + 63) // 64 * 64

        def at(name, shape, first, dt=F32):
            size = int(np.prod(shape[1:]))
            assert first + size <= TOP, (name, first + size, TOP)
            return nc.alloc_sbuf_tensor_at(name, shape, dt, offset=base + 4 * first)

        TOP = (nc.sbuf_top - base) // 4

        WS = at("w_staging", [P, 2, SLOT], 0)
        WR = at("w_ring", [P, 4, 2, SLOT], 2 * SLOT, F32R)
        c0 = 10 * SLOT
        IDENT = at("ident", [P, P], c0)
        VEC = at("vectors", [P, 3, VROWS], c0 + 128)
        SS = at("sumsq", [P, 16], c0 + 288)
        LN = at("ln", [P, 16], c0 + 304)
        YY = at("rsqrt_guess", [P, 16], c0 + 320)
        MM = at("mean", [P, 16], c0 + 336)
        YA = at("newton_a", [P, 16], c0 + 352)
        YB = at("newton_b", [P, 16], c0 + 368)
        RSTD = at("rstd", [P, 16], c0 + 384)
        RX = at("rstd_x", [P, 16], c0 + 400)
        ZERO = at("zero", [P, 8], c0 + 688)
        MX = at("row_max", [P, 2], c0 + 416)
        NB = at("minus_max", [P, 2], c0 + 424)
        IDR = at("ident_r", [P, P], c0 + 432, F32R)
        CAUSAL = at("causal", [P, P], c0 + 560, F32R)
        c1 = c0 + 696
        ROPE = at("rope", [P, 4, KTILES, DH], c1)
        A0 = c1 + 4 * KTILES * DH
        R1 = A0
        R2 = A0 + 17408
        assert TOP - R2 >= 22400 - 64, TOP - R2

        XIN, XN, GB = {}, {}, {}
        for block_uses, first in (((N_U, N_A1), R2 + 10240), ((N_A2, N_A3, N_A4), R2 + 8192)):
            xin = at(f"xin{block_uses[0]}", [P, 2, D], first)
            xn = at(f"xn{block_uses[0]}", [P, 2, D], first + 2048)
            gain = at(f"gain{block_uses[0]}", [P, D], first + 4096)
            for use in block_uses:
                XIN[use], XN[use], GB[use] = xin, xn, gain

        UT = at("u_t", [P, KT, POS], R2)
        FSUM = at("fold_sum", [P, 2, FOLDS], R2 + 15360)
        AF = at("u_folded", [P, 2, KT, 2 * FOLDS - 2], R1, F32R)
        FC = at("f_in", [P, 2, 2, NF, FW], R2, F32R)
        DE = at("dft", [P, 2, 2, 4, HALF], R1, F32R)
        TAILR = at("dft_tail_raw", [P, 4, HALF], R2 + 10240)
        TAIL = at("dft_tail", [P, 2, 4, HALF], R2 + 11280, F32R)
        CWRAW = at("channel_raw", [P, 2, P], R2 + 19456)
        WBD = at("w_fmix_blocks", [P, 4, P], R2 + 19712)
        CW = at("channel_w", [P, 2, 2, 4, P], R2 + 20224, F32R)
        ROPER = at("rope_raw", [P, 2, KTILES, DH], R2 + 16416)
        GAINS = at("qk_gains", [P, 2, DH], R2 + 17568)
        VROW = at("vector_rows", [VROWS, 3, P], R2 + 17696)
        CHA = at("channel_a", [P, 2, HALF], R1 + 4160)
        FT1 = at("f_out", [P, 4, N_TOK], R2 + 15360)
        A1 = at("u", [P, 2, KT, POS], R1, F32R)
        GE = at("gate_e", [P, 2, N_TOK], R2 + 10240)
        QS = at("q_stack", [P, HEADS, N_TOK], R2, F32R)
        KHH = at("k_hi_hi", [P, KV_HEADS, KEYS], R2 + 8192, F32R)
        KLL = at("k_lo_lo", [P, KV_HEADS, KEYS], R2 + 10280, F32R)
        VV = at("v_hi_ones_lo", [P, KTILES, KV_HEADS, 3 * DH], R2 + 12368, F32R)
        T0 = R2 + 15824
        SQ = at("square", [P, 2, FW], T0)
        YN = at("normed", [P, FW], T0 + 1024)
        YC = at("times_cos", [P, FW], T0 + 1536)
        YS = at("times_sin", [P, FW], T0 + 2048)
        RQ = at("rotated", [P, 2, FW], T0 + 2560)
        GE2 = at("gate_e2", [P, 2, N_TOK], T0 + 3584)
        PR = at("probs", [P, 2, KEYS], T0)
        AG = at("a_gate", [P, 2, FW], T0 + 2088)
        RC = at("row_sum_inv", [DH, FW], T0 + 3112)
        OT = at("attended", [P, 4, PAIR], T0 + 3624)
        PT = at("probs_t", [P, 2, KTILES, 4 * P], R1, F32R)
        MIXA = at("mixed_a", [P, 2, 4, N_TOK], R1 + 9216, F32R)
        MFR = at("mixed_f_raw", [P, 4, N_TOK], R2)
        MIXF = at("mixed_f", [P, 2, 4, N_TOK], R1, F32R)
        H = at("h", [P, TT, D], R2)
        XR = at("x_again", [P, 2, FW], R2 + 13312)
        GF = at("final_gain", [P, D], R2 + 14336)
        JUNK = at("junk", [P, D], R2 + 15360)

        A2 = at("h2", [P, 2, KT, N_TOK], R1, F32R)
        V2 = at("v2", [P, 2, TT, FW], R2, F32R)
        QT = at("q2_t", [P, 4, N_TOK], R2 + 8192)
        KT2 = at("k2_t", [P, 4, N_TOK], R2 + 12288)
        AT = at("att_t", [P, 4, N_TOK], R2 + 16384)
        WT = at("stick_w_t", [P, 2, TT, 4 * P], R1, F32R)
        QS2 = [at(f"q2_stack{i}", [P, N_TOK], f, F32R) for i, f in enumerate((R1 + 8192, R1 + 16384))]
        KHH2 = [at(f"k2_hi_hi{i}", [P, N_TOK], f, F32R) for i, f in enumerate((R1 + 9216, c1))]
        KLL2 = [at(f"k2_lo_lo{i}", [P, N_TOK], f, F32R) for i, f in enumerate((R1 + 10240, c1 + 1024))]
        CAUSALR = at("causal_raw", [P, P], c1 + 2048)
        ZL = at("softplus_part", [P, 2, N_TOK], R1 + 11264)
        ZS = at("softplus", [P, 2, N_TOK], R1 + 13312)
        ONES = at("ones", [P, N_TOK], R1 + 15360)
        ATS = at("att_split", [P, 2, 4, N_TOK], R2, F32R)
        CTS = at("conv_split", [P, 2, 4, N_TOK], R2 + 8192, F32R)
        CCB = at("cc", [P, N_TOK], R2 + 16384)
        PROD = at("cc_cx", [P, N_TOK + 2], R2 + 17408)
        CY = at("conv_y", [P, N_TOK], R2 + 18440)
        CO = at("conv_out", [P, N_TOK], R2 + 19464)
        MGE = at("merge_gates", [P, 2, N_TOK], R2 + 16384)
        MGO = at("merged", [P, 2, N_TOK], R2 + 18432)
        MRR = at("merged_raw", [P, 2, N_TOK], R2 + 16384)
        MR = at("merged_split", [P, 2, KT, N_TOK], R1, F32R)
        Y = at("mix_out", [P, TT, D], R2)
        GP = at("post_gain", [P, D], R2 + 13312)
        JUNK2 = at("junk2", [P, D], R2 + 14336)
        XRR = at("x1_again", [P, 2, D], R2 + 15360)
        UB = at("up_buf", [P, 3, N_TOK], c1)
        A4 = at("ffn_in", [P, 2, KT, N_TOK], c1 + 3072, F32R)
        FFT = at("ffn_mid", [P, FT, N_TOK], TOP - FT * N_TOK)
        FS = at("ffn_split", [P, 2, 2, FW], c1 + 3072, F32R)
        Y2 = at("ffn_out", [P, 4, D], c1 + 5120)
        XF = at("x2_again", [P, 2, D], c1 + 9216)
        GL = at("last_gain", [P, D], c1 + 11264)
        JUNK3 = at("junk3", [P, D], c1 + 12288)

        PB = ctx.enter_context(nc.psum_tensor("psum", [P, 8, 512], F32))

        def pair(d):
            return PB[:, 2 * d:2 * d + 2, :].rearrange("p b n -> p (b n)")

        def pair_tiles(d):
            return PB[:, 2 * d:2 * d + 2, :].rearrange("p b (k n) -> p (b k) n", n=P)

        def tm_bank(n):
            return 4 + n % 4

        def slot(c):
            return WR[:, c % 4, 0, :], WR[:, c % 4, 1, :]

        def plain(r):
            return r.bitcast(F32)

        def tokens_of(u):
            return (META + P * u, P) if u < TT else (0, META)

        def pair_place(p):
            r = DH * (p // 4 % 2)
            return slice(r, r + DH), slice(PAIR * (p % 4), PAIR * (p % 4) + PAIR), p % 4

        def turned(i):
            return i // TT * (TT // 4 * (TT // 4 + 1) * 2) + sum(t // 4 + 1 for t in range(i % TT))

        def folded(n):
            h, i = divmod(n, NF)
            return h, h * FOLDS + P * i, (P if i < 4 else REST[h])

        w_dram = weight_chunks(a, const)

        block = ctx.enter_context(nc.Block())

        @block.sync
        def _(sp):
            for c in range(C_UP):
                if c >= 2:
                    sp.wait_ge(S["w_split"], c - 1)
                width, parts = w_dram[c]
                for first, src in parts:
                    size = int(np.prod(src.shape[1:]))
                    dst = WS[:, c % 2, first:first + size]
                    if len(src.shape) == 3:
                        dst = dst.rearrange("p (k n) -> p k n", k=src.shape[1])
                    sp.dma_start(dst, src).then_inc(S[f"w_staged{c % 2}"], 16)
            up = a["w_up_2"][0].rearrange("(k p) n -> p k n", p=P)
            with sp.Fori(0, FT) as j:
                for s in range(2):
                    sp.wait_ge(S["w_split"], j * 2 + (C_UP + s - 1))
                    sp.dma_start(WS[:, s, 0:WCH].rearrange("p (k n) -> p k n", k=KT),
                                 up[:, :, bass.ds(j * P + s * FF, P)]).then_inc(S[f"w_staged{s}"], 16)
            down = a["w_down_2"][0].rearrange("(k p) n -> p k n", p=P)
            for half in range(2):
                with sp.Fori(0, FT // 2) as j:
                    for s in range(2):
                        sp.wait_ge(S["w_split"], j * 2 + (C_DOWN + FT * half + s - 1))
                        sp.dma_start(WS[:, s, 0:WCH].rearrange("p (k n) -> p k n", k=1),
                                     down[:, bass.ds(j * 2 + s, 1), :]).then_inc(S[f"w_staged{s}"], 16)

        @block.gpsimd
        def _(pool):
            def split(c, s, r, width, staged, free):
                pool.wait_ge(S[f"w_staged{s}"], staged)
                if free is not None:
                    pool.wait_ge(S["w_used"], free)
                w = width - 8
                pool.tensor_tensor(WR[:, r, 0, w:width], WS[:, s, w:width], ZERO[:, :], ALU.add)
                pool.tensor_scalar(WR[:, r, 0, 0:w], WS[:, s, 0:w], 1.0, 0.0, ALU.mult, ALU.add).then_inc(S["w_hi"], 1)
                pool.wait_ge(S["w_hi"], c + 1)
                pool.tensor_tensor(WR[:, r, 1, 0:width], WS[:, s, 0:width], plain(WR[:, r, 0, 0:width]),
                                   ALU.subtract).then_inc(S["w_split"], 1)

            pool.memset(ZERO[:, :], 0.0).then_inc(S["zero_set"], 1)
            pool.wait_ge(S["zero_set"], 1)
            peeled = C_FGATE + 2
            staged = [0, 0]
            for c in range(peeled):
                staged[c % 2] += 16 * len(w_dram[c][1])
                split(c, c % 2, c % 4, w_dram[c][0], staged[c % 2], c - 3 if c >= 4 else None)
            spans = [(peeled, C_MRG, 1), (C_MRG, C_OUT2, 3), (C_OUT2, C_END, 1)]
            for c_from, c_to, kind in spans:
                if kind == 3:
                    with pool.Fori(0, (c_to - c_from) // 12) as i:
                        loads = [0, 0]
                        for k in range(12):
                            c = c_from + k
                            loads[c % 2] += 32 if k % 3 == 2 else 16
                            split(i * 12 + c, c % 2, c % 4, WCH, i * 128 + (staged[c % 2] + loads[c % 2]),
                                  i * 12 + (c - 3))
                    staged = [staged[0] + 256, staged[1] + 256]
                else:
                    whole = (c_to - c_from) // 4 * 4
                    with pool.Fori(0, whole // 4) as i:
                        for k in range(4):
                            c = c_from + k
                            split(i * 4 + c, c % 2, c % 4, WCH, i * 32 + (staged[c % 2] + 16 * (k // 2 + 1)),
                                  i * 4 + (c - 3))
                    staged = [staged[0] + 8 * whole, staged[1] + 8 * whole]
                    for c in range(c_from + whole, c_to):
                        staged[c % 2] += 16
                        split(c, c % 2, c % 4, WCH, staged[c % 2], c - 3)

        @block.tensor
        def _(pe):
            n_nt, n_tm, n_fm = 0, 0, 0

            def settle(nt=0, tm=0, fm=0):
                for name, count in (("nt_free", nt), ("tm_free", tm), ("fm_free", fm)):
                    if count:
                        pe.wait_ge(S[name], count)

            def three(dst, sh, sl, mh, ml, first, last):
                pe.matmul(dst, sh, mh, start=first, stop=False)
                pe.matmul(dst, sh, ml, start=False, stop=False)
                return pe.matmul(dst, sl, mh, start=False, stop=last)

            def transpose_tile(n, n0, first_use, rows=P):
                pe.wait_ge(S["nt_xn"], n + 1)
                if n - first_use >= 2:
                    pe.wait_ge(S["nt_free"], n - 1)
                for k in range(KT):
                    ins = pe.transpose(pair_tiles(n % 2)[:, k, 0:rows], XN[first_use][0:rows, n % 2, P * k:P * k + P],
                                       IDENT[0:rows, 0:rows])
                ins.then_inc(S["nt_mm"], 1)

            def tm_units(t0, units, c0, chunks, ncols, stat, after=None):
                for u in range(units):
                    n = t0 + u
                    if u >= 4:
                        pe.wait_ge(S["tm_free"], n - 3)
                    d = None
                    for j in range(chunks):
                        if u == 0:
                            pe.wait_ge(S["w_split"], c0 + j + 1)
                        mh, ml = slot(c0 + j)
                        for q in range(WCH // ncols):
                            k = j * (WCH // ncols) + q
                            sh, sl = stat(u, k)
                            if d is None:
                                d = PB[0:sh.shape[1], tm_bank(n), 0:ncols]
                            ins = three(d, sh, sl, mh[:, q * ncols:(q + 1) * ncols],
                                        ml[:, q * ncols:(q + 1) * ncols], k == 0, k == KT - 1)
                        if u == units - 1:
                            ins.then_inc(S["w_used"], 1)
                    if u < units - 1:
                        ins.then_inc(S["tm_mm"], 1)
                    if after is not None:
                        after(u)

            def fm_unit(n, wait, c, mov):
                pe.wait_ge(S["w_split"], c + 1)
                if wait:
                    pe.wait_ge(S["fm_free"], n - 3)
                sh, sl = slot(c)
                for h in range(2):
                    for k in range(KT):
                        mh, ml = mov(k, h)
                        ins = three(PB[:, 2 * (n % 4) + h, :], sh[:, P * k:P * k + P], sl[:, P * k:P * k + P],
                                    mh, ml, k == 0, k == KT - 1)
                return ins

            pe.wait_ge(S["consts"], 16 * N_CONSTS)
            pe.wait_ge(S["vec_in"], 48)
            for i in range(3):
                ins = pe.transpose(PB[:, 7, VROWS * i:VROWS * (i + 1)], VROW[:, i, :], IDENT[0:VROWS, 0:VROWS])
            ins.then_inc(S["vec_t"], 1)

            for t in range(KTILES):
                transpose_tile(N_U + t, N_U, N_U, tokens_of(t)[1])
            settle(nt=KTILES)
            pe.wait_ge(S["cw_in"], 16 * 9)
            for i in range(2):
                ins = pe.matmul(PB[:, i, :], CWRAW[:, i, :], WBD[:, :, :].rearrange("p j n -> p (j n)"),
                                start=True, stop=True)
            ins.then_inc(S["cw_mm"], 1)
            pe.wait_ge(S["vec_done"], 1)
            pe.wait_ge(S["fold_done"], 2 * KT)

            def fold_stat(u, k):
                h, first, rows = folded(u)
                return AF[:, 0, k, first:first + rows], AF[:, 1, k, first:first + rows]

            tm_units(T_FIN, 2 * NF, C_FIN, 4, FW, fold_stat)

            pe.wait_ge(S["tail_done"], 1)
            pe.wait_ge(S["tm_free"], 2 * NF)
            for h in range(2):
                for kind in range(2):
                    c = C_DFT + 2 * h + kind
                    pe.wait_ge(S["w_split"], c + 1)
                    mh, ml = slot(c)
                    for ct in range(4):
                        n = T_DFT + 16 * h + 4 * kind + ct
                        pe.wait_ge(S["tm_free"], n - 3)
                        for i in range(NF):
                            sh, sl = (FC[:, x, kind, i, P * ct:P * ct + P] for x in range(2))
                            vh, vl = ((v[:, HALF * i:HALF * (i + 1)] for v in (mh, ml)) if i < 4 else
                                      (TAIL[:, x, 2 * h + kind, :] for x in range(2)))
                            ins = three(PB[:, tm_bank(n), 0:HALF], sh, sl, vh, vl, i == 0, i == NF - 1)
                        ins.then_inc(S["w_used"] if ct == 3 else S["tm_mm"], 1)
                pe.wait_ge(S["tm_free"], T_DFT + 16 * h + 8)
                pe.wait_ge(S["cw_done"], 2)
                for j in range(4):
                    for kind in range(2):
                        n = T_DFT + 16 * h + 8 + 2 * j + kind
                        pe.wait_ge(S["tm_free"], n - 3)
                        three(PB[:, tm_bank(n), 0:HALF], CW[:, 0, kind, j, :], CW[:, 1, kind, j, :],
                              DE[:, 0, kind, j, :], DE[:, 1, kind, j, :], True, True).then_inc(S["tm_mm"], 1)

            for t in range(KTILES):
                transpose_tile(N_A1 + t, N_A1, N_A1, tokens_of(t)[1])

            def a1_half(k, h):
                return (A1[:, x, k, META + FW * h:META + FW * (h + 1)] for x in range(2))

            def a1_stat(u, k):
                first, rows = tokens_of(u)
                return A1[:, 0, k, first:first + rows], A1[:, 1, k, first:first + rows]

            settle(nt=N_A1 + KTILES, tm=T_KV)
            for f in range(4):
                fm_unit(U_FGATE + f, False, C_FGATE + f, a1_half).then_inc(S["w_used"], 1)
            settle(fm=4)

            def turn_k(u):
                rows = tokens_of(u)[1]
                pe.wait_ge(S["pr_rope"], u + 1)
                if u >= 2:
                    pe.wait_ge(S["kv_kll"], 2 * (u - 1))
                for g in range(KV_HEADS):
                    ins = pe.transpose(pair_tiles(u % 2)[0:DH, g, 0:rows], RQ[0:rows, u % 2, DH * g:DH * g + DH],
                                       IDENT[0:rows, 0:rows])
                ins.then_inc(S["pr_t"], 1)

            def turn_q(u):
                pe.wait_ge(S["pr_rope"], KTILES + u + 1)
                if u >= 2:
                    pe.wait_ge(S["pr_done"], u - 1)
                for g in range(HEADS):
                    ins = pe.transpose(pair_tiles(u % 2)[0:DH, g, :], RQ[:, (KTILES + u) % 2, DH * g:DH * g + DH],
                                       IDENT[:, :])
                ins.then_inc(S["pr_t"], 1)

            tm_units(T_KV, KTILES, C_KV, 2, 256, a1_stat, lambda u: turn_k(u - 1) if u else None)
            turn_k(KTILES - 1)
            pe.wait_ge(S["kv_kll"], 2 * KTILES)
            tm_units(T_Q, TT, C_Q, 4, FW, a1_stat, lambda u: turn_q(u - 1) if u else None)
            turn_q(TT - 1)
            pe.wait_ge(S["pr_done"], TT)
            settle(tm=T_OUT)
            for f in range(4):
                fm_unit(U_AGATE + f, False, C_AGATE + f, a1_half).then_inc(S["w_used"], 1)
            settle(fm=8)

            def scores(i):
                h, t = divmod(i, TT)
                if i:
                    pe.wait_ge(S["sc_exp"], i)
                for x, k2 in enumerate((KHH, KLL)):
                    for b in range(3):
                        ins = pe.matmul(PB[:, b, 0:KPART], QS[:, h, P * t:P * t + P],
                                        k2[:, h // GROUP, KPART * b:KPART * (b + 1)], start=x == 0, stop=x == 1)
                ins.then_inc(S["sc_mm"], 1)

            def turn_probs(i):
                pe.wait_ge(S["sc_exp"], i + 1)
                for g in range(3):
                    if i:
                        pe.wait_ge(S["pt_lo"], 3 * (i - 1) + g + 1)
                    for kt in range(4 * g, min(4 * g + 4, KTILES)):
                        first, rows = tokens_of(kt)
                        ins = pe.transpose(PB[0:rows, 3 + g, P * (kt % 4):P * (kt % 4) + P],
                                           PR[:, i % 2, first:first + rows], IDENT[:, :])
                    ins.then_inc(S["pt_mm"], 1)

            def attend(p, part):
                g = p // 4 // GROUP
                if part == 0:
                    pe.wait_ge(S["pt_lo"], 6 * (p + 1))
                    if p >= 2:
                        pe.wait_ge(S["o_out"], p - 1)
                dst = PB[:, 6 + p % 2, 0:PAIR]
                for kt in (range(5), range(5, KTILES))[part]:
                    ph, pl = (PT[:, x, kt, PAIR * (p % 2):PAIR * (p % 2) + PAIR] for x in range(2))
                    pe.matmul(dst, VV[:, kt, g, 0:P], ph, start=kt == 0, stop=False)
                    pe.matmul(dst[0:DH, :], VV[:, kt, g, P:P + DH], ph, start=False, stop=False)
                    ins = pe.matmul(dst, VV[:, kt, g, 0:P], pl, start=False, stop=kt == KTILES - 1)
                if part:
                    ins.then_inc(S["av_mm"], 1)

            pe.wait_ge(S["kdup"], 2)
            scores(0)
            for i in range(1, HEADS * TT + 3):
                if i < HEADS * TT:
                    scores(i)
                if i <= HEADS * TT:
                    turn_probs(i - 1)
                if i >= 3:
                    attend((i - 3) // 2, (i - 3) % 2)
            pe.wait_ge(S["o_out"], PAIRS)
            pe.wait_ge(S["o_lo"], PAIRS)
            pe.wait_ge(S["mf_done"], 4)

            def mix_stat(u, k):
                m = MIXF if k < 4 else MIXA
                return (m[:, x, k % 4, P * u:P * u + P] for x in range(2))

            for c in range(2):
                tm_units(T_OUT + TT * c, TT, C_OUT + 4 * c, 4, FW, mix_stat)
                settle(tm=T_OUT + TT * (c + 1))

            for t in range(TT):
                transpose_tile(N_A2 + t, N_A2, N_A2)
            settle(nt=N_A3)

            def a2_stat(u, k):
                return (A2[:, x, k, P * u:P * u + P] for x in range(2))

            def a2_half(k, h):
                return (A2[:, x, k, FW * h:FW * (h + 1)] for x in range(2))

            tm_units(T_V2, TT, C_V2, 4, FW, a2_stat)
            settle(tm=T_OUT2)
            for f in range(8):
                fm_unit(U_QK2 + f, f >= 4, C_QK2 + f, a2_half).then_inc(S["w_used"], 1)
            settle(fm=U_CONV)

            def stick_scores(i):
                h, t = divmod(i, TT)
                n = P * (t + 1)
                if t == 0:
                    pe.wait_ge(S["st_a"], 3 * (h + 1) + 2)
                    pe.wait_ge(S["st_v"], 3 * (h + 1))
                if i >= 2:
                    pe.wait_ge(S["z_e"], i - 1)
                for b in range((n + FW - 1) // FW):
                    lo, hi = FW * b, min(n, FW * (b + 1))
                    q = QS2[h % 2][:, P * t:P * t + P]
                    pe.matmul(PB[:, 2 * (i % 2) + b, 0:hi - lo], q, KHH2[h % 2][:, lo:hi], start=True, stop=False)
                    pe.matmul(PB[:, 2 * (i % 2) + b, 0:hi - lo], q, KLL2[h % 2][:, lo:hi], start=False, stop=hi < n)
                ins = pe.matmul(PB[:, 2 * (i % 2) + b, hi - lo - P:hi - lo], IDR[:, :], CAUSAL[:, :],
                                start=False, stop=True)
                ins.then_inc(S["z_mm"], 1)

            def turn_weights(i):
                t = i % TT
                pe.wait_ge(S["z_w"], i + 1)
                for g in range(t // 4 + 1):
                    n = turned(i) + g
                    if n >= 2:
                        pe.wait_ge(S["wt_lo"], n - 1)
                    for kt in range(4 * g, min(4 * g + 4, t + 1)):
                        ins = pe.transpose(PB[:, 4 + n % 2, P * (kt % 4):P * (kt % 4) + P],
                                           ZS[:, i % 2, P * kt:P * kt + P], IDENT[:, :])
                    ins.then_inc(S["wt_mm"], 1)

            def stick_attend(p, part):
                h, c2 = p // 4, 2 * (p % 4)
                if part == 0:
                    pe.wait_ge(S["wt_lo"], turned(2 * p + 2))
                    if p >= 2:
                        pe.wait_ge(S["at_out"], p - 1)
                for kt in (range(c2 // 2 + 1), range(c2 // 2 + 1, c2 + 2))[part]:
                    q0 = P if kt > c2 else 0
                    vh, vl = (V2[:, x, kt, DH * h:DH * h + DH] for x in range(2))
                    wh, wl = (WT[:, x, kt, PAIR * (p % 2) + q0:PAIR * (p % 2) + PAIR] for x in range(2))
                    ins = three(PB[0:DH, 6 + p % 2, q0:PAIR], vh, vl, wh, wl,
                                kt == 0, kt == c2 + 1)
                if part:
                    ins.then_inc(S["av2_mm"], 1)

            stick_scores(0)
            for i in range(HEADS * TT + 4):
                if i + 1 < HEADS * TT:
                    stick_scores(i + 1)
                if i >= 4:
                    stick_attend((i - 4) // 2, i % 2)
                if 1 <= i <= HEADS * TT:
                    turn_weights(i - 1)
            pe.wait_ge(S["at_out"], PAIRS)

            for t in range(TT):
                transpose_tile(N_A3 + t, N_A3, N_A3)
            settle(nt=N_A4)
            for f in range(12):
                fm_unit(U_CONV + f, f >= 4, C_CONV + f, a2_half).then_inc(S["w_used"], 1)
            for f in range(KT):
                u, c = U_MRG + 4 * f, C_MRG + 3 * f
                fm_unit(u, True, c, a2_half).then_inc(S["w_used"], 1)
                fm_unit(u + 1, True, c + 1, a2_half).then_inc(S["w_used"], 1)
                pe.wait_ge(S["w_split"], c + 3)
                pe.wait_ge(S["at_done"], 4)
                pe.wait_ge(S["cv_done"], 4)
                sh, sl = slot(c + 2)
                for br, m in enumerate((ATS, CTS)):
                    pe.wait_ge(S["fm_free"], u + 2 + br - 3)
                    for h in range(2):
                        for k in range(4):
                            q = 4 * br + k
                            ins = three(PB[:, 2 * ((u + 2 + br) % 4) + h, :], sh[:, P * q:P * q + P],
                                        sl[:, P * q:P * q + P], m[:, 0, k, FW * h:FW * (h + 1)],
                                        m[:, 1, k, FW * h:FW * (h + 1)], k == 0, k == 3)
                ins.then_inc(S["w_used"], 1)
            settle(fm=U_UP)

            def mr_stat(u, k):
                return (MR[:, x, k, P * u:P * u + P] for x in range(2))

            pe.wait_ge(S["mr_done"], KT)
            for c in range(2):
                tm_units(T_OUT2 + TT * c, TT, C_OUT2 + 4 * c, 4, FW, mr_stat)
                settle(tm=T_OUT2 + TT * (c + 1))
            for t in range(TT):
                transpose_tile(N_A4 + t, N_A4, N_A4)
            settle(nt=N_A4 + TT)

            with pe.Fori(0, FT // 2) as i:
                for s in range(4):
                    pe.wait_ge(S["w_split"], i * 4 + (C_UP + s + 1))
                    pe.wait_ge(S["fm_free"], i * 4 + (U_UP + s - 3))
                    for h in range(2):
                        for k in range(KT):
                            ins = three(PB[:, 2 * s + h, :], WR[:, (C_UP + s) % 4, 0, P * k:P * k + P],
                                        WR[:, (C_UP + s) % 4, 1, P * k:P * k + P], A4[:, 0, k, FW * h:FW * (h + 1)],
                                        A4[:, 1, k, FW * h:FW * (h + 1)], k == 0, k == KT - 1)
                    ins.then_inc(S["w_used"], 1)
            pe.wait_ge(S["fm_free"], U_UP + 2 * FT)

            for half in range(2):
                if half:
                    pe.wait_ge(S["dn_ya"], 4)
                    pe.wait_ge(S["dn_yv"], 4)

                def down(j, s, first=False, last=False):
                    c = C_DOWN + FT * half
                    pe.wait_ge(S["w_split"], j + (c + 1))
                    pe.wait_ge(S["dn_lo"], j + (FT * half + 1))
                    r = (c + s) % 4
                    for t in range(4):
                        sh, sl = (FS[:, s % 2, x, P * t:P * t + P] for x in range(2))
                        for g in range(2):
                            ins = three(PB[:, 2 * t + g, :], sh, sl, WR[:, r, 0, FW * g:FW * (g + 1)],
                                        WR[:, r, 1, FW * g:FW * (g + 1)], first, last)
                    ins.then_inc(S["w_used"], 1)

                down(0, 0, first=True)
                down(1, 1)
                with pe.Fori(0, (FT - 4) // 4) as i:
                    for s in range(2, 6):
                        down(i * 4 + s, s)
                for s in range(FT - 4, FT):
                    down(s, s, last=s == FT - 1)

        @block.scalar
        def _(act):
            chain = [0]
            jobs = [0, 0]

            def link(ins):
                chain[0] += 1
                ins.then_inc(S["a_chain"], 1)
                act.wait_ge(S["a_chain"], chain[0])

            def load_tables():
                act.add_instruction(mybir.InstLoadActFuncSet(
                    name=nc.get_next_instruction_name(), act_func_set_id=EXP_AND_LN,
                    engine=mybir.EngineType.Activation, ins=[], outs=[]))

            def guess(rows, col, n, scale, by_vector):
                if by_vector:
                    jobs[1] += 1
                    act.wait_ge(S["rs_ss"], jobs[1])
                link(act.activation(LN[0:rows, col:col + n], SS[0:rows, col:col + n], ACT.Ln, bias=EPS, scale=scale))
                jobs[0] += 1
                act.activation(YY[0:rows, col:col + n], LN[0:rows, col:col + n], ACT.Exp,
                               scale=-0.5).then_inc(S["rs_y"], 1)

            def ready(n):
                name, value = TM[n]
                act.wait_ge(S[name], value)

            def x_rows(t):
                return a["x"][0, P * t:P * t + P, :] if t < TT else a["meta_tokens"]

            def load_tile(use, t, src, wait=None):
                if wait is not None:
                    act.wait_ge(S["nt_xn"], wait)
                act.dma_start(XIN[use][0:src.shape[0], (use + t) % 2, :], src).then_inc(S[f"nt_in{(use + t) % 2}"], 16)

            load_tables()
            load_tile(N_U, 0, x_rows(0))
            load_tile(N_U, 1, x_rows(1))
            act.dma_start(GB[N_U][:, :], a["norm_g"][0, :].partition_broadcast(P)).then_inc(S["consts"], 16)
            act.dma_start(IDENT[:, :], const["ident"]).then_inc(S["consts"], 16)
            act.dma_start(ROPER[:, :, :, :], const["rope"]).then_inc(S["rope_in"], 16)
            act.dma_start(GAINS[:, 0, :], a["q_norm_g"][0, :].partition_broadcast(P)).then_inc(S["rope_in"], 16)
            act.dma_start(GAINS[:, 1, :], a["k_norm_g"][0, :].partition_broadcast(P)).then_inc(S["rope_in"], 16)
            act.wait_ge(S["vec_zero"], 1)
            nf = 2 * FT
            act.dma_start(VROW[0:nf, :, :], a["conv_ffn_w_2"][0].rearrange("i (m p) -> m i p", p=P)).then_inc(S["vec_in"], 16)
            act.dma_start(VROW[nf:nf + 4, :, :], a["conv_mix_w_2"][0].rearrange("i (m p) -> m i p", p=P)).then_inc(S["vec_in"], 16)
            act.dma_start(VROW[nf + 4:nf + 8, 0, :], a["b_fmix"][0].rearrange("(m g) d -> m (g d)", g=2)).then_inc(S["vec_in"], 16)
            act.dma_start(CWRAW[:, :, :], const["channel"]).then_inc(S["cw_in"], 16)
            act.wait_ge(S["cw_zero"], 1)
            for g in range(8):
                r = DH * (g % 2)
                act.dma_start(WBD[r:r + DH, g // 2, r:r + DH], a["w_fmix"][0, g]).then_inc(S["cw_in"], 16)

            for t in range(KTILES + 1):
                if t < KTILES:
                    rows = tokens_of(t)[1]
                    act.wait_ge(S[f"nt_in{t % 2}"], 16 * (t // 2 + 1))
                    if t >= 2:
                        act.wait_ge(S["nt_mm"], t - 1)
                    link(act.activation(XN[N_U][0:rows, t % 2, :], XIN[N_U][0:rows, t % 2, :], ACT.Square,
                                        accum_out=SS[0:rows, t:t + 1]))
                    guess(rows, t, 1, 1.0 / D, False)
                if t:
                    first, rows = tokens_of(t - 1)
                    act.wait_ge(S["nt_mm"], t)
                    act.activation(UT[:, :, first:first + rows], pair_tiles((t - 1) % 2)[:, :, 0:rows],
                                   ACT.Copy).then_inc(S["nt_free"], 1)
                if t + 2 < KTILES:
                    load_tile(N_U, t + 2, x_rows(t + 2), t + 1)

            act.wait_ge(S["nt_xn"], KTILES)
            act.wait_ge(S["nt_mm"], KTILES)
            act.dma_start(TAILR[:, :, :], const["dft_tail"]).then_inc(S["tail_in"], 16)
            for j in range(2 * KT):
                k, h = divmod(j, 2)
                n = FOLD + 1 - 2 * h
                act.wait_ge(S["fold_sum"], j + 1)
                act.activation(AF[:, 0, k, FOLDS * h:FOLDS * h + n], FSUM[:, h, 0:n], ACT.Copy).then_inc(S["fold_hi"], 1)
            act.wait_ge(S["cw_mm"], 1)
            for i in range(2):
                act.activation(CW[:, 0, i, :, :], PB[:, i, :].rearrange("p (j n) -> p j n", j=4),
                               ACT.Copy).then_inc(S["cw_hi"], 1)
            act.wait_ge(S["tail_in"], 16)
            act.activation(TAIL[:, 0, :, :], TAILR[:, :, :], ACT.Copy).then_inc(S["tail_hi"], 1)

            act.wait_ge(S["fpad"], 1)
            for u in range(2 * NF):
                h, _, rows = folded(u)
                ready(T_FIN + u)
                act.activation(FC[0:rows, 0, h, u % NF, :], PB[0:rows, tm_bank(T_FIN + u), :],
                               ACT.Copy).then_inc(S["tm_hi"], 1)
            for h in range(2):
                for m in range(8):
                    n = T_DFT + 16 * h + m
                    if h and m == 0:
                        ready(T_DFT + 15)
                    ready(n)
                    act.activation(DE[:, 0, m // 4, m % 4, :], PB[:, tm_bank(n), 0:HALF], ACT.Copy).then_inc(S["tm_hi"], 1)
                for j in range(4):
                    n = T_DFT + 16 * h + 8 + 2 * j
                    ready(n)
                    if j >= 2 or h:
                        act.wait_ge(S["tm_free"], n - 2 if j >= 2 else T_DFT + 16)
                    act.activation(CHA[:, j % 2, :], PB[:, tm_bank(n), 0:HALF], ACT.Identity,
                                   bias=VEC[:, 0, nf + 4 + j:nf + 5 + j]).then_inc(S["ch_a"], 1)

            act.wait_ge(S["w_used"], C_DFT + 4)
            act.wait_ge(S["tm_free"], T_KV)
            load_tile(N_A1, 0, x_rows(0))
            load_tile(N_A1, 1, x_rows(1))
            for t in range(KTILES):
                n = N_A1 + t
                first, rows = tokens_of(t)
                if t + 2 < KTILES:
                    load_tile(N_A1, t + 2, x_rows(t + 2), n + 1)
                act.wait_ge(S["nt_mm"], n + 1)
                act.activation(A1[:, 0, :, first:first + rows], pair_tiles(n % 2)[:, :, 0:rows],
                               ACT.Copy).then_inc(S["nt_hi"], 1)

            for f in range(4):
                act.wait_ge(S["w_used"], C_FGATE + f + 1)
                if f >= 2:
                    act.wait_ge(S["gate_out"], f - 1)
                act.activation(GE[:, f % 2, :], pair(f), ACT.Sigmoid).then_inc(S["gate_sig"], 1)
                if f:
                    act.wait_ge(S["gate_out"], f)
                    act.dma_start(scratch["mixed_f"][P * (f - 1):P * f, :], FT1[:, f - 1, :]).then_inc(S["gate_stored"], 16)
            act.wait_ge(S["gate_out"], 4)
            act.dma_start(scratch["mixed_f"][3 * P:4 * P, :], FT1[:, 3, :]).then_inc(S["gate_stored"], 16)

            load_tables()
            act.wait_ge(S["gate_stored"], 64)
            act.wait_ge(S["vv_set"], 3)
            for u in range(KTILES + 1):
                if u < KTILES:
                    rows = tokens_of(u)[1]
                    n = T_KV + u
                    col = 8 * (u % 2)
                    ready(n)
                    act.activation(SQ[0:rows, u % 2, 0:P], PB[0:rows, tm_bank(n), 0:P], ACT.Square).then_inc(S["pr_sq"], 1)
                    act.activation(VV[0:rows, u, :, 0:DH],
                                   PB[0:rows, tm_bank(n), P:2 * P].rearrange("p (g d) -> p g d", g=KV_HEADS),
                                   ACT.Copy).then_inc(S["kv_vhi"], 1)
                    guess(rows, col, KV_HEADS, 1.0 / DH, True)
                if u:
                    first, rows = tokens_of(u - 1)
                    act.wait_ge(S["pr_t"], u)
                    for x in range(2):
                        act.activation(KHH[DH * x:DH * x + DH, :, first:first + rows],
                                       pair_tiles((u - 1) % 2)[0:DH, 0:KV_HEADS, 0:rows], ACT.Copy).then_inc(S["kv_khh"], 1)
            for u in range(TT + 1):
                if u < TT:
                    n = T_Q + u
                    ready(n)
                    act.activation(SQ[:, (KTILES + u) % 2, :], PB[:, tm_bank(n), :], ACT.Square).then_inc(S["pr_sq"], 1)
                    guess(P, 8 * ((KTILES + u) % 2), HEADS, 1.0 / DH, True)
                if u:
                    act.wait_ge(S["pr_t"], KTILES + u)
                    act.activation(QS[0:DH, :, P * (u - 1):P * u], pair_tiles((u - 1) % 2)[0:DH, :, :],
                                   ACT.Copy).then_inc(S["pr_hi"], 1)
            for f in range(4):
                act.wait_ge(S["w_used"], C_AGATE + f + 1)
                if f >= 2:
                    act.wait_ge(S["gate_stored"], 64 + 16 * (f - 1))
                act.activation(GE2[:, f % 2, :], pair(f), ACT.Sigmoid).then_inc(S["gate_sig"], 1)
                if f:
                    act.wait_ge(S["gate_out"], 4 + f)
                    act.dma_start(scratch["a_gate"][P * (f - 1):P * f, :], GE2[:, (f - 1) % 2, :]).then_inc(S["gate_stored"], 16)
            act.wait_ge(S["gate_out"], 8)
            act.dma_start(scratch["a_gate"][3 * P:4 * P, :], GE2[:, 1, :]).then_inc(S["gate_stored"], 16)

            def load_a_gate(b):
                h, c = divmod(b, 2)
                r = DH * (h % 2)
                act.dma_start(AG[r:r + DH, b % 2, :], scratch["a_gate"][DH * h:DH * h + DH, FW * c:FW * c + FW])\
                   .then_inc(S[f"ag_in{b % 2}"], 16)

            def probs_hi(i):
                t = i % 4
                if t % 2 == 0 and i >= 4:
                    act.wait_ge(S["av_mm"], i // 2 - 1)
                for g in range(3):
                    n = 3 * i + g
                    act.wait_ge(S["pt_mm"], n + 1)
                    rows = P if g < 2 else META
                    kts = slice(4 * g, min(4 * g + 4, KTILES))
                    act.activation(PT[0:rows, 0, kts, P * t:P * t + P],
                                   PB[0:rows, 3 + g, 0:P * (4 if g < 2 else 1)].rearrange("p (k n) -> p k n", n=P),
                                   ACT.Copy).then_inc(S["pt_hi"], 1)

            def row_sum_inv(p):
                act.wait_ge(S["av_mm"], p + 1)
                if p >= 2:
                    act.wait_ge(S["o_out"], p - 1)
                rc = RC[:, PAIR * (p % 2):PAIR * (p % 2) + PAIR]
                link(act.activation(rc, PB[DH:P, 6 + p % 2, 0:PAIR], ACT.Ln))
                act.activation(rc, rc, ACT.Exp, scale=-1.0).then_inc(S["o_inv"], 1)

            def attended_hi(p):
                row, col, buf = pair_place(p)
                act.wait_ge(S["o_out"], p + 1)
                act.activation(MIXA[row, 0, p // 8, col], OT[row, buf, :], ACT.Copy).then_inc(S["o_hi"], 1)
                if p % 2 and p // 2 + 2 < 2 * HEADS:
                    load_a_gate(p // 2 + 2)

            act.wait_ge(S["gate_stored"], 128)
            load_a_gate(0)
            load_a_gate(1)
            act.wait_ge(S["pt_zero"], 1)
            for i in range(HEADS * TT):
                if i:
                    probs_hi(i - 1)
                act.wait_ge(S["sc_max"], i + 1)
                act.activation(PR[:, i % 2, :].rearrange("p (b n) -> p b n", b=3), PB[:, 0:3, 0:KPART], ACT.Exp,
                               bias=NB[:, i % 2:i % 2 + 1], scale=DH ** -0.5).then_inc(S["sc_exp"], 1)
                if i >= 5 and i % 2:
                    row_sum_inv((i - 5) // 2)
                if i >= 8 and i % 2 == 0:
                    attended_hi((i - 8) // 2)
            probs_hi(HEADS * TT - 1)
            row_sum_inv(PAIRS - 2)
            attended_hi(PAIRS - 4)
            attended_hi(PAIRS - 3)
            row_sum_inv(PAIRS - 1)
            attended_hi(PAIRS - 2)
            attended_hi(PAIRS - 1)
            act.dma_start(MFR[:, :, :], scratch["mixed_f"].rearrange("(k p) n -> p k n", p=P)).then_inc(S["mf_in"], 16)
            act.dma_start(GF[:, :], a["final_g"].partition_broadcast(P)).then_inc(S["gains_in"], 16)
            act.dma_start(GB[N_A2][:, :], a["norm_mix_pre_2"][0, :].partition_broadcast(P)).then_inc(S["gains_in"], 16)
            act.wait_ge(S["mf_in"], 16)
            act.wait_ge(S["av_mm"], PAIRS)
            for f in range(4):
                act.activation(MIXF[:, 0, f, :], MFR[:, f, :], ACT.Copy).then_inc(S["mf_hi"], 1)

            def load_residual(m):
                c, u = divmod(m, TT)
                act.dma_start(XR[:, m % 2, :], a["x"][0, P * u:P * u + P, FW * c:FW * c + FW]).then_inc(S[f"op_in{m % 2}"], 16)

            load_residual(0)
            load_residual(1)
            for m in range(2, 2 * TT):
                act.wait_ge(S["tm_free"], T_OUT + m - 1)
                load_residual(m)

            def hi_of_tile(n, dst, t):
                act.wait_ge(S["nt_mm"], n + 1)
                act.activation(dst[:, 0, :, P * t:P * t + P], pair_tiles(n % 2), ACT.Copy).then_inc(S["nt_hi"], 1)

            load_tables()
            act.wait_ge(S["tm_free"], T_V2)
            for s in range(TT + 2):
                if s < TT:
                    link(act.activation(JUNK[:, :], H[:, s, :], ACT.Square, accum_out=SS[:, s:s + 1]))
                    guess(P, s, 1, 1.0 / D, False)
                if 1 <= s <= TT:
                    t = s - 1
                    act.wait_ge(S["x1_out"], t + 1)
                    act.dma_start(scratch["x1"][P * t:P * t + P, :], H[:, t, :]).then_inc(S["x1_stored"], 16)
                    link(act.activation(JUNK[:, :], H[:, t, :], ACT.Square, accum_out=SS[:, 8 + t:9 + t]))
                    guess(P, 8 + t, 1, 1.0 / D, False)
                if s >= 2:
                    hi_of_tile(N_A2 + s - 2, A2, s - 2)

            act.dma_start(CAUSALR[:, :], const["causal"]).then_inc(S["causal_in"], 16)
            act.wait_ge(S["x1_stored"], 16 * TT)
            act.wait_ge(S["nt_free"], N_A3)
            for u in range(TT):
                n = T_V2 + u
                ready(n)
                act.activation(V2[:, 0, u, :], PB[:, tm_bank(n), :], ACT.Copy).then_inc(S["tm_hi"], 1)
            for f in range(8):
                act.wait_ge(S["w_used"], C_QK2 + f + 1)
                act.activation((QT if f < 4 else KT2)[:, f % 4, :], pair((U_QK2 + f) % 4), ACT.Copy,
                               scale=DH ** -0.5 if f < 4 else 1.0).then_inc(S["fm_free"], 1)

            def stack_part(h, part):
                r = DH * (h % 2)
                if h >= 2:
                    act.wait_ge(S["z_mm"], TT * (h - 1))
                    act.wait_ge(S["st_v"], 3 * (h - 1))
                if part == 0:
                    act.activation(QS2[h % 2][r:r + DH, :], QT[r:r + DH, h // 2, :], ACT.Copy).then_inc(S["st_a"], 1)
                else:
                    q = (r, DH - r)[part - 1]
                    act.activation(KHH2[h % 2][q:q + DH, :], KT2[r:r + DH, h // 2, :], ACT.Copy).then_inc(S["st_a"], 1)

            def soft_part(i):
                t = i % TT
                n = P * (t + 1)
                b = ZL[:, i % 2, 0:n]
                act.wait_ge(S["z_mm"], i + 1)
                if i >= 2:
                    act.wait_ge(S["z_e"], i - 1)
                link(act.activation(b, pair(i % 2)[:, 0:n], ACT.Abs))
                link(act.activation(b, b, ACT.Exp, scale=-1.0))
                act.activation(b, b, ACT.Ln, bias=1.0).then_inc(S["z_l"], 1)

            def weights(i):
                n = P * (i % TT + 1)
                act.wait_ge(S["z_e"], i + 1)
                act.activation(ZS[:, i % 2, 0:n], ZS[:, i % 2, 0:n], ACT.Exp).then_inc(S["z_w"], 1)

            def weights_hi(i):
                t, c = i % TT, i % 4
                if c % 2 == 0 and i >= 4:
                    act.wait_ge(S["av2_mm"], i // 2 - 1)
                for g in range(t // 4 + 1):
                    n = turned(i) + g
                    w = min(4, t + 1 - 4 * g)
                    act.wait_ge(S["wt_mm"], n + 1)
                    act.activation(WT[:, 0, 4 * g:4 * g + w, P * c:P * c + P],
                                   PB[:, 4 + n % 2, 0:P * w].rearrange("p (k n) -> p k n", n=P),
                                   ACT.Copy).then_inc(S["wt_hi"], 1)

            act.wait_ge(S["causal_in"], 16)
            act.activation(CAUSAL[:, :], CAUSALR[:, :], ACT.Copy).then_inc(S["st_a"], 1)
            act.activation(IDR[:, :], IDENT[:, :], ACT.Copy).then_inc(S["st_a"], 1)
            act.wait_ge(S["fm_free"], U_CONV)
            for part in range(3):
                stack_part(0, part)
            for i in range(HEADS * TT + 2):
                if i < HEADS * TT:
                    soft_part(i)
                if 1 <= i <= HEADS * TT:
                    weights(i - 1)
                if i >= 2:
                    weights_hi(i - 2)
                if i % TT < 3 and i < (HEADS - 1) * TT:
                    stack_part(i // TT + 1, i % TT)

            def x1_rows(t):
                return scratch["x1"][P * t:P * t + P, :]

            act.wait_ge(S["at_out"], PAIRS)
            act.dma_start(GB[N_A3][:, :], a["norm_mix_pre_2"][0, :].partition_broadcast(P)).then_inc(S["gains_in"], 16)
            load_tile(N_A3, 0, x1_rows(0))
            load_tile(N_A3, 1, x1_rows(1))
            for f in range(4):
                act.activation(ATS[:, 0, f, :], AT[:, f, :], ACT.Copy).then_inc(S["at_hi"], 1)
            for t in range(TT):
                if t + 2 < TT:
                    load_tile(N_A3, t + 2, x1_rows(t + 2), N_A3 + t + 1)
                hi_of_tile(N_A3 + t, A2, t)

            act.wait_ge(S["at_done"], 4)
            act.wait_ge(S["nt_free"], N_A4)
            for f in range(5):
                if f < 4:
                    act.wait_ge(S["w_used"], C_CONV + 3 * f + 1)
                    if f:
                        act.wait_ge(S["fm_free"], U_CONV + 3 * f - 2)
                    act.activation(CCB[:, :], pair((U_CONV + 3 * f) % 4), ACT.Copy).then_inc(S["cv_cc"], 1)
                if f:
                    act.wait_ge(S["fm_free"], U_CONV + 3 * f)
                    act.activation(CTS[:, 0, f - 1, :], CO[:, :], ACT.Copy).then_inc(S["cv_hi"], 1)

            act.wait_ge(S["cv_done"], 4)
            for f in range(KT):
                if f:
                    act.wait_ge(S["mg_out"], f)
                for g in range(2):
                    act.wait_ge(S["w_used"], C_MRG + 3 * f + g + 1)
                    act.activation(MGE[:, g, :], pair((U_MRG + 4 * f + g) % 4), ACT.Sigmoid)\
                       .then_inc(S["fm_free"], 1)
                if f:
                    act.dma_start(scratch["merged"][P * (f - 1):P * f, :], MGO[:, (f - 1) % 2, :])\
                       .then_inc(S[f"mg_st{(f - 1) % 2}"], 16)
            act.wait_ge(S["mg_out"], KT)
            act.dma_start(scratch["merged"][P * (KT - 1):P * KT, :], MGO[:, 1, :]).then_inc(S["mg_st1"], 16)
            act.dma_start(GP[:, :], a["norm_mix_post_2"][0, :].partition_broadcast(P)).then_inc(S["gains2_in"], 16)
            act.dma_start(GB[N_A4][:, :], a["norm_ffn_pre_2"][0, :].partition_broadcast(P)).then_inc(S["gains2_in"], 16)
            act.wait_ge(S["mg_st0"], 64)
            act.wait_ge(S["mg_st1"], 64)
            act.wait_ge(S["w_used"], C_OUT2)
            for f in range(KT + 2):
                if f >= 2:
                    act.wait_ge(S[f"mr_in{f % 2}"], 16 * (f // 2))
                    act.activation(MR[:, 0, f - 2, :], MRR[:, f % 2, :], ACT.Copy).then_inc(S["mr_hi"], 1)
                    act.wait_ge(S["mr_done"], f - 1)
                if f < KT:
                    act.dma_start(MRR[:, f % 2, :], scratch["merged"][P * f:P * f + P, :]).then_inc(S[f"mr_in{f % 2}"], 16)
            for m in range(2 * TT):
                c, u = divmod(m, TT)
                n = T_OUT2 + m
                ready(n)
                act.activation(Y[:, u, FW * c:FW * c + FW], PB[:, tm_bank(n), :], ACT.Copy).then_inc(S["tm_free"], 1)

            def load_x1(t):
                act.dma_start(XRR[:, t % 2, :], x1_rows(t)).then_inc(S[f"xr_in{t % 2}"], 16)

            load_tables()
            load_x1(0)
            load_x1(1)
            act.wait_ge(S["tm_free"], T_OUT2 + 2 * TT)
            for s in range(TT + 2):
                if s < TT:
                    link(act.activation(JUNK2[:, :], Y[:, s, :], ACT.Square, accum_out=SS[:, s:s + 1]))
                    guess(P, s, 1, 1.0 / D, False)
                if 1 <= s <= TT:
                    t = s - 1
                    act.wait_ge(S["x2_out"], t + 1)
                    act.dma_start(scratch["x2"][P * t:P * t + P, :], Y[:, t, :]).then_inc(S["x2_stored"], 16)
                    if t + 2 < TT:
                        load_x1(t + 2)
                    link(act.activation(JUNK2[:, :], Y[:, t, :], ACT.Square, accum_out=SS[:, 8 + t:9 + t]))
                    guess(P, 8 + t, 1, 1.0 / D, False)
                if s >= 2:
                    hi_of_tile(N_A4 + s - 2, A4, s - 2)

            act.wait_ge(S["x2_stored"], 16 * TT)
            act.wait_ge(S["nt_free"], N_A4 + TT)
            with act.Fori(0, FT // 2) as i:
                for s in range(4):
                    q, g = divmod(s, 2)
                    act.wait_ge(S["w_used"], i * 4 + (C_UP + s + 1))
                    act.wait_ge(S["up_f"], i * 2 + (q + 1))
                    act.activation(UB[:, g, :], pair(s), ACT.Copy,
                                   scale=VEC[:, 2, bass.ds(i * 2 + (q + FT * g), 1)]).then_inc(S["up_c"], 1)
                    if g:
                        act.wait_ge(S["fm_free"], i * 4 + (U_UP + s + 1))
                        act.activation(UB[:, 1, :], UB[:, 1, :], ACT.Gelu_apprx_tanh).then_inc(S["up_g"], 1)

            def load_x2(m):
                act.dma_start(XF[:, m % 2, :], scratch["x2"][P * m:P * m + P, :]).then_inc(S[f"xf_in{m % 2}"], 16)

            def mid_hi(half, j, s):
                act.wait_ge(S["w_used"], j + (C_DOWN + FT * half - 1))
                act.activation(FS[:, s, 0, :], FFT[:, bass.ds(j, 1), FW * half:FW * half + FW].rearrange("p a n -> p (a n)")
                               if not isinstance(j, int) else FFT[:, j, FW * half:FW * half + FW],
                               ACT.Copy).then_inc(S["dn_hi"], 1)

            def finish(half):
                for s in range(5):
                    if s < 4:
                        link(act.activation(JUNK3[:, :], Y2[:, s, :], ACT.Square, accum_out=SS[:, s:s + 1]))
                        guess(P, s, 1, 1.0 / D, False)
                    if s:
                        m = 4 * half + s - 1
                        act.wait_ge(S["f_out"], m + 1)
                        act.dma_start(out[0, P * m:P * m + P, :], Y2[:, s - 1, :]).then_inc(S["f_stored"], 16)
                        if m + 2 < TT:
                            load_x2(m + 2)

            act.wait_ge(S["w_used"], C_DOWN)
            act.wait_ge(S["up_f"], FT + 1)
            load_tables()
            act.dma_start(GL[:, :], a["norm_ffn_post_2"][0, :].partition_broadcast(P)).then_inc(S["gains3_in"], 16)
            load_x2(0)
            load_x2(1)
            for half in range(2):
                mid_hi(half, 0, 0)
                mid_hi(half, 1, 1)
                if half:
                    finish(0)
                with act.Fori(1, FT // 2) as i:
                    for s in range(2):
                        mid_hi(half, i * 2 + s, s)
                act.wait_ge(S["w_used"], C_DOWN + FT * (half + 1))
                if half:
                    act.wait_ge(S["f_stored"], 64)
                for t in range(4):
                    act.activation(Y2[:, t, 0:FW], PB[:, 2 * t, :], ACT.Copy).then_inc(S["dn_ya"], 1)
                act.wait_ge(S["dn_ya"], 4 * half + 4)
                act.wait_ge(S["dn_yv"], 4 * half + 4)
            finish(1)
            act.wait_ge(S["f_stored"], 16 * TT)

        @block.vector
        def _(v):
            chain = [0]
            jobs = [0]

            def mark(ins):
                chain[0] += 1
                ins.then_inc(S["v_chain"], 1)
                return chain[0]

            def link(ins):
                v.wait_ge(S["v_chain"], mark(ins))

            def refine(rows, col, n, scale, dst):
                jobs[0] += 1
                m, y, ya, yb = (b[0:rows, col:col + n] for b in (MM, YY, YA, YB))
                v.wait_ge(S["rs_y"], jobs[0])
                mark(v.tensor_scalar(m, SS[0:rows, col:col + n], scale, EPS, ALU.mult, ALU.add))
                link(v.scalar_tensor_tensor(out=ya, in0=y, scalar=-0.5, in1=y, op0=ALU.mult, op1=ALU.mult))
                link(v.tensor_tensor(yb, ya, m, ALU.mult))
                link(v.scalar_tensor_tensor(out=dst, in0=yb, scalar=1.5, in1=y, op0=ALU.add, op1=ALU.mult))

            def ready(n):
                name, value = TM[n]
                v.wait_ge(S[name], value)

            def normalise(use, t, src, rstd, rows=P):
                n = use + t
                if t >= 2:
                    v.wait_ge(S["nt_mm"], n - 1)
                v.scalar_tensor_tensor(out=XN[use][0:rows, n % 2, :], in0=src, scalar=rstd, in1=GB[use][0:rows, :],
                                       op0=ALU.mult, op1=ALU.mult).then_inc(S["nt_xn"], 1)

            def lo_of_tile(n, dst, first, rows=P):
                v.wait_ge(S["nt_hi"], n - N_A1 + 1)
                v.tensor_tensor(dst[:, 1, :, first:first + rows], pair_tiles(n % 2)[:, :, 0:rows],
                                plain(dst[:, 0, :, first:first + rows]), ALU.subtract).then_inc(S["nt_free"], 1)

            v.memset(VROW[:, :, :], 0.0).then_inc(S["vec_zero"], 1)
            v.memset(WBD[:, :, :], 0.0).then_inc(S["cw_zero"], 1)
            v.wait_ge(S["consts"], 16 * N_CONSTS)
            for t in range(KTILES):
                rows = tokens_of(t)[1]
                refine(rows, t, 1, 1.0 / D, RX[0:rows, t:t + 1])
                normalise(N_U, t, XIN[N_U][0:rows, t % 2, :], RX[0:rows, t:t + 1], rows)
            v.wait_ge(S["rope_in"], 48)
            for q in range(2):
                gain = GAINS[:, q, :].unsqueeze(1).broadcast_to([P, KTILES, DH])
                swapped = GAINS[:, q, :].rearrange("p (f e) -> p f e", e=2)[:, :, ::-1].unsqueeze(1)\
                    .broadcast_to([P, KTILES, DH // 2, 2])
                v.tensor_tensor(ROPE[:, 2 * q, :, :], ROPER[:, 0, :, :], gain, ALU.mult)
                mark(v.tensor_tensor(ROPE[:, 2 * q + 1, :, :].rearrange("p t (f e) -> p t f e", e=2),
                                     ROPER[:, 1, :, :].rearrange("p t (f e) -> p t f e", e=2), swapped, ALU.mult))
            v.wait_ge(S["vec_t"], 1)
            v.tensor_copy(VEC[:, :, :], PB[:, 7, 0:3 * VROWS].rearrange("p (i m) -> p i m", i=3)).then_inc(S["vec_done"], 1)

            v.wait_ge(S["nt_free"], KTILES)

            def fold_lo(j):
                k, h = divmod(j, 2)
                n = FOLD + 1 - 2 * h
                v.wait_ge(S["fold_hi"], j + 1)
                v.tensor_tensor(AF[:, 1, k, FOLDS * h:FOLDS * h + n], FSUM[:, h, 0:n],
                                plain(AF[:, 0, k, FOLDS * h:FOLDS * h + n]), ALU.subtract).then_inc(S["fold_done"], 1)

            for j in range(2 * KT):
                k, h = divmod(j, 2)
                if j >= 2:
                    v.wait_ge(S["fold_done"], j - 1)
                if h == 0:
                    link(v.tensor_copy(FSUM[:, 0, 0:FOLD + 1:FOLD], UT[:, k, 0:FOLD + 1:FOLD]))
                v.tensor_tensor(FSUM[:, h, 1 - h:FOLD - h], UT[:, k, 1:FOLD], UT[:, k, POS - 1:FOLD:-1],
                                ALU.subtract if h else ALU.add).then_inc(S["fold_sum"], 1)
                if j:
                    fold_lo(j - 1)
            fold_lo(2 * KT - 1)
            v.wait_ge(S["fold_done"], 2 * KT)
            v.memset(plain(FC[:, :, :, NF - 1, :]), 0.0).then_inc(S["fpad"], 1)
            for i in range(2):
                v.wait_ge(S["cw_hi"], i + 1)
                v.tensor_tensor(CW[:, 1, i, :, :], PB[:, i, :].rearrange("p (j n) -> p j n", j=4),
                                plain(CW[:, 0, i, :, :]), ALU.subtract).then_inc(S["cw_done"], 1)
            v.wait_ge(S["tail_hi"], 1)
            v.tensor_tensor(TAIL[:, 1, :, :], TAILR[:, :, :], plain(TAIL[:, 0, :, :]), ALU.subtract).then_inc(S["tail_done"], 1)
            v.wait_ge(S["fpad"], 1)
            for u in range(2 * NF):
                h, _, rows = folded(u)
                v.wait_ge(S["tm_hi"], u + 1)
                v.tensor_tensor(FC[0:rows, 1, h, u % NF, :], PB[0:rows, tm_bank(T_FIN + u), :],
                                plain(FC[0:rows, 0, h, u % NF, :]), ALU.subtract).then_inc(S["tm_free"], 1)
            for h in range(2):
                for m in range(8):
                    n = T_DFT + 16 * h + m
                    v.wait_ge(S["tm_hi"], 2 * NF + 8 * h + m + 1)
                    v.tensor_tensor(DE[:, 1, m // 4, m % 4, :], PB[:, tm_bank(n), 0:HALF],
                                    plain(DE[:, 0, m // 4, m % 4, :]), ALU.subtract).then_inc(S["tm_free"], 1)
                skip = META - 1 if h == 0 else 0
                drop = 0 if h == 0 else 1
                for j in range(4):
                    n = T_DFT + 16 * h + 8 + 2 * j
                    ready(n + 1)
                    v.wait_ge(S["ch_a"], 4 * h + j + 1)
                    k0 = 1 + HALF * h
                    v.tensor_tensor(FT1[:, j, k0 + skip - META:k0 + HALF - META], CHA[:, j % 2, skip:HALF],
                                    PB[:, tm_bank(n + 1), skip:HALF], ALU.subtract).then_inc(S["tm_free"], 1)
                    last = POS - k0 - META
                    v.tensor_tensor(FT1[:, j, last:last - (HALF - drop):-1], CHA[:, j % 2, 0:HALF - drop],
                                    PB[:, tm_bank(n + 1), 0:HALF - drop], ALU.add).then_inc(S["tm_free"], 1)
            for t in range(KTILES + 1):
                if t < KTILES:
                    rows = tokens_of(t)[1]
                    n = N_A1 + t
                    v.wait_ge(S[f"nt_in{n % 2}"], 16 * (5 - n % 2 + t // 2 + 1))
                    normalise(N_A1, t, XIN[N_A1][0:rows, n % 2, :], RX[0:rows, t:t + 1], rows)
                if t:
                    lo_of_tile(N_A1 + t - 1, A1, *tokens_of(t - 1))

            for f in range(4):
                e = GE[:, f % 2, :]
                v.wait_ge(S["gate_sig"], f + 1)
                v.tensor_tensor(e, pair(f), e, ALU.mult).then_inc(S["fm_free"], 1)
                v.wait_ge(S["fm_free"], f + 1)
                v.tensor_tensor(FT1[:, f, :], FT1[:, f, :], e, ALU.mult).then_inc(S["gate_out"], 1)

            v.wait_ge(S["gate_stored"], 64)
            v.memset(plain(VV[:, TT, :, :]), 0.0).then_inc(S["vv_set"], 1)
            v.memset(plain(VV[:, 0:TT, :, DH:2 * DH]), 1.0).then_inc(S["vv_set"], 1)
            v.wait_ge(S["vv_set"], 1)
            v.memset(plain(VV[0:META, TT, :, DH:2 * DH]), 1.0).then_inc(S["vv_set"], 1)

            def rotate(n, m, q, t, rows, nh):
                w, col = nh * DH, 8 * (m % 2)
                heads = lambda b: b.rearrange("p (g d) -> p g d", d=DH)
                v.wait_ge(S["pr_sq"], m + 1)
                v.reduce_sum(SS[0:rows, col:col + nh], heads(SQ[0:rows, m % 2, 0:w]), AX).then_inc(S["rs_ss"], 1)
                return w, col, heads

            def rotate_rest(n, m, q, t, rows, nh):
                w, col = nh * DH, 8 * (m % 2)
                heads = lambda b: b.rearrange("p (g d) -> p g d", d=DH)
                pairs = lambda b: b.rearrange("p (g f e) -> p g f e", f=DH // 2, e=2)
                refine(rows, col, nh, 1.0 / DH, RSTD[0:rows, col:col + nh])
                v.tensor_tensor(heads(YN[0:rows, 0:w]), heads(PB[0:rows, tm_bank(n), 0:w]),
                                RSTD[0:rows, col:col + nh].unsqueeze(2).broadcast_to([rows, nh, DH]),
                                ALU.mult).then_inc(S["tm_free"], 1)
                v.wait_ge(S["tm_free"], n + 1)
                mark(v.tensor_tensor(heads(YC[0:rows, 0:w]), heads(YN[0:rows, 0:w]),
                                     ROPE[0:rows, 2 * q, t, :].unsqueeze(1).broadcast_to([rows, nh, DH]), ALU.mult))
                link(v.tensor_tensor(pairs(YS[0:rows, 0:w]), pairs(YN[0:rows, 0:w])[:, :, :, ::-1],
                                     ROPE[0:rows, 2 * q + 1, t, :].rearrange("p (f e) -> p f e", e=2).unsqueeze(1)
                                     .broadcast_to([rows, nh, DH // 2, 2]), ALU.mult))
                if m >= 2:
                    v.wait_ge(S["pr_t"], m - 1)
                v.tensor_tensor(RQ[0:rows, m % 2, 0:w], YC[0:rows, 0:w], YS[0:rows, 0:w], ALU.add).then_inc(S["pr_rope"], 1)

            for u in range(KTILES + 1):
                if u < KTILES:
                    rows = tokens_of(u)[1]
                    rotate(T_KV + u, u, 1, u, rows, KV_HEADS)
                    v.wait_ge(S["kv_vhi"], u + 1)
                    mark(v.tensor_tensor(VV[0:rows, u, :, 2 * DH:3 * DH],
                                         PB[0:rows, tm_bank(T_KV + u), P:2 * P].rearrange("p (g d) -> p g d", g=KV_HEADS),
                                         plain(VV[0:rows, u, :, 0:DH]), ALU.subtract))
                    rotate_rest(T_KV + u, u, 1, u, rows, KV_HEADS)
                if u:
                    first, rows = tokens_of(u - 1)
                    v.wait_ge(S["kv_khh"], 2 * u)
                    for x in range(2):
                        v.tensor_tensor(KLL[DH * x:DH * x + DH, :, first:first + rows],
                                        pair_tiles((u - 1) % 2)[0:DH, 0:KV_HEADS, 0:rows],
                                        plain(KHH[0:DH, :, first:first + rows]), ALU.subtract).then_inc(S["kv_kll"], 1)
            v.wait_ge(S["kv_kll"], 2 * KTILES)
            for b in (KHH, KLL):
                v.tensor_copy(b[:, :, POS:KEYS], plain(b[:, :, 0:KEYS - POS])).then_inc(S["kdup"], 1)
            for u in range(TT + 1):
                if u < TT:
                    rotate(T_Q + u, KTILES + u, 0, u, P, HEADS)
                    rotate_rest(T_Q + u, KTILES + u, 0, u, P, HEADS)
                if u:
                    cols = slice(P * (u - 1), P * u)
                    v.wait_ge(S["pr_hi"], u)
                    v.tensor_tensor(QS[DH:P, :, cols], pair_tiles((u - 1) % 2)[0:DH, :, :], plain(QS[0:DH, :, cols]),
                                    ALU.subtract).then_inc(S["pr_done"], 1)
            for f in range(4):
                e = GE2[:, f % 2, :]
                v.wait_ge(S["gate_sig"], 4 + f + 1)
                v.tensor_tensor(e, pair(f), e, ALU.mult).then_inc(S["fm_free"], 1)
                v.wait_ge(S["fm_free"], 4 + f + 1)
                v.tensor_scalar(e, e, 1.0, None, ALU.mult).then_inc(S["gate_out"], 1)

            def probs_lo(i):
                t = i % 4
                for g in range(3):
                    rows = P if g < 2 else META
                    kts = slice(4 * g, min(4 * g + 4, KTILES))
                    v.wait_ge(S["pt_hi"], 3 * i + g + 1)
                    v.tensor_tensor(PT[0:rows, 1, kts, P * t:P * t + P],
                                    PB[0:rows, 3 + g, 0:P * (4 if g < 2 else 1)].rearrange("p (k n) -> p k n", n=P),
                                    plain(PT[0:rows, 0, kts, P * t:P * t + P]), ALU.subtract).then_inc(S["pt_lo"], 1)

            def attended(p):
                row, col, buf = pair_place(p)
                b = p // 2
                v.wait_ge(S["o_inv"], p + 1)
                if p >= 4:
                    v.wait_ge(S["o_lo"], p - 3)
                link(v.tensor_tensor(OT[row, buf, :], PB[0:DH, 6 + p % 2, 0:PAIR],
                                     RC[:, PAIR * (p % 2):PAIR * (p % 2) + PAIR], ALU.mult))
                v.wait_ge(S[f"ag_in{b % 2}"], 16 * (b // 2 + 1))
                v.tensor_tensor(OT[row, buf, :], OT[row, buf, :], AG[row, b % 2, PAIR * (p % 2):PAIR * (p % 2) + PAIR],
                                ALU.mult).then_inc(S["o_out"], 1)

            def attended_lo(p):
                row, col, buf = pair_place(p)
                v.wait_ge(S["o_hi"], p + 1)
                v.tensor_tensor(MIXA[row, 1, p // 8, col], OT[row, buf, :], plain(MIXA[row, 0, p // 8, col]),
                                ALU.subtract).then_inc(S["o_lo"], 1)

            v.wait_ge(S["gate_stored"], 128)
            v.wait_ge(S["w_used"], C_OUT)
            v.memset(plain(PT[:, :, KTILES - 1, :]), 0.0).then_inc(S["pt_zero"], 1)
            v.wait_ge(S["pt_zero"], 1)
            for i in range(HEADS * TT):
                v.wait_ge(S["sc_mm"], i + 1)
                link(v.reduce_max(MX[:, i % 2:i % 2 + 1], PB[:, 0:3, 0:KPART], mybir.AxisListType.XY))
                v.tensor_scalar(NB[:, i % 2:i % 2 + 1], MX[:, i % 2:i % 2 + 1], -DH ** -0.5, None,
                                ALU.mult).then_inc(S["sc_max"], 1)
                if i:
                    probs_lo(i - 1)
                if i >= 6 and i % 2 == 0:
                    attended((i - 6) // 2)
                if i >= 9 and i % 2:
                    attended_lo((i - 9) // 2)
            probs_lo(HEADS * TT - 1)
            attended(PAIRS - 3)
            attended(PAIRS - 2)
            attended_lo(PAIRS - 4)
            attended_lo(PAIRS - 3)
            attended(PAIRS - 1)
            attended_lo(PAIRS - 2)
            attended_lo(PAIRS - 1)
            for f in range(4):
                v.wait_ge(S["mf_hi"], f + 1)
                v.tensor_tensor(MIXF[:, 1, f, :], MFR[:, f, :], plain(MIXF[:, 0, f, :]), ALU.subtract).then_inc(S["mf_done"], 1)
            v.wait_ge(S["mf_done"], 4)
            for m in range(2 * TT):
                c, u = divmod(m, TT)
                ready(T_OUT + m)
                v.wait_ge(S[f"op_in{m % 2}"], 16 * (m // 2 + 1))
                v.tensor_tensor(H[:, u, FW * c:FW * c + FW], PB[:, tm_bank(T_OUT + m), :], XR[:, m % 2, :],
                                ALU.add).then_inc(S["tm_free"], 1)
            v.wait_ge(S["gains_in"], 32)
            v.wait_ge(S["tm_free"], T_V2)
            for s in range(TT + 2):
                if s < TT:
                    refine(P, s, 1, 1.0 / D, RSTD[:, s:s + 1])
                    v.scalar_tensor_tensor(out=H[:, s, :], in0=H[:, s, :], scalar=RSTD[:, s:s + 1], in1=GF[:, :],
                                           op0=ALU.mult, op1=ALU.mult).then_inc(S["x1_out"], 1)
                if 1 <= s <= TT:
                    t = s - 1
                    refine(P, 8 + t, 1, 1.0 / D, RX[:, t:t + 1])
                    normalise(N_A2, t, H[:, t, :], RX[:, t:t + 1])
                if s >= 2:
                    lo_of_tile(N_A2 + s - 2, A2, P * (s - 2))
            v.wait_ge(S["x1_stored"], 16 * TT)
            for u in range(TT):
                n = T_V2 + u
                v.wait_ge(S["tm_hi"], 2 * NF + 16 + u + 1)
                v.tensor_tensor(V2[:, 1, u, :], PB[:, tm_bank(n), :], plain(V2[:, 0, u, :]), ALU.subtract)\
                 .then_inc(S["tm_free"], 1)

            def stack_part_lo(h, part):
                r = DH * (h % 2)
                v.wait_ge(S["st_a"], 3 * h + part + 3)
                if part == 0:
                    v.tensor_tensor(QS2[h % 2][DH - r:P - r, :], QT[r:r + DH, h // 2, :], plain(QS2[h % 2][r:r + DH, :]),
                                    ALU.subtract).then_inc(S["st_v"], 1)
                else:
                    q = (r, DH - r)[part - 1]
                    v.tensor_tensor(KLL2[h % 2][q:q + DH, :], KT2[r:r + DH, h // 2, :], plain(KHH2[h % 2][r:r + DH, :]),
                                    ALU.subtract).then_inc(S["st_v"], 1)

            def exponent(i):
                n = P * (i % TT + 1)
                z, l, s = pair(i % 2)[:, 0:n], ZL[:, i % 2, 0:n], ZS[:, i % 2, 0:n]
                v.wait_ge(S["z_l"], i + 1)
                if i >= 2:
                    v.wait_ge(S["wt_mm"], turned(i - 1))
                link(v.scalar_tensor_tensor(out=s, in0=z, scalar=0.0, in1=l, op0=ALU.max, op1=ALU.add))
                link(v.tensor_tensor_scan(ZL[:, i % 2, n - 1::-1], ONES[:, 0:n], ZS[:, i % 2, n - 1::-1], 0.0,
                                          ALU.mult, ALU.add))
                v.tensor_tensor(s, z, l, ALU.subtract).then_inc(S["z_e"], 1)

            def weights_lo(i):
                t, c = i % TT, i % 4
                for g in range(t // 4 + 1):
                    n = turned(i) + g
                    w = min(4, t + 1 - 4 * g)
                    v.wait_ge(S["wt_hi"], n + 1)
                    v.tensor_tensor(WT[:, 1, 4 * g:4 * g + w, P * c:P * c + P],
                                    PB[:, 4 + n % 2, 0:P * w].rearrange("p (k n) -> p k n", n=P),
                                    plain(WT[:, 0, 4 * g:4 * g + w, P * c:P * c + P]), ALU.subtract).then_inc(S["wt_lo"], 1)

            def attended2(p):
                row, col, _ = pair_place(p)
                v.wait_ge(S["av2_mm"], p + 1)
                v.tensor_copy(AT[row, p // 8, col], PB[0:DH, 6 + p % 2, 0:PAIR])\
                 .then_inc(S["at_out"], 1)

            v.wait_ge(S["w_used"], C_CONV)
            v.memset(ONES[:, :], 1.0).then_inc(S["ones_set"], 1)
            v.wait_ge(S["ones_set"], 1)
            for part in range(3):
                stack_part_lo(0, part)
            for i in range(HEADS * TT + 2):
                if i < HEADS * TT:
                    exponent(i)
                if i >= 2:
                    weights_lo(i - 2)
                if i >= 6 and i % 2 == 0:
                    attended2((i - 6) // 2)
                if 1 <= i % TT <= 3 and i < (HEADS - 1) * TT:
                    stack_part_lo(i // TT + 1, i % TT - 1)
            attended2(PAIRS - 2)
            attended2(PAIRS - 1)

            for f in range(4):
                v.wait_ge(S["at_hi"], f + 1)
                v.tensor_tensor(ATS[:, 1, f, :], AT[:, f, :], plain(ATS[:, 0, f, :]), ALU.subtract).then_inc(S["at_done"], 1)
            v.wait_ge(S["gains_in"], 48)
            for t in range(TT + 1):
                if t < TT:
                    n = N_A3 + t
                    v.wait_ge(S[f"nt_in{n % 2}"], 16 * (9 + t // 2 + 1))
                    normalise(N_A3, t, XIN[N_A3][:, n % 2, :], RX[:, t:t + 1])
                if t:
                    lo_of_tile(N_A3 + t - 1, A2, P * (t - 1))

            v.wait_ge(S["at_done"], 4)
            v.memset(PROD[:, 0:2], 0.0).then_inc(S["cv_pad"], 1)
            v.wait_ge(S["cv_pad"], 1)
            nf = 2 * FT
            for f in range(5):
                if f < 4:
                    u = U_CONV + 3 * f
                    v.wait_ge(S["w_used"], C_CONV + 3 * f + 2)
                    v.wait_ge(S["cv_cc"], f + 1)
                    v.tensor_tensor(PROD[:, 2:N_TOK + 2], pair((u + 1) % 4), CCB[:, :], ALU.mult).then_inc(S["fm_free"], 1)
                    v.wait_ge(S["fm_free"], u + 1)
                    v.tensor_scalar(CY[:, :], PROD[:, 2:N_TOK + 2], VEC[:, 2, nf + f:nf + f + 1], None,
                                    ALU.mult).then_inc(S["fm_free"], 1)
                    v.wait_ge(S["fm_free"], u + 2)
                    for i in (1, 0):
                        link(v.scalar_tensor_tensor(out=CY[:, :], in0=PROD[:, i:N_TOK + i], scalar=VEC[:, i, nf + f:nf + f + 1],
                                                    in1=CY[:, :], op0=ALU.mult, op1=ALU.add))
                if f:
                    v.wait_ge(S["cv_hi"], f)
                    v.tensor_tensor(CTS[:, 1, f - 1, :], CO[:, :], plain(CTS[:, 0, f - 1, :]), ALU.subtract).then_inc(S["cv_done"], 1)
                    v.wait_ge(S["cv_done"], f)
                if f < 4:
                    v.wait_ge(S["w_used"], C_CONV + 3 * f + 3)
                    v.tensor_tensor(CO[:, :], pair((u + 2) % 4), CY[:, :], ALU.mult).then_inc(S["fm_free"], 1)
                    v.wait_ge(S["fm_free"], u + 3)

            for f in range(KT):
                u = U_MRG + 4 * f
                v.wait_ge(S["fm_free"], u + 2)
                v.wait_ge(S["w_used"], C_MRG + 3 * f + 3)
                for g in range(2):
                    v.tensor_tensor(MGE[:, g, :], pair((u + 2 + g) % 4), MGE[:, g, :], ALU.mult).then_inc(S["fm_free"], 1)
                v.wait_ge(S["fm_free"], u + 4)
                if f >= 2:
                    v.wait_ge(S[f"mg_st{f % 2}"], 16 * (f // 2))
                v.tensor_tensor(MGO[:, f % 2, :], MGE[:, 0, :], MGE[:, 1, :], ALU.add).then_inc(S["mg_out"], 1)
            for f in range(KT):
                v.wait_ge(S["mr_hi"], f + 1)
                v.tensor_tensor(MR[:, 1, f, :], MRR[:, f % 2, :], plain(MR[:, 0, f, :]), ALU.subtract).then_inc(S["mr_done"], 1)

            v.wait_ge(S["gains2_in"], 32)
            for s in range(TT + 2):
                if s < TT:
                    refine(P, s, 1, 1.0 / D, RSTD[:, s:s + 1])
                    link(v.scalar_tensor_tensor(out=Y[:, s, :], in0=Y[:, s, :], scalar=RSTD[:, s:s + 1], in1=GP[:, :],
                                                op0=ALU.mult, op1=ALU.mult))
                    v.wait_ge(S[f"xr_in{s % 2}"], 16 * (s // 2 + 1))
                    v.tensor_tensor(Y[:, s, :], Y[:, s, :], XRR[:, s % 2, :], ALU.add).then_inc(S["x2_out"], 1)
                if 1 <= s <= TT:
                    t = s - 1
                    refine(P, 8 + t, 1, 1.0 / D, RX[:, t:t + 1])
                    normalise(N_A4, t, Y[:, t, :], RX[:, t:t + 1])
                if s >= 2:
                    lo_of_tile(N_A4 + s - 2, A4, P * (s - 2))

            v.sem_inc(S["up_f"], 1)
            with v.Fori(0, FT // 2) as i:
                for s in range(4):
                    q, g = divmod(s, 2)
                    up = pair(s)
                    w1, w0 = (VEC[:, x, bass.ds(i * 2 + (q + FT * g), 1)] for x in (1, 0))
                    v.wait_ge(S["up_c"], i * 4 + (s + 1))
                    v.scalar_tensor_tensor(out=UB[:, g, 1:N_TOK], in0=up[:, 0:N_TOK - 1], scalar=w1,
                                           in1=UB[:, g, 1:N_TOK], op0=ALU.mult, op1=ALU.add).then_inc(S["up_s"], 1)
                    v.wait_ge(S["up_s"], i * 4 + (s + 1))
                    v.scalar_tensor_tensor(out=UB[:, g, 2:N_TOK], in0=up[:, 0:N_TOK - 2], scalar=w0,
                                           in1=UB[:, g, 2:N_TOK], op0=ALU.mult, op1=ALU.add).then_inc(S["fm_free"], 1)
                    if g:
                        v.wait_ge(S["up_g"], i * 2 + (q + 1))
                        v.tensor_tensor(FFT[:, bass.ds(i * 2 + q, 1), :].rearrange("p a n -> p (a n)"), UB[:, 0, :],
                                        UB[:, 1, :], ALU.mult).then_inc(S["up_f"], 1)

            def mid_lo(half, j, s):
                v.wait_ge(S["dn_hi"], j + (FT * half + 1))
                src = FFT[:, j, FW * half:FW * half + FW] if isinstance(j, int) else \
                    FFT[:, bass.ds(j, 1), FW * half:FW * half + FW].rearrange("p a n -> p (a n)")
                v.tensor_tensor(FS[:, s, 1, :], src, plain(FS[:, s, 0, :]), ALU.subtract).then_inc(S["dn_lo"], 1)

            def finish(half):
                for s in range(4):
                    m = 4 * half + s
                    refine(P, s, 1, 1.0 / D, RSTD[:, s:s + 1])
                    link(v.scalar_tensor_tensor(out=Y2[:, s, :], in0=Y2[:, s, :], scalar=RSTD[:, s:s + 1],
                                                in1=GL[:, :], op0=ALU.mult, op1=ALU.mult))
                    v.wait_ge(S[f"xf_in{m % 2}"], 16 * (m // 2 + 1))
                    v.tensor_tensor(Y2[:, s, :], Y2[:, s, :], XF[:, m % 2, :], ALU.add).then_inc(S["f_out"], 1)

            v.wait_ge(S["gains3_in"], 16)
            v.wait_ge(S["up_f"], FT + 1)
            for half in range(2):
                mid_lo(half, 0, 0)
                mid_lo(half, 1, 1)
                if half:
                    finish(0)
                with v.Fori(1, FT // 2) as i:
                    for s in range(2):
                        mid_lo(half, i * 2 + s, s)
                v.wait_ge(S["w_used"], C_DOWN + FT * (half + 1))
                if half:
                    v.wait_ge(S["f_stored"], 64)
                for t in range(4):
                    v.tensor_copy(Y2[:, t, FW:D], PB[:, 2 * t + 1, :]).then_inc(S["dn_yv"], 1)
            finish(1)


N_CONSTS = 2


def weight_chunks(a, const):
    def token_major(w, first, n):
        per = WCH // n
        v = w.rearrange("(k p) n -> p k n", p=P)
        return [(WCH, [(0, v[:, per * j:per * j + per, first:first + n])]) for j in range(KT // per)]

    def feature_tile(w, first):
        return (WCH, [(0, w.rearrange("(k p) n -> p k n", p=P)[:, :, first:first + P])])

    w1, w2 = a["w_in"][0], a["w_in_2"][0]
    out = token_major(w1, 0, FW)
    out += [(SLOT, [(0, const["dft_main"][i])]) for i in range(4)]
    out += [feature_tile(w1, FW + P * f) for f in range(4)]
    out += token_major(w1, 1536, 256) + token_major(w1, 1024, FW)
    out += [feature_tile(w1, GATE1 + P * f) for f in range(4)]
    out += token_major(a["w_out"][0], 0, FW) + token_major(a["w_out"][0], FW, FW)
    out += token_major(w2, 1024, FW)
    out += [feature_tile(w2, P * f) for f in range(8)]
    for f in range(4):
        out += [feature_tile(w2, c + P * f) for c in (2048, 2560, 1536)]
    branches = [a[k][0].rearrange("(k p) n -> p k n", p=P) for k in ("w_att_branch_2", "w_conv_branch_2")]
    for f in range(KT):
        out += [feature_tile(w2, 3072 + P * f), feature_tile(w2, 4096 + P * f)]
        out.append((WCH, [(FW * i, b[:, :, P * f:P * f + P]) for i, b in enumerate(branches)]))
    out += token_major(a["w_out_2"][0], 0, FW) + token_major(a["w_out_2"][0], FW, FW)
    assert len(out) == C_UP
    return out


def constants():
    ident = np.eye(P, dtype=np.float32)
    q, k = np.arange(P)[:, None], np.arange(P)[None, :]
    causal = np.where(k < q, 0.0, NEG).astype(np.float32)
    grid, axis = 64, 16
    j = np.arange(N_TOK)
    row, col = j // grid - (N_TOK // grid) // 2, j % grid - grid // 2
    freqs = 1.0 / (10000.0 ** (np.arange(axis) * 2.0 / (2 * axis)))
    ang = np.concatenate([row[:, None] * freqs, col[:, None] * freqs], axis=-1)
    cos, sin = np.repeat(np.cos(ang), 2, axis=1), np.repeat(np.sin(ang), 2, axis=1)
    sin[:, 0::2] *= -1.0
    rope = np.zeros((P, 2, KTILES, DH), np.float32)
    rope[:, 0, TT] = 1.0
    for t in range(TT):
        rope[:, 0, t], rope[:, 1, t] = cos[P * t:P * t + P], sin[P * t:P * t + P]
    c = np.arange(DH)
    ang = 2 * np.pi * (np.outer(c, c) % DH) / DH
    channel = np.zeros((P, 2, P), np.float32)
    for g in range(2):
        s = slice(DH * g, DH * g + DH)
        channel[s, 0, s], channel[s, 1, s] = np.cos(ang), np.sin(ang)
    main = np.zeros((4, P, 4, HALF), np.float64)
    tail = np.zeros((P, 4, HALF), np.float64)
    for h in range(2):
        freq = 1 + HALF * h + np.arange(HALF)
        for kind in range(2):
            n = np.arange(FOLD + 1) if kind == 0 else np.arange(1, FOLD)
            ang = 2 * np.pi * (np.outer(n, freq) % POS) / POS
            table = (np.sin(ang) if kind else np.cos(ang)) / np.sqrt(POS * DH)
            main[2 * h + kind] = table[:4 * P].reshape(4, P, HALF).transpose(1, 0, 2)
            tail[:len(n) - 4 * P, 2 * h + kind] = table[4 * P:]
    return {"ident": ident, "causal": causal, "rope": rope, "channel": channel,
            "dft_main": main.reshape(4, P, SLOT).astype(np.float32), "dft_tail": tail.astype(np.float32)}


_INS = ["x", "meta_tokens", "norm_g", "w_in", "w_fmix", "b_fmix", "q_norm_g", "k_norm_g", "w_out", "final_g",
        "norm_mix_pre_2", "w_in_2", "conv_mix_w_2", "w_att_branch_2", "w_conv_branch_2", "w_out_2",
        "norm_mix_post_2", "norm_ffn_pre_2", "w_up_2", "conv_ffn_w_2", "w_down_2", "norm_ffn_post_2"]
_SCRATCH = {"mixed_f": (512, N_TOK), "a_gate": (512, N_TOK), "x1": (N_TOK, D), "merged": (D, N_TOK), "x2": (N_TOK, D)}


def kernel(**inputs):
    import concourse.bacc as bacc
    from concourse.bass_utils import run_bass_kernel_spmd

    nc = bacc.Bacc("TRN2", target_bir_lowering=False, num_devices=1)
    arrays, a, const = {}, {}, {}
    for name in _INS:
        array = np.ascontiguousarray(inputs[name])
        arrays[f"in_{name}"] = array
        a[name] = nc.dram_tensor(f"in_{name}", array.shape, mybir.dt.from_np(array.dtype), kind="ExternalInput").ap()
    for name, array in constants().items():
        arrays[f"const_{name}"] = array
        const[name] = nc.dram_tensor(f"const_{name}", array.shape, F32, kind="ExternalInput").ap()
    scratch = {name: nc.dram_tensor(f"scratch_{name}", shape, F32, kind="Internal").ap()
               for name, shape in _SCRATCH.items()}
    out = nc.dram_tensor("out_0", (1, N_TOK, D), F32, kind="ExternalOutput").ap()
    two_block_kernel(nc, a, const, scratch, out)
    r = run_bass_kernel_spmd(nc, [arrays], core_ids=[0])
    return r.results[0]["out_0"]
```

```python
from contextlib import ExitStack

import concourse.bass as bass
import numpy as np
from concourse import mybir

F32 = mybir.dt.float32
F32R = mybir.dt.float32r
ALU = mybir.AluOpType
ACT = mybir.ActivationFunctionType
AX = mybir.AxisListType.X

P = 128
D = 1024
KT = D // P
N_TOK = 1024
TT = N_TOK // P
META = 16
POS = N_TOK + META
EPS = 1e-6
DH = 64
HEADS = 8
KV_HEADS = 2
GROUP = HEADS // KV_HEADS
FW = 512
FOLD = POS // 2
FOLDS = 522
NF = 5
REST = {0: FOLD + 1 - 4 * P, 1: FOLD - 1 - 4 * P}
HALF = FOLD // 2
SLOT = 4 * HALF
WCH = 1024
KEYS = 1044
KPART = KEYS // 3
KTILES = 9
FF = 2816
FT = FF // P
PAIR = 2 * P
PAIRS = HEADS * TT // 2
NEG = -2.0 ** 100
LAG = 3
MERGED_ORDER = (2, 3, 4, 5, 0, 1, 6, 7)
VROWS = FT * 2 + 4 + 4
EXP_AND_LN = 6
A_GATE_PAIRS = (2, 0, 1, 3)
GATE1 = 1792

C_FIN = 0
C_DFT = C_FIN + 4
C_FGATE = C_DFT + 4
C_KV = C_FGATE + 4
C_Q = C_KV + 2
C_AGATE = C_Q + 4
C_OUT = C_AGATE + 4
C_V2 = C_OUT + 8
C_QK2 = C_V2 + 4
C_CONV = C_QK2 + 8
C_MRG = C_CONV + 12
C_OUT2 = C_MRG + 24
C_UP = C_OUT2 + 8
C_DOWN = C_UP + 2 * FT
C_END = C_DOWN + 2 * FT

T_FIN = 0
T_DFT = T_FIN + 2 * NF
T_KV = T_DFT + 32
T_Q = T_KV + KTILES
T_OUT = T_Q + TT
T_V2 = T_OUT + 2 * TT
T_OUT2 = T_V2 + TT
U_FGATE = 0
U_AGATE = 4
U_QK2 = 8
U_CONV = 16
U_MRG = 28
U_UP = U_MRG + 32

N_U = 0
N_A1 = N_U + KTILES
N_A2 = N_A1 + KTILES
N_A3 = N_A2 + TT
N_A4 = N_A3 + TT


def tm_signals():
    groups = [(2 * NF, C_FIN + 4)]
    for h in range(2):
        groups += [(4, C_DFT + 2 * h + 1), (4, C_DFT + 2 * h + 2), (8, None)]
    groups += [(KTILES, C_KV + 2), (TT, C_Q + 4), (TT, C_OUT + 4), (TT, C_OUT + 8), (TT, C_V2 + 4),
               (TT, C_OUT2 + 4), (TT, C_OUT2 + 8)]
    out, count = [], 0
    for units, used in groups:
        for u in range(units):
            if used is not None and u == units - 1:
                out.append(("w_used", used))
            else:
                count += 1
                out.append(("tm_mm", count))
    return out


SEMS = """
x_in0 x_in1 x_in2 x_in3 x_in4 x_in5 x_in6 x_in7 x_in8
zero_set w_staged0 w_staged1 w_hi w_split w_used tm_mm tm_free fm_free nt_in0 nt_in1 nt_xn nt_mm nt_hi nt_free
v_chain a_chain rs_ss rs_y consts vec_zero vec_in vec_t vec_done rope_in cw_zero cw_in cw_mm cw_hi cw_done
fold_sum fold_hi fold_done fpad tm_hi tail_in tail_hi tail_done ch_a
gate_sig gate_out gate_stored f_gate_last vv_set
pr_sq pr_rope pr_t pr_hi pr_done kv_khh kv_kll kv_vhi kdup
sc_mm sc_max sc_exp pt_mm pt_zero pt_hi pt_lo av_mm ag_in0 ag_in1 o_inv o_out o_hi o_lo
mf_in mf_hi mf_done op_in0 op_in1 gains_in x1_out x1_stored
causal_in st_a st_v z_mm z_l z_e z_w wt_mm wt_hi wt_lo av2_mm at_out ones_set
at_hi at_done cv_pad cv_cc cv_hi cv_done mg_out mg_st0 mg_st1 mr_in0 mr_in1 mr_hi mr_done
gains2_in xr_in0 xr_in1 x2_out x2_stored
dn_mm up_half up_c up_s up_g up_f dn_hi dn_lo dn_ya dn_yv gains3_in xf_in0 xf_in1 f_out f_stored
""".split()


def two_block_kernel(nc, a, const, scratch, out):
    ctx = ExitStack()
    with ctx:
        S = {name: ctx.enter_context(nc.semaphore(name)) for name in SEMS}
        TM = tm_signals()
        base = (nc.sbuf_base + 63) // 64 * 64

        def at(name, shape, first, dt=F32):
            size = int(np.prod(shape[1:]))
            assert first + size <= TOP, (name, first + size, TOP)
            return nc.alloc_sbuf_tensor_at(name, shape, dt, offset=base + 4 * first)

        TOP = (nc.sbuf_top - base) // 4

        WS = at("w_staging", [P, 2, SLOT], 0)
        WR = at("w_ring", [P, 4, 2, SLOT], 2 * SLOT, F32R)
        c0 = 10 * SLOT
        IDENT = at("ident", [P, P], c0)
        VEC = at("vectors", [P, 3, VROWS], c0 + 128)
        SS = at("sumsq", [P, 16], c0 + 288)
        LN = at("ln", [P, 16], c0 + 304)
        YY = at("rsqrt_guess", [P, 16], c0 + 320)
        MM = at("mean", [P, 16], c0 + 336)
        YA = at("newton_a", [P, 16], c0 + 352)
        YB = at("newton_b", [P, 16], c0 + 368)
        RSTD = at("rstd", [P, 16], c0 + 384)
        RX = at("rstd_x", [P, 16], c0 + 400)
        ZERO = at("zero", [P, 8], c0 + 688)
        NB = at("minus_max", [P, 2], c0 + 424)
        IDR = at("ident_r", [P, P], c0 + 432, F32R)
        CAUSAL = at("causal", [P, P], c0 + 560, F32R)
        c1 = c0 + 696
        ROPE = at("rope", [P, 4, KTILES, DH], c1)
        A0 = c1 + 4 * KTILES * DH
        R1 = A0
        R2 = A0 + 17408
        assert TOP - R2 >= 22400 - 64, TOP - R2

        XIN, XN, GB = {}, {}, {}
        for block_uses, first in (((N_U, N_A1), R2 + 10240), ((N_A2, N_A4), R2 + 8192)):
            xin = at(f"xin{block_uses[0]}", [P, 2, D], first)
            xn = at(f"xn{block_uses[0]}", [P, 2, D], first + 2048)
            gain = at(f"gain{block_uses[0]}", [P, D], first + 4096)
            for use in block_uses:
                XIN[use], XN[use], GB[use] = xin, xn, gain

        XALL = at("x_tiles", [P, KTILES, D], R1)
        JUNK0 = at("junk0", [P, D], R1 + KTILES * D)
        UT = at("u_t", [P, KT, POS], R2)
        FSUM = at("fold_sum", [P, 2, FOLDS], R2 + 15360)
        AF = at("u_folded", [P, 2, KT, 2 * FOLDS - 2], R1, F32R)
        FC = at("f_in", [P, 2, 2, NF, FW], R2, F32R)
        DE = at("dft", [P, 2, 2, 4, HALF], R1, F32R)
        TAILR = at("dft_tail_raw", [P, 4, HALF], R2 + 10240)
        TAIL = at("dft_tail", [P, 2, 4, HALF], R2 + 11280, F32R)
        CWRAW = at("channel_raw", [P, 2, P], R2 + 19456)
        WBD = at("w_fmix_blocks", [P, 4, P], R2 + 19712)
        CW = at("channel_w", [P, 2, 2, 4, P], R2 + 20224, F32R)
        ROPER = at("rope_raw", [P, 2, KTILES, DH], R2 + 16416)
        GAINS = at("qk_gains", [P, 2, DH], R2 + 17568)
        VROW = at("vector_rows", [VROWS, 3, P], R2 + 17696)
        CHA = at("channel_a", [P, 2, HALF], R1 + 4160)
        FT1 = at("f_out", [P, 4, N_TOK], R2 + 15360)
        A1 = at("u", [P, 2, KT, POS], R1, F32R)
        GE = at("gate_e", [P, 2, N_TOK], R2 + 10240)
        QS = at("q_stack", [P, HEADS, N_TOK], R2, F32R)
        KHH = at("k_hi_hi", [P, KV_HEADS, KEYS], R2 + 8192, F32R)
        KLL = at("k_lo_lo", [P, KV_HEADS, KEYS], R2 + 10280, F32R)
        VV = at("v_hi_ones_lo", [P, KTILES, KV_HEADS, 3 * DH], R2 + 12368, F32R)
        T0 = R2 + 15824
        SQ = at("square", [P, 2, FW], T0)
        YN = at("normed", [P, FW], T0 + 1024)
        YC = at("times_cos", [P, FW], T0 + 1536)
        YS = at("times_sin", [P, FW], T0 + 2048)
        RQ = at("rotated", [P, 2, FW], T0 + 2560)
        GE2 = at("gate_e2", [P, 2, N_TOK], T0 + 3584)
        PR = at("probs", [P, 2, KEYS], T0)
        AG = at("a_gate", [P, 2, FW], T0 + 2088)
        RC = at("row_sum_inv", [DH, FW], T0 + 3112)
        OT = at("attended", [P, 4, PAIR], T0 + 3624)
        PT = at("probs_t", [P, 2, KTILES, 4 * P], R1, F32R)
        MIXA = at("mixed_a", [P, 2, 4, N_TOK], R1 + 9216, F32R)
        MFR = at("mixed_f_raw", [P, 4, N_TOK], R2)
        MIXF = at("mixed_f", [P, 2, 4, N_TOK], R1, F32R)
        H = at("h", [P, TT, D], R2)
        XR = at("x_again", [P, 2, FW], R2 + 13312)
        GF = at("final_gain", [P, D], R2 + 14336)
        JUNK = at("junk", [P, D], R2 + 15360)

        A2 = at("h2", [P, 2, KT, N_TOK], R1, F32R)
        V2 = at("v2", [P, 2, TT, FW], R2, F32R)
        X1N = at("x1_tiles", [P, TT, D], R2 + 8192)
        GB[N_A3] = at("gain_again", [P, D], R2 + 20480)
        QT = at("q2_t", [P, 4, N_TOK], R2 + 8192)
        KT2 = at("k2_t", [P, 4, N_TOK], R2 + 12288)
        AT = at("att_t", [P, 4, N_TOK], R2 + 16384)
        WT = at("stick_w_t", [P, 2, TT, 4 * P], R1, F32R)
        QS2 = [at(f"q2_stack{i}", [P, N_TOK], f, F32R) for i, f in enumerate((R1 + 16384, R1 + 8192))]
        KHH2 = [at(f"k2_hi_hi{i}", [P, N_TOK], f, F32R) for i, f in enumerate((c1, R1 + 9216))]
        KLL2 = [at(f"k2_lo_lo{i}", [P, N_TOK], f, F32R) for i, f in enumerate((c1 + 1024, R1 + 10240))]
        CAUSALR = at("causal_raw", [P, P], c1 + 2048)
        ZL = at("softplus_part", [P, 2, N_TOK], R1 + 11264)
        ZS = at("softplus", [P, 2, N_TOK], R1 + 13312)
        ONES = at("ones", [P, N_TOK], R1 + 15360)
        ATS = at("att_split", [P, 2, 4, N_TOK], R2, F32R)
        CTS = at("conv_split", [P, 2, 4, N_TOK], R2 + 8192, F32R)
        CCB = at("cc", [P, N_TOK], R2 + 16384)
        PROD = at("cc_cx", [P, N_TOK + 2], R2 + 17408)
        CY = at("conv_y", [P, N_TOK], R2 + 18440)
        CO = at("conv_out", [P, N_TOK], R2 + 19464)
        MGE = at("merge_gates", [P, 2, N_TOK], R2 + 16384)
        MGO = [at(f"merged{i}", [P, N_TOK], f)
               for i, f in enumerate((R2 + 18432, R2 + 19456, R1 + 16384, c1, c1 + 1024, R2 + 20480))]
        MRR = at("merged_raw", [P, 2, N_TOK], R1 + 8192)
        MR = at("merged_split", [P, 2, KT, N_TOK], R1, F32R)
        Y = at("mix_out", [P, TT, D], R2)
        GP = at("post_gain", [P, D], R2 + 13312)
        JUNK2 = at("junk2", [P, D], R2 + 14336)
        XRR = at("x1_again", [P, 2, D], R2 + 15360)
        UB = at("up_buf", [P, 2, N_TOK], c1)
        A4 = at("ffn_in", [P, 2, KT, N_TOK], R1, F32R)
        FFT = at("ffn_mid", [P, FT, N_TOK], TOP - FT * N_TOK)
        FS = at("ffn_split", [P, 2, 2, N_TOK], R1, F32R)[:, :, :, 0:FW]
        Y2 = at("ffn_out", [P, 4, D], R1 + 4096)
        XF = at("x2_again", [P, 2, D], R1 + 8192)
        GL = at("last_gain", [P, D], R1 + 10240)
        JUNK3 = at("junk3", [P, D], R1 + 11264)

        PB = ctx.enter_context(nc.psum_tensor("psum", [P, 8, 512], F32))

        def pair(d):
            return PB[:, 2 * d:2 * d + 2, :].rearrange("p b n -> p (b n)")

        def pair_tiles(d):
            return PB[:, 2 * d:2 * d + 2, :].rearrange("p b (k n) -> p (b k) n", n=P)

        def nt_pair(n):
            return (n - N_A3) % 4 if N_A3 <= n < N_A4 else n % 2

        def tm_bank(n):
            return 4 + n % 4

        def slot(c):
            return WR[:, c % 4, 0, :], WR[:, c % 4, 1, :]

        def plain(r):
            return r.bitcast(F32)

        def tokens_of(u):
            return (META + P * u, P) if u < TT else (0, META)

        def pair_place(p):
            r = DH * (p // 4 % 2)
            return slice(r, r + DH), slice(PAIR * (p % 4), PAIR * (p % 4) + PAIR), p % 4

        def stick_tile(i):
            h, t = divmod(i, TT)
            return TT - 1 - t if h % 2 else t

        def turned(i):
            return sum(stick_tile(x) // 4 + 1 for x in range(i))

        def down_ready(eng, half, t):
            if t < 3:
                eng.wait_ge(S["dn_mm"], 3 * half + t + 1)
            else:
                eng.wait_ge(S["w_used"], C_DOWN + FT * (half + 1))

        def merged_tile(f):
            return MRR[:, f, :] if f < 2 else MGO[f % 6][:, :]

        def folded(n):
            h, i = divmod(n, NF)
            return h, h * FOLDS + P * i, (P if i < 4 else REST[h])

        w_dram = weight_chunks(a, const)

        block = ctx.enter_context(nc.Block())

        def x_tile(t):
            return a["x"][0, P * t:P * t + P, :] if t < TT else a["meta_tokens"]

        def small_loads(sp):
            nf = 2 * FT
            sp.wait_ge(S["vec_zero"], 1)
            sp.dma_start(VROW[0:nf, :, :], a["conv_ffn_w_2"][0].rearrange("i (m p) -> m i p", p=P)).then_inc(S["vec_in"], 16)
            sp.dma_start(VROW[nf:nf + 4, :, :], a["conv_mix_w_2"][0].rearrange("i (m p) -> m i p", p=P)).then_inc(S["vec_in"], 16)
            sp.dma_start(VROW[nf + 4:nf + 8, 0, :], a["b_fmix"][0].rearrange("(m g) d -> m (g d)", g=2)).then_inc(S["vec_in"], 16)
            sp.dma_start(CWRAW[:, :, :], const["channel"]).then_inc(S["cw_in"], 16)
            sp.wait_ge(S["cw_zero"], 1)
            for g in range(8):
                r = DH * (g % 2)
                sp.dma_start(WBD[r:r + DH, g // 2, r:r + DH], a["w_fmix"][0, g]).then_inc(S["cw_in"], 16)
            sp.dma_start(ROPER[:, :, :, :], const["rope"]).then_inc(S["rope_in"], 16)
            sp.dma_start(GAINS[:, 0, :], a["q_norm_g"][0, :].partition_broadcast(P)).then_inc(S["rope_in"], 16)
            sp.dma_start(GAINS[:, 1, :], a["k_norm_g"][0, :].partition_broadcast(P)).then_inc(S["rope_in"], 16)

        @block.sync
        def _(sp):
            for t in range(1, KTILES, 2):
                sp.dma_start(XALL[0:tokens_of(t)[1], t, :], x_tile(t)).then_inc(S[f"x_in{t}"], 16)
                if t == 1:
                    sp.dma_start(IDENT[:, :], const["ident"]).then_inc(S["consts"], 16)
            for c in range(C_UP):
                if c == 2:
                    small_loads(sp)
                if c >= 2:
                    sp.wait_ge(S["w_split"], c - 1)
                width, parts = w_dram[c]
                for first, src in parts:
                    size = int(np.prod(src.shape[1:]))
                    dst = WS[:, c % 2, first:first + size]
                    if len(src.shape) == 3:
                        dst = dst.rearrange("p (k n) -> p k n", k=src.shape[1])
                    sp.dma_start(dst, src).then_inc(S[f"w_staged{c % 2}"], 16)
            up = a["w_up_2"][0].rearrange("(k p) n -> p k n", p=P)
            with sp.Fori(0, FT) as j:
                for s in range(2):
                    sp.wait_ge(S["w_split"], j * 2 + (C_UP + s - 1))
                    sp.dma_start(WS[:, s, 0:WCH].rearrange("p (k n) -> p k n", k=KT),
                                 up[:, :, bass.ds(j * P + s * FF, P)]).then_inc(S[f"w_staged{s}"], 16)
            down = a["w_down_2"][0].rearrange("(k p) n -> p k n", p=P)
            for half in range(2):
                with sp.Fori(0, FT // 2) as j:
                    for s in range(2):
                        sp.wait_ge(S["w_split"], j * 2 + (C_DOWN + FT * half + s - 1))
                        sp.dma_start(WS[:, s, 0:WCH].rearrange("p (k n) -> p k n", k=1),
                                     down[:, bass.ds(j * 2 + s, 1), :]).then_inc(S[f"w_staged{s}"], 16)

        @block.gpsimd
        def _(pool):
            def split(c, s, r, width, staged, free):
                pool.wait_ge(S[f"w_staged{s}"], staged)
                if free is not None:
                    pool.wait_ge(S["w_used"], free)
                w = width - 8
                pool.tensor_tensor(WR[:, r, 0, w:width], WS[:, s, w:width], ZERO[:, :], ALU.add)
                pool.tensor_scalar(WR[:, r, 0, 0:w], WS[:, s, 0:w], 1.0, 0.0, ALU.mult, ALU.add).then_inc(S["w_hi"], 1)
                pool.wait_ge(S["w_hi"], c + 1)
                pool.tensor_tensor(WR[:, r, 1, 0:width], WS[:, s, 0:width], plain(WR[:, r, 0, 0:width]),
                                   ALU.subtract).then_inc(S["w_split"], 1)

            pool.memset(ZERO[:, :], 0.0).then_inc(S["zero_set"], 1)
            pool.wait_ge(S["zero_set"], 1)
            peeled = C_FGATE + 2
            staged = [0, 0]
            for c in range(peeled):
                staged[c % 2] += 16 * len(w_dram[c][1])
                split(c, c % 2, c % 4, w_dram[c][0], staged[c % 2], c - 3 if c >= 4 else None)
            spans = [(peeled, C_CONV + 4, 1), (C_CONV + 4, C_MRG, 1), (C_MRG, C_OUT2, 3), (C_OUT2, C_END, 1)]
            def stack_part_lo(h, part):
                r = DH * (h % 2)
                pool.wait_ge(S["st_a"], 3 * h + part + 3)
                pool.wait_ge(S["st_v"], 3 * h + part)
                if part == 0:
                    pool.tensor_tensor(QS2[h % 2][DH - r:P - r, :], QT[r:r + DH, h // 2, :], plain(QS2[h % 2][r:r + DH, :]),
                                    ALU.subtract).then_inc(S["st_v"], 1)
                else:
                    q = (r, DH - r)[part - 1]
                    pool.tensor_tensor(KLL2[h % 2][q:q + DH, :], KT2[r:r + DH, h // 2, :], plain(KHH2[h % 2][r:r + DH, :]),
                                    ALU.subtract).then_inc(S["st_v"], 1)

            for c_from, c_to, kind in spans:
                if c_from == C_CONV + 4:
                    pool.wait_ge(S["w_split"], C_CONV + 4)
                    for h in range(1, HEADS):
                        for part in range(3):
                            stack_part_lo(h, part)
                    pool.wait_ge(S["st_v"], 3 * HEADS)
                if kind == 3:
                    with pool.Fori(0, (c_to - c_from) // 12) as i:
                        loads = [0, 0]
                        for k in range(12):
                            c = c_from + k
                            loads[c % 2] += 32 if k % 3 == 2 else 16
                            split(i * 12 + c, c % 2, c % 4, WCH, i * 128 + (staged[c % 2] + loads[c % 2]),
                                  i * 12 + (c - 3))
                    staged = [staged[0] + 256, staged[1] + 256]
                else:
                    whole = (c_to - c_from) // 4 * 4
                    with pool.Fori(0, whole // 4) as i:
                        for k in range(4):
                            c = c_from + k
                            split(i * 4 + c, c % 2, c % 4, WCH, i * 32 + (staged[c % 2] + 16 * (k // 2 + 1)),
                                  i * 4 + (c - 3))
                    staged = [staged[0] + 8 * whole, staged[1] + 8 * whole]
                    for c in range(c_from + whole, c_to):
                        staged[c % 2] += 16
                        split(c, c % 2, c % 4, WCH, staged[c % 2], c - 3)

        @block.tensor
        def _(pe):
            n_nt, n_tm, n_fm = 0, 0, 0

            def settle(nt=0, tm=0, fm=0):
                for name, count in (("nt_free", nt), ("tm_free", tm), ("fm_free", fm)):
                    if count:
                        pe.wait_ge(S[name], count)

            def three(dst, sh, sl, mh, ml, first, last):
                pe.matmul(dst, sh, mh, start=first, stop=False)
                pe.matmul(dst, sh, ml, start=False, stop=False)
                return pe.matmul(dst, sl, mh, start=False, stop=last)

            def transpose_tile(n, n0, first_use, rows=P):
                pe.wait_ge(S["nt_xn"], n + 1)
                if n - first_use >= 2:
                    pe.wait_ge(S["nt_free"], n - 1)
                for k in range(KT):
                    ins = pe.transpose(pair_tiles(n % 2)[:, k, 0:rows], XN[first_use][0:rows, n % 2, P * k:P * k + P],
                                       IDENT[0:rows, 0:rows])
                ins.then_inc(S["nt_mm"], 1)

            def tm_units(t0, units, c0, chunks, ncols, stat, before=None, after=None, follows=False):
                def part(u, j):
                    n, ins = t0 + u, None
                    if j == 0:
                        if before is not None:
                            before(u)
                        if u >= 4 or follows:
                            pe.wait_ge(S["tm_free"], n - 3)
                    if u == 0:
                        pe.wait_ge(S["w_split"], c0 + j + 1)
                    mh, ml = slot(c0 + j)
                    for q in range(WCH // ncols):
                        k = j * (WCH // ncols) + q
                        sh, sl = stat(u, k)
                        ins = three(PB[0:sh.shape[1], tm_bank(n), 0:ncols], sh, sl, mh[:, q * ncols:(q + 1) * ncols],
                                    ml[:, q * ncols:(q + 1) * ncols], k == 0, k == KT - 1)
                    if u == units - 1:
                        ins.then_inc(S["w_used"], 1)
                    elif j == chunks - 1:
                        ins.then_inc(S["tm_mm"], 1)

                for u in range(units - 2):
                    for j in range(chunks):
                        part(u, j)
                    if after is not None:
                        after(u)
                for j in range(chunks):
                    part(units - 2, j)
                    part(units - 1, j)
                if after is not None:
                    after(units - 2)
                    after(units - 1)

            def fm_unit(n, wait, c, mov, banks=None):
                banks = n % 4 if banks is None else banks
                pe.wait_ge(S["w_split"], c + 1)
                if wait:
                    pe.wait_ge(S["fm_free"], n - 3)
                sh, sl = slot(c)
                for h in range(2):
                    for k in range(KT):
                        mh, ml = mov(k, h)
                        ins = three(PB[:, 2 * banks + h, :], sh[:, P * k:P * k + P], sl[:, P * k:P * k + P],
                                    mh, ml, k == 0, k == KT - 1)
                return ins

            pe.wait_ge(S["consts"], 16 * N_CONSTS)
            for t in range(KTILES):
                transpose_tile(N_U + t, N_U, N_U, tokens_of(t)[1])
            pe.wait_ge(S["vec_in"], 48)
            for i in range(3):
                ins = pe.transpose(PB[:, 7, VROWS * i:VROWS * (i + 1)], VROW[:, i, :], IDENT[0:VROWS, 0:VROWS])
            ins.then_inc(S["vec_t"], 1)
            settle(nt=KTILES)
            pe.wait_ge(S["cw_in"], 16 * 9)
            for i in range(2):
                ins = pe.matmul(PB[:, i, :], CWRAW[:, i, :], WBD[:, :, :].rearrange("p j n -> p (j n)"),
                                start=True, stop=True)
            ins.then_inc(S["cw_mm"], 1)
            pe.wait_ge(S["vec_done"], 1)

            def fold_stat(u, k):
                h, first, rows = folded(u)
                if u % NF == 0:
                    pe.wait_ge(S["fold_done"], KT * h + k + 1)
                return AF[:, 0, k, first:first + rows], AF[:, 1, k, first:first + rows]

            tm_units(T_FIN, 2 * NF, C_FIN, 4, FW, fold_stat)

            pe.wait_ge(S["tail_done"], 1)
            pe.wait_ge(S["tm_free"], 2 * NF)
            for h in range(2):
                for kind in range(2):
                    c = C_DFT + 2 * h + kind
                    pe.wait_ge(S["w_split"], c + 1)
                    mh, ml = slot(c)
                    for ct in range(4):
                        n = T_DFT + 16 * h + 4 * kind + ct
                        pe.wait_ge(S["tm_free"], n - 3)
                        for i in range(NF):
                            sh, sl = (FC[:, x, kind, i, P * ct:P * ct + P] for x in range(2))
                            vh, vl = ((v[:, HALF * i:HALF * (i + 1)] for v in (mh, ml)) if i < 4 else
                                      (TAIL[:, x, 2 * h + kind, :] for x in range(2)))
                            ins = three(PB[:, tm_bank(n), 0:HALF], sh, sl, vh, vl, i == 0, i == NF - 1)
                        ins.then_inc(S["w_used"] if ct == 3 else S["tm_mm"], 1)
                pe.wait_ge(S["tm_free"], T_DFT + 16 * h + 8)
                pe.wait_ge(S["cw_done"], 2)
                for j in range(4):
                    for kind in range(2):
                        n = T_DFT + 16 * h + 8 + 2 * j + kind
                        pe.wait_ge(S["tm_free"], n - 3)
                        three(PB[:, tm_bank(n), 0:HALF], CW[:, 0, kind, j, :], CW[:, 1, kind, j, :],
                              DE[:, 0, kind, j, :], DE[:, 1, kind, j, :], True, True).then_inc(S["tm_mm"], 1)

            for t in range(KTILES):
                transpose_tile(N_A1 + t, N_A1, N_A1, tokens_of(t)[1])

            def a1_half(k, h):
                return (A1[:, x, k, META + FW * h:META + FW * (h + 1)] for x in range(2))

            def a1_stat(u, k):
                first, rows = tokens_of(u)
                return A1[:, 0, k, first:first + rows], A1[:, 1, k, first:first + rows]

            settle(nt=N_A1 + KTILES, tm=T_KV)
            for f in range(4):
                fm_unit(U_FGATE + f, False, C_FGATE + f, a1_half).then_inc(S["w_used"], 1)
            settle(fm=4)

            def turn_k(u):
                rows = tokens_of(u)[1]
                pe.wait_ge(S["pr_rope"], u + 1)
                if u >= 2:
                    pe.wait_ge(S["kv_kll"], 2 * (u - 1))
                for g in range(KV_HEADS):
                    ins = pe.transpose(pair_tiles(u % 2)[0:DH, g, 0:rows], RQ[0:rows, u % 2, DH * g:DH * g + DH],
                                       IDENT[0:rows, 0:rows])
                ins.then_inc(S["pr_t"], 1)

            def turn_q(u):
                pe.wait_ge(S["pr_rope"], KTILES + u + 1)
                if u >= 2:
                    pe.wait_ge(S["pr_done"], u - 1)
                for g in range(HEADS):
                    ins = pe.transpose(pair_tiles(u % 2)[0:DH, g, :], RQ[:, (KTILES + u) % 2, DH * g:DH * g + DH],
                                       IDENT[:, :])
                ins.then_inc(S["pr_t"], 1)

            tm_units(T_KV, KTILES, C_KV, 2, 256, a1_stat, after=lambda u: turn_k(u - 1) if u else None)
            turn_k(KTILES - 1)
            pe.wait_ge(S["kv_kll"], 2 * KTILES)
            tm_units(T_Q, TT, C_Q, 4, FW, a1_stat, after=lambda u: turn_q(u - 1) if u else None)
            for f in range(4):
                if f < 2:
                    settle(tm=T_Q + TT - 1 + f)
                if f:
                    pe.wait_ge(S["pr_done"], TT - 2 + min(f, 2))
                fm_unit(U_AGATE + f, False, C_AGATE + f, a1_half, A_GATE_PAIRS[f]).then_inc(S["w_used"], 1)
                if f == 0:
                    turn_q(TT - 1)
            settle(fm=7)

            def scores(i):
                h, t = divmod(i, TT)
                for b in range(3):
                    if i:
                        pe.wait_ge(S["sc_exp"], 3 * i - 2 + b)
                    for x, k2 in enumerate((KHH, KLL)):
                        ins = pe.matmul(PB[:, b, 0:KPART], QS[:, h, P * t:P * t + P],
                                        k2[:, h // GROUP, KPART * b:KPART * (b + 1)], start=x == 0, stop=x == 1)
                ins.then_inc(S["sc_mm"], 1)

            def turn_probs(i):
                pe.wait_ge(S["sc_exp"], 3 * i + 3)
                for g in range(3):
                    if i:
                        pe.wait_ge(S["pt_lo"], 3 * (i - 1) + g + 1)
                    for kt in range(4 * g, min(4 * g + 4, KTILES)):
                        first, rows = tokens_of(kt)
                        ins = pe.transpose(PB[0:rows, 3 + g, P * (kt % 4):P * (kt % 4) + P],
                                           PR[:, i % 2, first:first + rows], IDENT[:, :])
                    ins.then_inc(S["pt_mm"], 1)

            def attend(p, part):
                g = p // 4 // GROUP
                if part == 0:
                    pe.wait_ge(S["pt_lo"], 6 * (p + 1))
                    if p >= 2:
                        pe.wait_ge(S["o_out"], p - 1)
                dst = PB[:, 6 + p % 2, 0:PAIR]
                for kt in (range(5), range(5, KTILES))[part]:
                    ph, pl = (PT[:, x, kt, PAIR * (p % 2):PAIR * (p % 2) + PAIR] for x in range(2))
                    pe.matmul(dst, VV[:, kt, g, 0:P], ph, start=kt == 0, stop=False)
                    pe.matmul(dst[0:DH, :], VV[:, kt, g, P:P + DH], ph, start=False, stop=False)
                    ins = pe.matmul(dst, VV[:, kt, g, 0:P], pl, start=False, stop=kt == KTILES - 1)
                if part:
                    ins.then_inc(S["av_mm"], 1)

            pe.wait_ge(S["kdup"], 2)
            scores(0)
            settle(fm=8)
            for i in range(1, HEADS * TT + 3):
                if i < HEADS * TT:
                    scores(i)
                if i <= HEADS * TT:
                    turn_probs(i - 1)
                if i >= 3:
                    attend((i - 3) // 2, (i - 3) % 2)
            pe.wait_ge(S["o_out"], PAIRS)

            def mix_stat(u, k):
                if u == 0 and k < 4:
                    pe.wait_ge(S["mf_done"], k + 1)
                elif u == 0 and k == 4:
                    pe.wait_ge(S["o_lo"], PAIRS)
                m = MIXF if k < 4 else MIXA
                return (m[:, x, k % 4, P * u:P * u + P] for x in range(2))

            tm_units(T_OUT, TT, C_OUT, 4, FW, mix_stat)
            tm_units(T_OUT + TT, TT, C_OUT + 4, 4, FW, mix_stat, follows=True,
                     after=lambda u: transpose_tile(N_A2 + u - LAG, N_A2, N_A2) if u >= LAG else None)

            def a2_stat(u, k):
                return (A2[:, x, k, P * u:P * u + P] for x in range(2))

            def a2_half(k, h):
                return (A2[:, x, k, FW * h:FW * (h + 1)] for x in range(2))

            tm_units(T_V2, TT, C_V2, 4, FW, a2_stat, follows=True,
                     before=lambda u: pe.wait_ge(S["nt_free"], N_A2 + u + 1),
                     after=lambda u: transpose_tile(N_A2 + TT - LAG + u, N_A2, N_A2) if u < LAG else None)
            settle(tm=T_OUT2)
            for f in range(8):
                fm_unit(U_QK2 + f, f >= 4, C_QK2 + f, a2_half).then_inc(S["w_used"], 1)
            settle(fm=U_QK2 + 5)

            def stick_scores(i):
                h, t = i // TT, stick_tile(i)
                n = P * (t + 1)
                if i % TT == 0:
                    pe.wait_ge(S["st_a"], 3 * (h + 1) + 2)
                    pe.wait_ge(S["st_v"], 3 * (h + 1))
                if i >= 2:
                    pe.wait_ge(S["z_e"], i - 1)
                for b in range((n + FW - 1) // FW):
                    lo, hi = FW * b, min(n, FW * (b + 1))
                    q = QS2[h % 2][:, P * t:P * t + P]
                    pe.matmul(PB[:, 2 * (i % 2) + b, 0:hi - lo], q, KHH2[h % 2][:, lo:hi], start=True, stop=False)
                    pe.matmul(PB[:, 2 * (i % 2) + b, 0:hi - lo], q, KLL2[h % 2][:, lo:hi], start=False, stop=hi < n)
                ins = pe.matmul(PB[:, 2 * (i % 2) + b, hi - lo - P:hi - lo], IDR[:, :], CAUSAL[:, :],
                                start=False, stop=True)
                ins.then_inc(S["z_mm"], 1)

            def turn_weights(i):
                t = stick_tile(i)
                pe.wait_ge(S["z_w"], i + 1)
                for g in range(t // 4 + 1):
                    n = turned(i) + g
                    if n >= 2:
                        pe.wait_ge(S["wt_lo"], n - 1)
                    for kt in range(4 * g, min(4 * g + 4, t + 1)):
                        ins = pe.transpose(PB[:, 4 + n % 2, P * (kt % 4):P * (kt % 4) + P],
                                           ZS[:, i % 2, P * kt:P * kt + P], IDENT[:, :])
                    ins.then_inc(S["wt_mm"], 1)

            def stick_attend(p, part):
                h, c2 = p // 4, stick_tile(2 * p) // 2 * 2
                if part == 0:
                    pe.wait_ge(S["wt_lo"], turned(2 * p + 2))
                    if p >= 2:
                        pe.wait_ge(S["at_out"], p - 1)
                for kt in (range(c2 // 2 + 1), range(c2 // 2 + 1, c2 + 2))[part]:
                    q0 = P if kt > c2 else 0
                    vh, vl = (V2[:, x, kt, DH * h:DH * h + DH] for x in range(2))
                    wh, wl = (WT[:, x, kt, PAIR * (p % 2) + q0:PAIR * (p % 2) + PAIR] for x in range(2))
                    ins = three(PB[0:DH, 6 + p % 2, q0:PAIR], vh, vl, wh, wl,
                                kt == 0, kt == c2 + 1)
                if part:
                    ins.then_inc(S["av2_mm"], 1)

            def turn_x1(t):
                n = N_A3 + t
                pe.wait_ge(S["nt_xn"], n + 1)
                if t < 2:
                    pe.wait_ge(S["z_e"], HEADS * TT)
                elif t == 2:
                    pe.wait_ge(S["wt_lo"], turned(HEADS * TT))
                elif t == 3:
                    pe.wait_ge(S["at_out"], PAIRS)
                else:
                    pe.wait_ge(S["nt_free"], n - 3)
                for k in range(KT):
                    ins = pe.transpose(pair_tiles(nt_pair(n))[:, k, :], X1N[:, t, P * k:P * k + P], IDENT[:, :])
                ins.then_inc(S["nt_mm"], 1)

            stick_scores(0)
            settle(fm=U_CONV)
            for i in range(HEADS * TT + 4):
                if i + 1 < HEADS * TT:
                    stick_scores(i + 1)
                if i >= 4:
                    stick_attend((i - 4) // 2, i % 2)
                if 1 <= i <= HEADS * TT:
                    turn_weights(i - 1)
                if i >= HEADS * TT + 2:
                    turn_x1(i - HEADS * TT - 2)
            for t in range(2, TT):
                turn_x1(t)

            settle(nt=N_A4)
            for f in range(12):
                fm_unit(U_CONV + f, f >= 4, C_CONV + f, a2_half).then_inc(S["w_used"], 1)
            for f in range(KT):
                u, c = U_MRG + 4 * f, C_MRG + 3 * f
                fm_unit(u, True, c, a2_half).then_inc(S["w_used"], 1)
                fm_unit(u + 1, True, c + 1, a2_half).then_inc(S["w_used"], 1)
                pe.wait_ge(S["w_split"], c + 3)
                pe.wait_ge(S["at_done"], 4)
                pe.wait_ge(S["cv_done"], 4)
                sh, sl = slot(c + 2)
                for br, m in enumerate((ATS, CTS)):
                    pe.wait_ge(S["fm_free"], u + 2 + br - 3)
                    for h in range(2):
                        for k in range(4):
                            q = 4 * br + k
                            ins = three(PB[:, 2 * ((u + 2 + br) % 4) + h, :], sh[:, P * q:P * q + P],
                                        sl[:, P * q:P * q + P], m[:, 0, k, FW * h:FW * (h + 1)],
                                        m[:, 1, k, FW * h:FW * (h + 1)], k == 0, k == 3)
                ins.then_inc(S["w_used"], 1)
            settle(fm=U_UP)

            def mr_stat(u, k):
                if u == 0:
                    pe.wait_ge(S["mr_done"], MERGED_ORDER.index(k) + 1)
                return (MR[:, x, k, P * u:P * u + P] for x in range(2))

            tm_units(T_OUT2, TT, C_OUT2, 4, FW, mr_stat)
            tm_units(T_OUT2 + TT, TT, C_OUT2 + 4, 4, FW, mr_stat, follows=True,
                     after=lambda u: transpose_tile(N_A4 + u - LAG, N_A4, N_A4) if u >= LAG else None)

            def up_half(s, h):
                for k in range(KT):
                    ins = three(PB[:, 2 * ((s + 2) % 4) + h, :], WR[:, (C_UP + s) % 4, 0, P * k:P * k + P],
                                WR[:, (C_UP + s) % 4, 1, P * k:P * k + P], A4[:, 0, k, FW * h:FW * (h + 1)],
                                A4[:, 1, k, FW * h:FW * (h + 1)], k == 0, k == KT - 1)
                if h:
                    ins.then_inc(S["w_used"], 1)
                elif s == 3:
                    ins.then_inc(S["up_half"], 1)

            for s in range(2):
                pe.wait_ge(S["nt_free"], N_A4 + TT // 2)
                pe.wait_ge(S["tm_free"], T_OUT2 + 2 * TT)
                pe.wait_ge(S["w_split"], C_UP + s + 1)
                up_half(s, 0)
                transpose_tile(N_A4 + TT - LAG + s, N_A4, N_A4)
            transpose_tile(N_A4 + TT - 1, N_A4, N_A4)
            settle(nt=N_A4 + TT)
            for s in range(2):
                up_half(s, 1)
            for s in range(2, 4):
                pe.wait_ge(S["w_split"], C_UP + s + 1)
                up_half(s, 0)
                up_half(s, 1)
            with pe.Fori(1, FT // 2) as i:
                for s in range(4):
                    pe.wait_ge(S["w_split"], i * 4 + (C_UP + s + 1))
                    pe.wait_ge(S["fm_free"], i * 4 + (U_UP + s - 3))
                    up_half(s, 0)
                    up_half(s, 1)

            for half in range(2):
                def down(j, s, first=False, last=False):
                    c = C_DOWN + FT * half
                    pe.wait_ge(S["w_split"], j + (c + 1))
                    pe.wait_ge(S["dn_lo"], j + (FT * half + 1))
                    r = (c + s) % 4
                    for t in ((2, 3, 0, 1) if first and not half else range(4)):
                        if first and not half:
                            pe.wait_ge(S["fm_free"], U_UP + 2 * FT - 3 + (t + 2) % 4)
                        elif first:
                            pe.wait_ge(S["dn_ya"], t + 1)
                            pe.wait_ge(S["dn_yv"], t + 1)
                        sh, sl = (FS[:, s % 2, x, P * t:P * t + P] for x in range(2))
                        for g in range(2):
                            ins = three(PB[:, 2 * t + g, :], sh, sl, WR[:, r, 0, FW * g:FW * (g + 1)],
                                        WR[:, r, 1, FW * g:FW * (g + 1)], first, last)
                        if last and t < 3:
                            ins.then_inc(S["dn_mm"], 1)
                    ins.then_inc(S["w_used"], 1)

                down(0, 0, first=True)
                down(1, 1)
                with pe.Fori(0, (FT - 4) // 4) as i:
                    for s in range(2, 6):
                        down(i * 4 + s, s)
                for s in range(FT - 4, FT):
                    down(s, s, last=s == FT - 1)

        @block.scalar
        def _(act):
            chain = [0]
            jobs = [0, 0]

            def mark(ins):
                chain[0] += 1
                ins.then_inc(S["a_chain"], 1)
                return chain[0]

            def link(ins):
                act.wait_ge(S["a_chain"], mark(ins))

            def load_tables():
                act.add_instruction(mybir.InstLoadActFuncSet(
                    name=nc.get_next_instruction_name(), act_func_set_id=EXP_AND_LN,
                    engine=mybir.EngineType.Activation, ins=[], outs=[]))

            def guess(rows, col, n, scale, by_vector, step=1):
                ss, ln, yy = (b[0:rows, col:col + step * (n - 1) + 1:step] for b in (SS, LN, YY))
                if by_vector:
                    jobs[1] += 1
                    act.wait_ge(S["rs_ss"], jobs[1])
                link(act.activation(ln, ss, ACT.Ln, bias=EPS, scale=scale))
                jobs[0] += 1
                act.activation(yy, ln, ACT.Exp, scale=-0.5).then_inc(S["rs_y"], 1)

            def guess_pair(s):
                if s == 0 or s == TT:
                    guess(P, s if s == 0 else 7 + s, 1, 1.0 / D, False)
                elif s < TT:
                    guess(P, s, 2, 1.0 / D, False, 7)

            def ready(n):
                name, value = TM[n]
                act.wait_ge(S[name], value)

            def load_tile(use, t, src, wait=None):
                if wait is not None:
                    act.wait_ge(S["nt_xn"], wait)
                act.dma_start(XIN[use][0:src.shape[0], (use + t) % 2, :], src).then_inc(S[f"nt_in{(use + t) % 2}"], 16)

            for t in range(0, KTILES, 2):
                act.dma_start(XALL[0:tokens_of(t)[1], t, :], x_tile(t)).then_inc(S[f"x_in{t}"], 16)
                if t == 0:
                    act.dma_start(GB[N_U][:, :], a["norm_g"][0, :].partition_broadcast(P)).then_inc(S["consts"], 16)
                    load_tables()
            nf = 2 * FT

            def u_out(t):
                first, rows = tokens_of(t)
                act.wait_ge(S["nt_mm"], t + 1)
                act.activation(UT[:, :, first:first + rows], pair_tiles(t % 2)[:, :, 0:rows],
                               ACT.Copy).then_inc(S["nt_free"], 1)

            for t in range(0, KTILES, 2):
                both = range(t, min(t + 2, KTILES))
                for x in both:
                    rows = tokens_of(x)[1]
                    act.wait_ge(S[f"x_in{x}"], 16)
                    link(act.activation(JUNK0[0:rows, :], XALL[0:rows, x, :], ACT.Square, accum_out=SS[0:rows, x:x + 1]))
                guess(rows, t, len(both), 1.0 / D, False)
                if t:
                    u_out(t - 2)
                    u_out(t - 1)
            u_out(KTILES - 1)

            act.wait_ge(S["nt_xn"], KTILES)
            act.wait_ge(S["nt_mm"], KTILES)
            act.dma_start(TAILR[:, :, :], const["dft_tail"]).then_inc(S["tail_in"], 16)
            for j in range(2 * KT):
                h, k = divmod(j, KT)
                n = FOLD + 1 - 2 * h
                act.wait_ge(S["fold_sum"], j + 1)
                act.activation(AF[:, 0, k, FOLDS * h:FOLDS * h + n], FSUM[:, j % 2, 0:n], ACT.Copy).then_inc(S["fold_hi"], 1)
            act.wait_ge(S["cw_mm"], 1)
            for i in range(2):
                act.activation(CW[:, 0, i, :, :], PB[:, i, :].rearrange("p (j n) -> p j n", j=4),
                               ACT.Copy).then_inc(S["cw_hi"], 1)
            act.wait_ge(S["tail_in"], 16)
            act.activation(TAIL[:, 0, :, :], TAILR[:, :, :], ACT.Copy).then_inc(S["tail_hi"], 1)

            act.wait_ge(S["fpad"], 1)
            for u in range(2 * NF):
                h, _, rows = folded(u)
                ready(T_FIN + u)
                act.activation(FC[0:rows, 0, h, u % NF, :], PB[0:rows, tm_bank(T_FIN + u), :],
                               ACT.Copy).then_inc(S["tm_hi"], 1)
            for h in range(2):
                for m in range(8):
                    n = T_DFT + 16 * h + m
                    if h and m == 0:
                        ready(T_DFT + 15)
                    ready(n)
                    act.activation(DE[:, 0, m // 4, m % 4, :], PB[:, tm_bank(n), 0:HALF], ACT.Copy).then_inc(S["tm_hi"], 1)
                if h:
                    act.wait_ge(S["w_used"], C_DFT + 4)
                    load_tile(N_A1, 0, x_tile(0))
                    load_tile(N_A1, 1, x_tile(1))
                for j in range(4):
                    n = T_DFT + 16 * h + 8 + 2 * j
                    ready(n)
                    if j >= 2 or h:
                        act.wait_ge(S["tm_free"], n - 2 if j >= 2 else T_DFT + 16)
                    act.activation(CHA[:, j % 2, :], PB[:, tm_bank(n), 0:HALF], ACT.Identity,
                                   bias=VEC[:, 0, nf + 4 + j:nf + 5 + j]).then_inc(S["ch_a"], 1)

            act.wait_ge(S["tm_free"], T_KV)
            for t in range(KTILES):
                n = N_A1 + t
                first, rows = tokens_of(t)
                if t + 2 < KTILES:
                    load_tile(N_A1, t + 2, x_tile(t + 2), n + 1)
                act.wait_ge(S["nt_mm"], n + 1)
                act.activation(A1[:, 0, :, first:first + rows], pair_tiles(n % 2)[:, :, 0:rows],
                               ACT.Copy).then_inc(S["nt_hi"], 1)

            for f in range(4):
                act.wait_ge(S["w_used"], C_FGATE + f + 1)
                if f >= 2:
                    act.wait_ge(S["gate_out"], f - 1)
                act.activation(GE[:, f % 2, :], pair(f), ACT.Sigmoid).then_inc(S["gate_sig"], 1)
                if f:
                    act.wait_ge(S["gate_out"], f)
                    act.dma_start(scratch["mixed_f"][P * (f - 1):P * f, :], FT1[:, f - 1, :]).then_inc(S["gate_stored"], 16)
            act.wait_ge(S["gate_out"], 4)
            act.dma_start(scratch["mixed_f"][3 * P:4 * P, :], FT1[:, 3, :]).then_inc(S["f_gate_last"], 16)

            load_tables()
            act.wait_ge(S["gate_stored"], 48)
            act.wait_ge(S["vv_set"], 3)
            for u in range(KTILES + 1):
                if u < KTILES:
                    rows = tokens_of(u)[1]
                    n = T_KV + u
                    col = 8 * (u % 2)
                    ready(n)
                    act.activation(SQ[0:rows, u % 2, 0:P], PB[0:rows, tm_bank(n), 0:P], ACT.Square).then_inc(S["pr_sq"], 1)
                    act.activation(VV[0:rows, u, :, 0:DH],
                                   PB[0:rows, tm_bank(n), P:2 * P].rearrange("p (g d) -> p g d", g=KV_HEADS),
                                   ACT.Copy).then_inc(S["kv_vhi"], 1)
                    guess(rows, col, KV_HEADS, 1.0 / DH, True)
                if u:
                    first, rows = tokens_of(u - 1)
                    act.wait_ge(S["pr_t"], u)
                    for x in range(2):
                        act.activation(KHH[DH * x:DH * x + DH, :, first:first + rows],
                                       pair_tiles((u - 1) % 2)[0:DH, 0:KV_HEADS, 0:rows], ACT.Copy).then_inc(S["kv_khh"], 1)
            for u in range(TT + 1):
                if u < TT:
                    n = T_Q + u
                    ready(n)
                    act.activation(SQ[:, (KTILES + u) % 2, :], PB[:, tm_bank(n), :], ACT.Square).then_inc(S["pr_sq"], 1)
                    guess(P, 8 * ((KTILES + u) % 2), HEADS, 1.0 / DH, True)
                if u:
                    act.wait_ge(S["pr_t"], KTILES + u)
                    act.activation(QS[0:DH, :, P * (u - 1):P * u], pair_tiles((u - 1) % 2)[0:DH, :, :],
                                   ACT.Copy).then_inc(S["pr_hi"], 1)
            act.wait_ge(S["f_gate_last"], 16)
            for f in range(4):
                act.wait_ge(S["w_used"], C_AGATE + f + 1)
                if f >= 2:
                    act.wait_ge(S["gate_stored"], 48 + 16 * (f - 1))
                act.activation(GE2[:, f % 2, :], pair(A_GATE_PAIRS[f]), ACT.Sigmoid).then_inc(S["gate_sig"], 1)
                if f:
                    act.wait_ge(S["gate_out"], 4 + f)
                    act.dma_start(scratch["a_gate"][P * (f - 1):P * f, :], GE2[:, (f - 1) % 2, :]).then_inc(S["gate_stored"], 16)
            act.wait_ge(S["gate_out"], 8)
            act.dma_start(scratch["a_gate"][3 * P:4 * P, :], GE2[:, 1, :]).then_inc(S["gate_stored"], 16)

            def load_a_gate(b):
                h, c = divmod(b, 2)
                r = DH * (h % 2)
                act.dma_start(AG[r:r + DH, b % 2, :], scratch["a_gate"][DH * h:DH * h + DH, FW * c:FW * c + FW])\
                   .then_inc(S[f"ag_in{b % 2}"], 16)

            def probs_hi(i, groups=range(3)):
                t = i % 4
                if t % 2 == 0 and i >= 4:
                    act.wait_ge(S["av_mm"], i // 2 - 1)
                for g in groups:
                    n = 3 * i + g
                    act.wait_ge(S["pt_mm"], n + 1)
                    rows = P if g < 2 else META
                    kts = slice(4 * g, min(4 * g + 4, KTILES))
                    act.activation(PT[0:rows, 0, kts, P * t:P * t + P],
                                   PB[0:rows, 3 + g, 0:P * (4 if g < 2 else 1)].rearrange("p (k n) -> p k n", n=P),
                                   ACT.Copy).then_inc(S["pt_hi"], 1)

            def row_sum_inv(p):
                act.wait_ge(S["av_mm"], p + 1)
                if p >= 2:
                    act.wait_ge(S["o_out"], p - 1)
                rc = RC[:, PAIR * (p % 2):PAIR * (p % 2) + PAIR]
                link(act.activation(rc, PB[DH:P, 6 + p % 2, 0:PAIR], ACT.Ln))
                act.activation(rc, rc, ACT.Exp, scale=-1.0).then_inc(S["o_inv"], 1)

            def attended_hi(p):
                row, col, buf = pair_place(p)
                act.wait_ge(S["o_out"], p + 1)
                act.activation(MIXA[row, 0, p // 8, col], OT[row, buf, :], ACT.Copy).then_inc(S["o_hi"], 1)
                if p % 2 and p // 2 + 2 < 2 * HEADS:
                    load_a_gate(p // 2 + 2)

            load_tables()
            for i in range(HEADS * TT):
                if i == 1:
                    act.wait_ge(S["pt_zero"], 1)
                if i == 2:
                    act.wait_ge(S["gate_stored"], 112)
                    load_a_gate(0)
                    load_a_gate(1)
                if i:
                    probs_hi(i - 1, range(2))
                act.wait_ge(S["sc_max"], i + 1)
                for b in range(3):
                    act.activation(PR[:, i % 2, KPART * b:KPART * (b + 1)], PB[:, b, 0:KPART], ACT.Exp,
                                   bias=NB[:, i % 2:i % 2 + 1], scale=-1.0).then_inc(S["sc_exp"], 1)
                if i:
                    probs_hi(i - 1, range(2, 3))
                if i >= 5 and i % 2:
                    row_sum_inv((i - 5) // 2)
                if i >= 8 and i % 2 == 0:
                    attended_hi((i - 8) // 2)
                if i == HEADS * TT // 2 + 2:
                    act.dma_start(MFR[:, :, :], scratch["mixed_f"].rearrange("(k p) n -> p k n", p=P)).then_inc(S["mf_in"], 16)
            probs_hi(HEADS * TT - 1)
            row_sum_inv(PAIRS - 2)
            attended_hi(PAIRS - 4)
            attended_hi(PAIRS - 3)
            row_sum_inv(PAIRS - 1)
            act.wait_ge(S["mf_in"], 16)
            for f in range(4):
                if f >= 2:
                    attended_hi(PAIRS - 4 + f)
                act.activation(MIXF[:, 0, f, :], MFR[:, f, :], ACT.Copy).then_inc(S["mf_hi"], 1)
            act.dma_start(GF[:, :], a["final_g"].partition_broadcast(P)).then_inc(S["gains_in"], 16)
            act.dma_start(GB[N_A2][:, :], a["norm_mix_pre_2"][0, :].partition_broadcast(P)).then_inc(S["gains_in"], 16)

            def load_residual(m):
                c, u = divmod(m, TT)
                act.dma_start(XR[:, m % 2, :], a["x"][0, P * u:P * u + P, FW * c:FW * c + FW]).then_inc(S[f"op_in{m % 2}"], 16)

            load_residual(0)
            load_residual(1)
            for m in range(2, TT + 2):
                act.wait_ge(S["tm_free"], T_OUT + m - 1)
                load_residual(m)

            def hi_of_tile(n, dst, t):
                act.wait_ge(S["nt_mm"], n + 1)
                act.activation(dst[:, 0, :, P * t:P * t + P], pair_tiles(nt_pair(n)), ACT.Copy).then_inc(S["nt_hi"], 1)

            load_tables()
            for s in range(TT + LAG):
                if s < TT:
                    act.wait_ge(S["tm_free"], T_OUT + TT + s + 1)
                    if s + 2 < TT:
                        load_residual(TT + s + 2)
                    link(act.activation(JUNK[:, :], H[:, s, :], ACT.Square, accum_out=SS[:, s:s + 1]))
                if 1 <= s <= TT:
                    t = s - 1
                    act.wait_ge(S["x1_out"], t + 1)
                    act.dma_start(scratch["x1"][P * t:P * t + P, :], H[:, t, :]).then_inc(S["x1_stored"], 16)
                    link(act.activation(JUNK[:, :], H[:, t, :], ACT.Square, accum_out=SS[:, 8 + t:9 + t]))
                guess_pair(s)
                if s >= LAG:
                    hi_of_tile(N_A2 + s - LAG, A2, s - LAG)

            act.dma_start(CAUSALR[:, :], const["causal"]).then_inc(S["causal_in"], 16)
            act.wait_ge(S["x1_stored"], 16 * TT)
            act.wait_ge(S["nt_free"], N_A3)
            for u in range(TT):
                n = T_V2 + u
                ready(n)
                act.activation(V2[:, 0, u, :], PB[:, tm_bank(n), :], ACT.Copy).then_inc(S["tm_hi"], 1)
            def stack_part(h, part):
                r = DH * (h % 2)
                if h >= 2:
                    act.wait_ge(S["z_mm"], TT * (h - 1))
                    act.wait_ge(S["st_v"], 3 * (h - 1))
                if part == 0:
                    act.activation(QS2[h % 2][r:r + DH, :], QT[r:r + DH, h // 2, :], ACT.Copy).then_inc(S["st_a"], 1)
                else:
                    q = (r, DH - r)[part - 1]
                    act.activation(KHH2[h % 2][q:q + DH, :], KT2[r:r + DH, h // 2, :], ACT.Copy).then_inc(S["st_a"], 1)

            for f in range(8):
                act.wait_ge(S["w_used"], C_QK2 + f + 1)
                act.activation((QT if f < 4 else KT2)[:, f % 4, :], pair((U_QK2 + f) % 4), ACT.Copy,
                               scale=DH ** -0.5 if f < 4 else 1.0).then_inc(S["fm_free"], 1)
                if f == 4:
                    act.wait_ge(S["fm_free"], U_QK2 + 5)
                    act.wait_ge(S["causal_in"], 16)
                    act.activation(CAUSAL[:, :], CAUSALR[:, :], ACT.Copy).then_inc(S["st_a"], 1)
                    act.activation(IDR[:, :], IDENT[:, :], ACT.Copy).then_inc(S["st_a"], 1)
                    for part in range(3):
                        stack_part(0, part)

            def soft_part(i, between):
                n = P * (stick_tile(i) + 1)
                b = ZL[:, i % 2, 0:n]
                act.wait_ge(S["z_mm"], i + 1)
                if i >= 2:
                    act.wait_ge(S["z_e"], i - 1)
                link(act.activation(b, pair(i % 2)[:, 0:n], ACT.Abs))
                count = mark(act.activation(b, b, ACT.Exp, scale=-1.0))
                between()
                act.wait_ge(S["a_chain"], count)
                act.activation(b, b, ACT.Ln, bias=1.0).then_inc(S["z_l"], 1)

            def weights(i):
                n = P * (stick_tile(i) + 1)
                act.wait_ge(S["z_e"], i + 1)
                act.activation(ZS[:, i % 2, 0:n], ZS[:, i % 2, 0:n], ACT.Exp).then_inc(S["z_w"], 1)

            def x1_rows(t):
                return scratch["x1"][P * t:P * t + P, :]

            def weights_hi(i, g):
                if i < 0:
                    return
                t = stick_tile(i)
                c = i // 2 % 2 * 2 + t % 2
                if i % 2 == 0 and i >= 4 and g == 0:
                    act.wait_ge(S["av2_mm"], i // 2 - 1)
                if g <= t // 4:
                    n = turned(i) + g
                    w = min(4, t + 1 - 4 * g)
                    act.wait_ge(S["wt_mm"], n + 1)
                    act.activation(WT[:, 0, 4 * g:4 * g + w, P * c:P * c + P],
                                   PB[:, 4 + n % 2, 0:P * w].rearrange("p (k n) -> p k n", n=P),
                                   ACT.Copy).then_inc(S["wt_hi"], 1)

            act.wait_ge(S["w_used"], C_CONV)
            for i in range(HEADS * TT + 2):
                if i < HEADS * TT:
                    soft_part(i, lambda: weights_hi(i - 2, 0))
                else:
                    weights_hi(i - 2, 0)
                if 1 <= i <= HEADS * TT:
                    weights(i - 1)
                weights_hi(i - 2, 1)
                if i == HEADS * TT - TT:
                    act.wait_ge(S["st_v"], 3 * HEADS)
                    act.dma_start(GB[N_A3][:, :], a["norm_mix_pre_2"][0, :].partition_broadcast(P)).then_inc(S["gains_in"], 16)
                    for t in range(TT):
                        act.dma_start(X1N[:, t, :], x1_rows(t)).then_inc(S[f"x_in{t}"], 16)
                part = i % TT - 3 * (i // TT % 2)
                if 0 <= part < 3 and i < (HEADS - 1) * TT:
                    stack_part(i // TT + 1, part)

            act.wait_ge(S["av2_mm"], PAIRS)
            for t in range(TT):
                hi_of_tile(N_A3 + t, A2, t)
            act.wait_ge(S["at_out"], PAIRS)
            for f in range(4):
                act.activation(ATS[:, 0, f, :], AT[:, f, :], ACT.Copy).then_inc(S["at_hi"], 1)

            act.wait_ge(S["at_done"], 4)
            act.wait_ge(S["nt_free"], N_A4)
            for f in range(5):
                if f < 4:
                    act.wait_ge(S["w_used"], C_CONV + 3 * f + 1)
                    if f:
                        act.wait_ge(S["fm_free"], U_CONV + 3 * f - 2)
                    act.activation(CCB[:, :], pair((U_CONV + 3 * f) % 4), ACT.Copy).then_inc(S["cv_cc"], 1)
                if f:
                    act.wait_ge(S["fm_free"], U_CONV + 3 * f)
                    act.activation(CTS[:, 0, f - 1, :], CO[:, :], ACT.Copy).then_inc(S["cv_hi"], 1)

            act.wait_ge(S["cv_done"], 4)
            for f in range(KT):
                if f:
                    act.wait_ge(S["mg_out"], f)
                for g in range(2):
                    act.wait_ge(S["w_used"], C_MRG + 3 * f + g + 1)
                    act.activation(MGE[:, g, :], pair((U_MRG + 4 * f + g) % 4), ACT.Sigmoid)\
                       .then_inc(S["fm_free"], 1)
                if 1 <= f <= 2:
                    act.dma_start(scratch["merged"][P * (f - 1):P * f, :], MGO[f - 1][:, :])\
                       .then_inc(S[f"mg_st{f - 1}"], 16)
            act.wait_ge(S["w_used"], C_OUT2 - 1)
            for i in range(2):
                act.wait_ge(S[f"mg_st{i}"], 16)
                act.dma_start(MRR[:, i, :], scratch["merged"][P * i:P * i + P, :]).then_inc(S[f"mr_in{i}"], 16)
            for f in MERGED_ORDER:
                if f >= 2:
                    act.wait_ge(S["mg_out"], f + 1)
                else:
                    act.wait_ge(S[f"mr_in{f}"], 16)
                act.activation(MR[:, 0, f, :], merged_tile(f), ACT.Copy).then_inc(S["mr_hi"], 1)
            act.dma_start(GP[:, :], a["norm_mix_post_2"][0, :].partition_broadcast(P)).then_inc(S["gains2_in"], 16)
            act.dma_start(GB[N_A4][:, :], a["norm_ffn_pre_2"][0, :].partition_broadcast(P)).then_inc(S["gains2_in"], 16)

            def mix_out(m):
                c, u = divmod(m, TT)
                n = T_OUT2 + m
                ready(n)
                act.activation(Y[:, u, FW * c:FW * c + FW], PB[:, tm_bank(n), :], ACT.Copy).then_inc(S["tm_free"], 1)

            def load_x1(t):
                act.dma_start(XRR[:, t % 2, :], x1_rows(t)).then_inc(S[f"xr_in{t % 2}"], 16)

            load_tables()
            load_x1(0)
            load_x1(1)
            for m in range(TT):
                mix_out(m)
            for s in range(TT + LAG):
                if s < TT:
                    mix_out(TT + s)
                if s < TT:
                    act.wait_ge(S["tm_free"], T_OUT2 + TT + s + 1)
                    link(act.activation(JUNK2[:, :], Y[:, s, :], ACT.Square, accum_out=SS[:, s:s + 1]))
                if 1 <= s <= TT:
                    t = s - 1
                    act.wait_ge(S["x2_out"], t + 1)
                    act.dma_start(scratch["x2"][P * t:P * t + P, :], Y[:, t, :]).then_inc(S["x2_stored"], 16)
                    if t + 2 < TT:
                        load_x1(t + 2)
                    link(act.activation(JUNK2[:, :], Y[:, t, :], ACT.Square, accum_out=SS[:, 8 + t:9 + t]))
                guess_pair(s)
                if s >= LAG:
                    hi_of_tile(N_A4 + s - LAG, A4, s - LAG)

            act.wait_ge(S["x2_stored"], 16 * TT)
            act.wait_ge(S["nt_free"], N_A4 + TT)
            def up_steps(i, last):
                for s in range(4):
                    q, g = divmod(s, 2)
                    if last and s == 3:
                        act.wait_ge(S["up_half"], FT // 2)
                        mid_hi(0, 0, 0)
                        mid_hi(0, 1, 1)
                    act.wait_ge(S["w_used"], i * 4 + (C_UP + s + 1))
                    act.wait_ge(S["up_f"], i * 2 + (q + 1))
                    act.activation(UB[:, g, :], pair((s + 2) % 4), ACT.Copy,
                                   scale=VEC[:, 2, bass.ds(i * 2 + (q + FT * g), 1)]).then_inc(S["up_c"], 1)
                    if g:
                        act.wait_ge(S["fm_free"], i * 4 + (U_UP + s + 1))
                        act.activation(UB[:, 1, :], UB[:, 1, :], ACT.Gelu_apprx_tanh).then_inc(S["up_g"], 1)

            def mid_hi(half, j, s):
                if half or not isinstance(j, int) or j >= 2:
                    act.wait_ge(S["w_used"], j + (C_DOWN + FT * half - 1))
                src = FFT[:, j, FW * half:FW * half + FW] if isinstance(j, int) else \
                    FFT[:, bass.ds(j, 1), FW * half:FW * half + FW].rearrange("p a n -> p (a n)")
                act.activation(FS[:, s, 0, :], src, ACT.Copy).then_inc(S["dn_hi"], 1)

            with act.Fori(0, FT // 2 - 1) as i:
                up_steps(i, False)
            up_steps(FT // 2 - 1, True)

            def load_x2(m):
                act.dma_start(XF[:, m % 2, :], scratch["x2"][P * m:P * m + P, :]).then_inc(S[f"xf_in{m % 2}"], 16)

            def finish(half, s):
                if s < 4:
                    link(act.activation(JUNK3[:, :], Y2[:, s, :], ACT.Square, accum_out=SS[:, s:s + 1]))
                    guess(P, s, 1, 1.0 / D, False)
                if s:
                    m = 4 * half + s - 1
                    act.wait_ge(S["f_out"], m + 1)
                    act.dma_start(out[0, P * m:P * m + P, :], Y2[:, s - 1, :]).then_inc(S["f_stored"], 16)
                    if m + 2 < TT:
                        load_x2(m + 2)

            act.wait_ge(S["w_used"], C_DOWN)
            act.wait_ge(S["up_f"], FT + 1)
            load_tables()
            act.dma_start(GL[:, :], a["norm_ffn_post_2"][0, :].partition_broadcast(P)).then_inc(S["gains3_in"], 16)
            load_x2(0)
            load_x2(1)
            for half in range(2):
                if half:
                    mid_hi(1, 1, 1)
                    for s in range(6):
                        if s < 5:
                            finish(0, s)
                        mid_hi(1, s + 2, s % 2)
                with act.Fori(4 if half else 1, FT // 2) as i:
                    for s in range(2):
                        mid_hi(half, i * 2 + s, s)
                if half:
                    act.wait_ge(S["f_stored"], 64)
                else:
                    mid_hi(1, 0, 0)
                for t in range(4):
                    down_ready(act, half, t)
                    act.activation(Y2[:, t, 0:FW], PB[:, 2 * t, :], ACT.Copy).then_inc(S["dn_ya"], 1)
                act.wait_ge(S["dn_ya"], 4 * half + 4)
                act.wait_ge(S["dn_yv"], 4 * half + 4)
            for s in range(5):
                finish(1, s)
            act.wait_ge(S["f_stored"], 16 * TT)

        @block.vector
        def _(v):
            chain = [0]
            jobs = [0]

            def mark(ins):
                chain[0] += 1
                ins.then_inc(S["v_chain"], 1)
                return chain[0]

            def link(ins):
                v.wait_ge(S["v_chain"], mark(ins))

            def refine(rows, col, n, scale, dst, step=1):
                jobs[0] += 1
                ss, m, y, ya, yb, dst = (b[0:rows, col:col + step * (n - 1) + 1:step] for b in (SS, MM, YY, YA, YB, dst))
                v.wait_ge(S["rs_y"], jobs[0])
                mark(v.tensor_scalar(m, ss, scale, EPS, ALU.mult, ALU.add))
                link(v.scalar_tensor_tensor(out=ya, in0=y, scalar=-0.5, in1=y, op0=ALU.mult, op1=ALU.mult))
                link(v.tensor_tensor(yb, ya, m, ALU.mult))
                link(v.scalar_tensor_tensor(out=dst, in0=yb, scalar=1.5, in1=y, op0=ALU.add, op1=ALU.mult))

            def ready(n):
                name, value = TM[n]
                v.wait_ge(S[name], value)

            def refine_pair(s):
                if s == 0 or s == TT:
                    refine(P, s if s == 0 else 7 + s, 1, 1.0 / D, RX)
                elif s < TT:
                    refine(P, s, 2, 1.0 / D, RX, 7)

            def normalise(use, t, src, rstd, rows=P):
                n = use + t
                if t >= 2:
                    v.wait_ge(S["nt_mm"], n - 1)
                v.scalar_tensor_tensor(out=XN[use][0:rows, n % 2, :], in0=src, scalar=rstd, in1=GB[use][0:rows, :],
                                       op0=ALU.mult, op1=ALU.mult).then_inc(S["nt_xn"], 1)

            def lo_of_tile(n, dst, first, rows=P):
                v.wait_ge(S["nt_hi"], n - N_A1 + 1)
                v.tensor_tensor(dst[:, 1, :, first:first + rows], pair_tiles(nt_pair(n))[:, :, 0:rows],
                                plain(dst[:, 0, :, first:first + rows]), ALU.subtract).then_inc(S["nt_free"], 1)

            v.memset(VROW[:, :, :], 0.0).then_inc(S["vec_zero"], 1)
            v.memset(WBD[:, :, :], 0.0).then_inc(S["cw_zero"], 1)
            v.wait_ge(S["consts"], 16 * N_CONSTS)
            for t in range(KTILES):
                rows = tokens_of(t)[1]
                if t % 2 == 0:
                    n = min(2, KTILES - t)
                    refine(rows, t, n, 1.0 / D, RX)
                normalise(N_U, t, XALL[0:rows, t, :], RX[0:rows, t:t + 1], rows)
            v.wait_ge(S["vec_t"], 1)
            v.tensor_copy(VEC[:, :, :], PB[:, 7, 0:3 * VROWS].rearrange("p (i m) -> p i m", i=3)).then_inc(S["vec_done"], 1)

            v.wait_ge(S["nt_free"], KTILES)

            def fold_lo(j):
                h, k = divmod(j, KT)
                n = FOLD + 1 - 2 * h
                v.wait_ge(S["fold_hi"], j + 1)
                v.tensor_tensor(AF[:, 1, k, FOLDS * h:FOLDS * h + n], FSUM[:, j % 2, 0:n],
                                plain(AF[:, 0, k, FOLDS * h:FOLDS * h + n]), ALU.subtract).then_inc(S["fold_done"], 1)

            for j in range(2 * KT):
                h, k = divmod(j, KT)
                if j >= 2:
                    v.wait_ge(S["fold_done"], j - 1)
                if h == 0:
                    link(v.tensor_copy(FSUM[:, j % 2, 0:FOLD + 1:FOLD], UT[:, k, 0:FOLD + 1:FOLD]))
                v.tensor_tensor(FSUM[:, j % 2, 1 - h:FOLD - h], UT[:, k, 1:FOLD], UT[:, k, POS - 1:FOLD:-1],
                                ALU.subtract if h else ALU.add).then_inc(S["fold_sum"], 1)
                if j:
                    fold_lo(j - 1)
            fold_lo(2 * KT - 1)
            v.wait_ge(S["fold_done"], 2 * KT)
            v.memset(plain(FC[:, :, :, NF - 1, :]), 0.0).then_inc(S["fpad"], 1)
            for i in range(2):
                v.wait_ge(S["cw_hi"], i + 1)
                v.tensor_tensor(CW[:, 1, i, :, :], PB[:, i, :].rearrange("p (j n) -> p j n", j=4),
                                plain(CW[:, 0, i, :, :]), ALU.subtract).then_inc(S["cw_done"], 1)
            v.wait_ge(S["tail_hi"], 1)
            v.tensor_tensor(TAIL[:, 1, :, :], TAILR[:, :, :], plain(TAIL[:, 0, :, :]), ALU.subtract).then_inc(S["tail_done"], 1)
            v.wait_ge(S["rope_in"], 48)
            link(v.tensor_scalar(GAINS[:, 0, :], GAINS[:, 0, :], -DH ** -0.5, None, ALU.mult))
            for q in range(2):
                gain = GAINS[:, q, :].unsqueeze(1).broadcast_to([P, KTILES, DH])
                swapped = GAINS[:, q, :].rearrange("p (f e) -> p f e", e=2)[:, :, ::-1].unsqueeze(1)\
                    .broadcast_to([P, KTILES, DH // 2, 2])
                v.tensor_tensor(ROPE[:, 2 * q, :, :], ROPER[:, 0, :, :], gain, ALU.mult)
                mark(v.tensor_tensor(ROPE[:, 2 * q + 1, :, :].rearrange("p t (f e) -> p t f e", e=2),
                                     ROPER[:, 1, :, :].rearrange("p t (f e) -> p t f e", e=2), swapped, ALU.mult))
            v.wait_ge(S["fpad"], 1)
            for u in range(2 * NF):
                h, _, rows = folded(u)
                v.wait_ge(S["tm_hi"], u + 1)
                v.tensor_tensor(FC[0:rows, 1, h, u % NF, :], PB[0:rows, tm_bank(T_FIN + u), :],
                                plain(FC[0:rows, 0, h, u % NF, :]), ALU.subtract).then_inc(S["tm_free"], 1)
            for h in range(2):
                for m in range(8):
                    n = T_DFT + 16 * h + m
                    v.wait_ge(S["tm_hi"], 2 * NF + 8 * h + m + 1)
                    v.tensor_tensor(DE[:, 1, m // 4, m % 4, :], PB[:, tm_bank(n), 0:HALF],
                                    plain(DE[:, 0, m // 4, m % 4, :]), ALU.subtract).then_inc(S["tm_free"], 1)
                skip = META - 1 if h == 0 else 0
                drop = 0 if h == 0 else 1
                for j in range(4):
                    n = T_DFT + 16 * h + 8 + 2 * j
                    ready(n + 1)
                    v.wait_ge(S["ch_a"], 4 * h + j + 1)
                    k0 = 1 + HALF * h
                    v.tensor_tensor(FT1[:, j, k0 + skip - META:k0 + HALF - META], CHA[:, j % 2, skip:HALF],
                                    PB[:, tm_bank(n + 1), skip:HALF], ALU.subtract).then_inc(S["tm_free"], 1)
                    last = POS - k0 - META
                    v.tensor_tensor(FT1[:, j, last:last - (HALF - drop):-1], CHA[:, j % 2, 0:HALF - drop],
                                    PB[:, tm_bank(n + 1), 0:HALF - drop], ALU.add).then_inc(S["tm_free"], 1)
            for t in range(KTILES + 1):
                if t < KTILES:
                    rows = tokens_of(t)[1]
                    n = N_A1 + t
                    v.wait_ge(S[f"nt_in{n % 2}"], 16 * (t // 2 + 1))
                    normalise(N_A1, t, XIN[N_A1][0:rows, n % 2, :], RX[0:rows, t:t + 1], rows)
                if t:
                    lo_of_tile(N_A1 + t - 1, A1, *tokens_of(t - 1))

            for f in range(4):
                e = GE[:, f % 2, :]
                v.wait_ge(S["gate_sig"], f + 1)
                v.tensor_tensor(e, pair(f), e, ALU.mult).then_inc(S["fm_free"], 1)
                v.wait_ge(S["fm_free"], f + 1)
                v.tensor_tensor(FT1[:, f, :], FT1[:, f, :], e, ALU.mult).then_inc(S["gate_out"], 1)

            v.wait_ge(S["gate_stored"], 48)
            v.memset(plain(VV[:, TT, :, :]), 0.0).then_inc(S["vv_set"], 1)
            v.memset(plain(VV[:, 0:TT, :, DH:2 * DH]), 1.0).then_inc(S["vv_set"], 1)
            v.wait_ge(S["vv_set"], 1)
            v.memset(plain(VV[0:META, TT, :, DH:2 * DH]), 1.0).then_inc(S["vv_set"], 1)

            def head_sums(m, rows, nh):
                col = 8 * (m % 2)
                v.wait_ge(S["pr_sq"], m + 1)
                v.reduce_sum(SS[0:rows, col:col + nh], SQ[0:rows, m % 2, 0:nh * DH].rearrange("p (g d) -> p g d", d=DH),
                             AX).then_inc(S["rs_ss"], 1)

            def rotate(n, m, q, t, rows, nh):
                w, col = nh * DH, 8 * (m % 2)
                heads = lambda b: b.rearrange("p (g d) -> p g d", d=DH)
                pairs = lambda b: b.rearrange("p (g f e) -> p g f e", f=DH // 2, e=2)
                refine(rows, col, nh, 1.0 / DH, RSTD)
                v.tensor_tensor(heads(YN[0:rows, 0:w]), heads(PB[0:rows, tm_bank(n), 0:w]),
                                RSTD[0:rows, col:col + nh].unsqueeze(2).broadcast_to([rows, nh, DH]),
                                ALU.mult).then_inc(S["tm_free"], 1)
                v.wait_ge(S["tm_free"], n + 1)
                mark(v.tensor_tensor(heads(YC[0:rows, 0:w]), heads(YN[0:rows, 0:w]),
                                     ROPE[0:rows, 2 * q, t, :].unsqueeze(1).broadcast_to([rows, nh, DH]), ALU.mult))
                link(v.tensor_tensor(pairs(YS[0:rows, 0:w]), pairs(YN[0:rows, 0:w])[:, :, :, ::-1],
                                     ROPE[0:rows, 2 * q + 1, t, :].rearrange("p (f e) -> p f e", e=2).unsqueeze(1)
                                     .broadcast_to([rows, nh, DH // 2, 2]), ALU.mult))
                if m >= 2:
                    v.wait_ge(S["pr_t"], m - 1)
                elif m == 0:
                    v.wait_ge(S["f_gate_last"], 16)
                v.tensor_tensor(RQ[0:rows, m % 2, 0:w], YC[0:rows, 0:w], YS[0:rows, 0:w], ALU.add).then_inc(S["pr_rope"], 1)

            for u in range(KTILES + 1):
                if u < KTILES:
                    rows = tokens_of(u)[1]
                    head_sums(u, rows, KV_HEADS)
                    v.wait_ge(S["kv_vhi"], u + 1)
                    mark(v.tensor_tensor(VV[0:rows, u, :, 2 * DH:3 * DH],
                                         PB[0:rows, tm_bank(T_KV + u), P:2 * P].rearrange("p (g d) -> p g d", g=KV_HEADS),
                                         plain(VV[0:rows, u, :, 0:DH]), ALU.subtract))
                    rotate(T_KV + u, u, 1, u, rows, KV_HEADS)
                if u:
                    first, rows = tokens_of(u - 1)
                    v.wait_ge(S["kv_khh"], 2 * u)
                    for x in range(2):
                        v.tensor_tensor(KLL[DH * x:DH * x + DH, :, first:first + rows],
                                        pair_tiles((u - 1) % 2)[0:DH, 0:KV_HEADS, 0:rows],
                                        plain(KHH[0:DH, :, first:first + rows]), ALU.subtract).then_inc(S["kv_kll"], 1)
            v.wait_ge(S["kv_kll"], 2 * KTILES)
            for b in (KHH, KLL):
                v.tensor_copy(b[:, :, POS:KEYS], plain(b[:, :, 0:KEYS - POS])).then_inc(S["kdup"], 1)
            for u in range(TT + 1):
                if u < TT:
                    head_sums(KTILES + u, P, HEADS)
                    rotate(T_Q + u, KTILES + u, 0, u, P, HEADS)
                if u:
                    cols = slice(P * (u - 1), P * u)
                    v.wait_ge(S["pr_hi"], u)
                    v.tensor_tensor(QS[DH:P, :, cols], pair_tiles((u - 1) % 2)[0:DH, :, :], plain(QS[0:DH, :, cols]),
                                    ALU.subtract).then_inc(S["pr_done"], 1)
            for f in range(4):
                e = GE2[:, f % 2, :]
                v.wait_ge(S["gate_sig"], 4 + f + 1)
                v.tensor_tensor(e, pair(A_GATE_PAIRS[f]), e, ALU.mult).then_inc(S["fm_free"], 1)
                v.wait_ge(S["fm_free"], 4 + f + 1)
                v.tensor_scalar(e, e, 1.0, None, ALU.mult).then_inc(S["gate_out"], 1)

            def probs_lo(i, groups=range(3)):
                t = i % 4
                for g in groups:
                    rows = P if g < 2 else META
                    kts = slice(4 * g, min(4 * g + 4, KTILES))
                    v.wait_ge(S["pt_hi"], 3 * i + g + 1)
                    v.tensor_tensor(PT[0:rows, 1, kts, P * t:P * t + P],
                                    PB[0:rows, 3 + g, 0:P * (4 if g < 2 else 1)].rearrange("p (k n) -> p k n", n=P),
                                    plain(PT[0:rows, 0, kts, P * t:P * t + P]), ALU.subtract).then_inc(S["pt_lo"], 1)

            def attended(p):
                row, col, buf = pair_place(p)
                b = p // 2
                v.wait_ge(S["o_inv"], p + 1)
                if p == 0:
                    v.wait_ge(S["gate_stored"], 112)
                if p >= 4:
                    v.wait_ge(S["o_lo"], p - 3)
                link(v.tensor_tensor(OT[row, buf, :], PB[0:DH, 6 + p % 2, 0:PAIR],
                                     RC[:, PAIR * (p % 2):PAIR * (p % 2) + PAIR], ALU.mult))
                v.wait_ge(S[f"ag_in{b % 2}"], 16 * (b // 2 + 1))
                v.tensor_tensor(OT[row, buf, :], OT[row, buf, :], AG[row, b % 2, PAIR * (p % 2):PAIR * (p % 2) + PAIR],
                                ALU.mult).then_inc(S["o_out"], 1)

            def attended_lo(p):
                row, col, buf = pair_place(p)
                v.wait_ge(S["o_hi"], p + 1)
                v.tensor_tensor(MIXA[row, 1, p // 8, col], OT[row, buf, :], plain(MIXA[row, 0, p // 8, col]),
                                ALU.subtract).then_inc(S["o_lo"], 1)

            for i in range(HEADS * TT):
                v.wait_ge(S["sc_mm"], i + 1)
                v.tensor_reduce(NB[:, i % 2:i % 2 + 1], PB[:, 0:3, 0:KPART], mybir.AxisListType.XY,
                                ALU.min).then_inc(S["sc_max"], 1)
                if i == 0:
                    v.wait_ge(S["w_used"], C_OUT)
                    v.memset(plain(PT[:, :, KTILES - 1, :]), 0.0).then_inc(S["pt_zero"], 1)
                    v.wait_ge(S["pt_zero"], 1)
                if i:
                    probs_lo(i - 1, range(2))
                if i >= 6 and i % 2 == 0:
                    attended((i - 6) // 2)
                if i >= 9 and i % 2:
                    attended_lo((i - 9) // 2)
                if i:
                    probs_lo(i - 1, range(2, 3))
            probs_lo(HEADS * TT - 1)
            attended(PAIRS - 3)
            attended(PAIRS - 2)
            attended_lo(PAIRS - 4)
            attended_lo(PAIRS - 3)
            attended(PAIRS - 1)
            for f in range(4):
                if f >= 2:
                    attended_lo(PAIRS - 4 + f)
                v.wait_ge(S["mf_hi"], f + 1)
                v.tensor_tensor(MIXF[:, 1, f, :], MFR[:, f, :], plain(MIXF[:, 0, f, :]), ALU.subtract).then_inc(S["mf_done"], 1)
            v.wait_ge(S["mf_done"], 4)

            def residual(m):
                c, u = divmod(m, TT)
                ready(T_OUT + m)
                v.wait_ge(S[f"op_in{m % 2}"], 16 * (m // 2 + 1))
                v.tensor_tensor(H[:, u, FW * c:FW * c + FW], PB[:, tm_bank(T_OUT + m), :], XR[:, m % 2, :],
                                ALU.add).then_inc(S["tm_free"], 1)

            for m in range(TT):
                residual(m)
            v.wait_ge(S["gains_in"], 32)
            for s in range(TT + LAG):
                if s < TT:
                    residual(TT + s)
                if 2 <= s < TT + 2:
                    t = s - 2
                    normalise(N_A2, t, H[:, t, :], RX[:, 8 + t:9 + t])
                if s >= LAG:
                    lo_of_tile(N_A2 + s - LAG, A2, P * (s - LAG))
                refine_pair(s)
                if s < TT:
                    v.scalar_tensor_tensor(out=H[:, s, :], in0=H[:, s, :], scalar=RX[:, s:s + 1], in1=GF[:, :],
                                           op0=ALU.mult, op1=ALU.mult).then_inc(S["x1_out"], 1)
            v.wait_ge(S["x1_stored"], 16 * TT)
            for u in range(TT):
                n = T_V2 + u
                v.wait_ge(S["tm_hi"], 2 * NF + 16 + u + 1)
                v.tensor_tensor(V2[:, 1, u, :], PB[:, tm_bank(n), :], plain(V2[:, 0, u, :]), ALU.subtract)\
                 .then_inc(S["tm_free"], 1)

            def exponent(i, between):
                n = P * (stick_tile(i) + 1)
                z, l, s = pair(i % 2)[:, 0:n], ZL[:, i % 2, 0:n], ZS[:, i % 2, 0:n]
                v.wait_ge(S["z_l"], i + 1)
                if i >= 2:
                    v.wait_ge(S["wt_mm"], turned(i - 1))
                count = mark(v.scalar_tensor_tensor(out=s, in0=z, scalar=0.0, in1=l, op0=ALU.max, op1=ALU.add))
                between()
                v.wait_ge(S["v_chain"], count)
                link(v.tensor_tensor_scan(ZL[:, i % 2, n - 1::-1], ONES[:, 0:n], ZS[:, i % 2, n - 1::-1], 0.0,
                                          ALU.mult, ALU.add))
                v.tensor_tensor(s, z, l, ALU.subtract).then_inc(S["z_e"], 1)

            def weights_lo(i, g):
                t = stick_tile(i)
                c = i // 2 % 2 * 2 + t % 2
                if i >= 0 and g <= t // 4:
                    n = turned(i) + g
                    w = min(4, t + 1 - 4 * g)
                    v.wait_ge(S["wt_hi"], n + 1)
                    v.tensor_tensor(WT[:, 1, 4 * g:4 * g + w, P * c:P * c + P],
                                    PB[:, 4 + n % 2, 0:P * w].rearrange("p (k n) -> p k n", n=P),
                                    plain(WT[:, 0, 4 * g:4 * g + w, P * c:P * c + P]), ALU.subtract).then_inc(S["wt_lo"], 1)

            def normalise_x1(t):
                if t == 0:
                    v.wait_ge(S["gains_in"], 48)
                v.wait_ge(S[f"x_in{t}"], 32)
                v.scalar_tensor_tensor(out=X1N[:, t, :], in0=X1N[:, t, :], scalar=RX[:, 8 + t:9 + t], in1=GB[N_A3][:, :],
                                       op0=ALU.mult, op1=ALU.mult).then_inc(S["nt_xn"], 1)

            def attended2(p):
                row = slice(DH * (p // 4 % 2), DH * (p // 4 % 2) + DH)
                col = P * (stick_tile(2 * p) // 2 * 2)
                v.wait_ge(S["av2_mm"], p + 1)
                v.tensor_copy(AT[row, p // 8, col:col + PAIR], PB[0:DH, 6 + p % 2, 0:PAIR])\
                 .then_inc(S["at_out"], 1)

            v.wait_ge(S["st_a"], 3)
            v.tensor_tensor(QS2[0][DH:P, :], QT[0:DH, 0, :], plain(QS2[0][0:DH, :]), ALU.subtract).then_inc(S["st_v"], 1)
            v.wait_ge(S["st_a"], 4)
            for q in range(2):
                v.tensor_tensor(KLL2[0][DH * q:DH * q + DH, :], KT2[0:DH, 0, :], plain(KHH2[0][0:DH, :]),
                                ALU.subtract).then_inc(S["st_v"], 1)
            v.wait_ge(S["w_used"], C_CONV)
            v.memset(ONES[:, :], 1.0).then_inc(S["ones_set"], 1)
            v.wait_ge(S["ones_set"], 1)
            for i in range(HEADS * TT + 2):
                if i < HEADS * TT:
                    exponent(i, lambda: weights_lo(i - 2, 0))
                else:
                    weights_lo(i - 2, 0)
                weights_lo(i - 2, 1)
                if i >= 6 and i % 2 == 0:
                    attended2((i - 6) // 2)
                if i >= HEADS * TT - 6:
                    normalise_x1(i - HEADS * TT + 6)
            attended2(PAIRS - 2)
            attended2(PAIRS - 1)

            for t in range(TT):
                lo_of_tile(N_A3 + t, A2, P * t)
            for f in range(4):
                v.wait_ge(S["at_hi"], f + 1)
                v.tensor_tensor(ATS[:, 1, f, :], AT[:, f, :], plain(ATS[:, 0, f, :]), ALU.subtract).then_inc(S["at_done"], 1)

            v.wait_ge(S["at_done"], 4)
            v.memset(PROD[:, 0:2], 0.0).then_inc(S["cv_pad"], 1)
            v.wait_ge(S["cv_pad"], 1)
            nf = 2 * FT
            for f in range(5):
                if f < 4:
                    u = U_CONV + 3 * f
                    v.wait_ge(S["w_used"], C_CONV + 3 * f + 2)
                    v.wait_ge(S["cv_cc"], f + 1)
                    v.tensor_tensor(PROD[:, 2:N_TOK + 2], pair((u + 1) % 4), CCB[:, :], ALU.mult).then_inc(S["fm_free"], 1)
                    v.wait_ge(S["fm_free"], u + 1)
                    v.tensor_scalar(CY[:, :], PROD[:, 2:N_TOK + 2], VEC[:, 2, nf + f:nf + f + 1], None,
                                    ALU.mult).then_inc(S["fm_free"], 1)
                    v.wait_ge(S["fm_free"], u + 2)
                    for i in (1, 0):
                        link(v.scalar_tensor_tensor(out=CY[:, :], in0=PROD[:, i:N_TOK + i], scalar=VEC[:, i, nf + f:nf + f + 1],
                                                    in1=CY[:, :], op0=ALU.mult, op1=ALU.add))
                if f:
                    v.wait_ge(S["cv_hi"], f)
                    v.tensor_tensor(CTS[:, 1, f - 1, :], CO[:, :], plain(CTS[:, 0, f - 1, :]), ALU.subtract).then_inc(S["cv_done"], 1)
                    v.wait_ge(S["cv_done"], f)
                if f < 4:
                    v.wait_ge(S["w_used"], C_CONV + 3 * f + 3)
                    v.tensor_tensor(CO[:, :], pair((u + 2) % 4), CY[:, :], ALU.mult).then_inc(S["fm_free"], 1)
                    v.wait_ge(S["fm_free"], u + 3)

            def merged_lo(i):
                f = MERGED_ORDER[i]
                v.wait_ge(S["mr_hi"], i + 1)
                v.tensor_tensor(MR[:, 1, f, :], merged_tile(f), plain(MR[:, 0, f, :]), ALU.subtract).then_inc(S["mr_done"], 1)

            for f in range(KT):
                u = U_MRG + 4 * f
                v.wait_ge(S["fm_free"], u + 2)
                if f == KT - 1:
                    for i in range(KT - 1):
                        merged_lo(i)
                v.wait_ge(S["w_used"], C_MRG + 3 * f + 3)
                for g in range(2):
                    v.tensor_tensor(MGE[:, g, :], pair((u + 2 + g) % 4), MGE[:, g, :], ALU.mult).then_inc(S["fm_free"], 1)
                v.wait_ge(S["fm_free"], u + 4)
                if f >= 6:
                    v.wait_ge(S[f"mg_st{f % 2}"], 16)
                v.tensor_tensor(MGO[f % 6][:, :], MGE[:, 0, :], MGE[:, 1, :], ALU.add).then_inc(S["mg_out"], 1)
            merged_lo(KT - 1)

            v.wait_ge(S["gains2_in"], 32)
            for s in range(TT + LAG):
                refine_pair(s)
                if s < TT:
                    link(v.scalar_tensor_tensor(out=Y[:, s, :], in0=Y[:, s, :], scalar=RX[:, s:s + 1], in1=GP[:, :],
                                                op0=ALU.mult, op1=ALU.mult))
                    v.wait_ge(S[f"xr_in{s % 2}"], 16 * (s // 2 + 1))
                    v.tensor_tensor(Y[:, s, :], Y[:, s, :], XRR[:, s % 2, :], ALU.add).then_inc(S["x2_out"], 1)
                if 1 <= s <= TT:
                    t = s - 1
                    normalise(N_A4, t, Y[:, t, :], RX[:, 8 + t:9 + t])
                if s >= LAG:
                    lo_of_tile(N_A4 + s - LAG, A4, P * (s - LAG))

            v.sem_inc(S["up_f"], 1)
            def up_steps(i, last):
                for s in range(4):
                    q, g = divmod(s, 2)
                    if last and s == 3:
                        mid_lo(0, 0, 0)
                        mid_lo(0, 1, 1)
                    up = pair((s + 2) % 4)
                    w1, w0 = (VEC[:, x, bass.ds(i * 2 + (q + FT * g), 1)] for x in (1, 0))
                    v.wait_ge(S["up_c"], i * 4 + (s + 1))
                    v.scalar_tensor_tensor(out=UB[:, g, 1:N_TOK], in0=up[:, 0:N_TOK - 1], scalar=w1,
                                           in1=UB[:, g, 1:N_TOK], op0=ALU.mult, op1=ALU.add).then_inc(S["up_s"], 1)
                    v.wait_ge(S["up_s"], i * 4 + (s + 1))
                    v.scalar_tensor_tensor(out=UB[:, g, 2:N_TOK], in0=up[:, 0:N_TOK - 2], scalar=w0,
                                           in1=UB[:, g, 2:N_TOK], op0=ALU.mult, op1=ALU.add).then_inc(S["fm_free"], 1)
                    if g:
                        v.wait_ge(S["up_g"], i * 2 + (q + 1))
                        v.tensor_tensor(FFT[:, bass.ds(i * 2 + q, 1), :].rearrange("p a n -> p (a n)"), UB[:, 0, :],
                                        UB[:, 1, :], ALU.mult).then_inc(S["up_f"], 1)

            def mid_lo(half, j, s):
                v.wait_ge(S["dn_hi"], j + (FT * half + 1))
                src = FFT[:, j, FW * half:FW * half + FW] if isinstance(j, int) else \
                    FFT[:, bass.ds(j, 1), FW * half:FW * half + FW].rearrange("p a n -> p (a n)")
                v.tensor_tensor(FS[:, s, 1, :], src, plain(FS[:, s, 0, :]), ALU.subtract).then_inc(S["dn_lo"], 1)

            with v.Fori(0, FT // 2 - 1) as i:
                up_steps(i, False)
            up_steps(FT // 2 - 1, True)

            def finish(half, s):
                m = 4 * half + s
                refine(P, s, 1, 1.0 / D, RSTD)
                link(v.scalar_tensor_tensor(out=Y2[:, s, :], in0=Y2[:, s, :], scalar=RSTD[:, s:s + 1],
                                            in1=GL[:, :], op0=ALU.mult, op1=ALU.mult))
                v.wait_ge(S[f"xf_in{m % 2}"], 16 * (m // 2 + 1))
                v.tensor_tensor(Y2[:, s, :], Y2[:, s, :], XF[:, m % 2, :], ALU.add).then_inc(S["f_out"], 1)

            v.wait_ge(S["gains3_in"], 16)
            v.wait_ge(S["up_f"], FT + 1)
            for half in range(2):
                if half:
                    mid_lo(1, 1, 1)
                    for s in range(6):
                        if 1 <= s < 5:
                            finish(0, s - 1)
                        mid_lo(1, s + 2, s % 2)
                with v.Fori(4 if half else 1, FT // 2) as i:
                    for s in range(2):
                        mid_lo(half, i * 2 + s, s)
                if half:
                    v.wait_ge(S["f_stored"], 64)
                else:
                    mid_lo(1, 0, 0)
                for t in range(4):
                    down_ready(v, half, t)
                    v.tensor_copy(Y2[:, t, FW:D], PB[:, 2 * t + 1, :]).then_inc(S["dn_yv"], 1)
            for s in range(4):
                finish(1, s)


N_CONSTS = 2


def weight_chunks(a, const):
    def token_major(w, first, n):
        per = WCH // n
        v = w.rearrange("(k p) n -> p k n", p=P)
        return [(WCH, [(0, v[:, per * j:per * j + per, first:first + n])]) for j in range(KT // per)]

    def feature_tile(w, first):
        return (WCH, [(0, w.rearrange("(k p) n -> p k n", p=P)[:, :, first:first + P])])

    w1, w2 = a["w_in"][0], a["w_in_2"][0]
    out = token_major(w1, 0, FW)
    out += [(SLOT, [(0, const["dft_main"][i])]) for i in range(4)]
    out += [feature_tile(w1, FW + P * f) for f in range(4)]
    out += token_major(w1, 1536, 256) + token_major(w1, 1024, FW)
    out += [feature_tile(w1, GATE1 + P * f) for f in range(4)]
    out += token_major(a["w_out"][0], 0, FW) + token_major(a["w_out"][0], FW, FW)
    out += token_major(w2, 1024, FW)
    out += [feature_tile(w2, P * f) for f in range(8)]
    for f in range(4):
        out += [feature_tile(w2, c + P * f) for c in (2048, 2560, 1536)]
    branches = [a[k][0].rearrange("(k p) n -> p k n", p=P) for k in ("w_att_branch_2", "w_conv_branch_2")]
    for f in range(KT):
        out += [feature_tile(w2, 3072 + P * f), feature_tile(w2, 4096 + P * f)]
        out.append((WCH, [(FW * i, b[:, :, P * f:P * f + P]) for i, b in enumerate(branches)]))
    out += token_major(a["w_out_2"][0], 0, FW) + token_major(a["w_out_2"][0], FW, FW)
    assert len(out) == C_UP
    return out


def constants():
    ident = np.eye(P, dtype=np.float32)
    q, k = np.arange(P)[:, None], np.arange(P)[None, :]
    causal = np.where(k < q, 0.0, NEG).astype(np.float32)
    grid, axis = 64, 16
    j = np.arange(N_TOK)
    row, col = j // grid - (N_TOK // grid) // 2, j % grid - grid // 2
    freqs = 1.0 / (10000.0 ** (np.arange(axis) * 2.0 / (2 * axis)))
    ang = np.concatenate([row[:, None] * freqs, col[:, None] * freqs], axis=-1)
    cos, sin = np.repeat(np.cos(ang), 2, axis=1), np.repeat(np.sin(ang), 2, axis=1)
    sin[:, 0::2] *= -1.0
    rope = np.zeros((P, 2, KTILES, DH), np.float32)
    rope[:, 0, TT] = 1.0
    for t in range(TT):
        rope[:, 0, t], rope[:, 1, t] = cos[P * t:P * t + P], sin[P * t:P * t + P]
    c = np.arange(DH)
    ang = 2 * np.pi * (np.outer(c, c) % DH) / DH
    channel = np.zeros((P, 2, P), np.float32)
    for g in range(2):
        s = slice(DH * g, DH * g + DH)
        channel[s, 0, s], channel[s, 1, s] = np.cos(ang), np.sin(ang)
    main = np.zeros((4, P, 4, HALF), np.float64)
    tail = np.zeros((P, 4, HALF), np.float64)
    for h in range(2):
        freq = 1 + HALF * h + np.arange(HALF)
        for kind in range(2):
            n = np.arange(FOLD + 1) if kind == 0 else np.arange(1, FOLD)
            ang = 2 * np.pi * (np.outer(n, freq) % POS) / POS
            table = (np.sin(ang) if kind else np.cos(ang)) / np.sqrt(POS * DH)
            main[2 * h + kind] = table[:4 * P].reshape(4, P, HALF).transpose(1, 0, 2)
            tail[:len(n) - 4 * P, 2 * h + kind] = table[4 * P:]
    return {"ident": ident, "causal": causal, "rope": rope, "channel": channel,
            "dft_main": main.reshape(4, P, SLOT).astype(np.float32), "dft_tail": tail.astype(np.float32)}


_INS = ["x", "meta_tokens", "norm_g", "w_in", "w_fmix", "b_fmix", "q_norm_g", "k_norm_g", "w_out", "final_g",
        "norm_mix_pre_2", "w_in_2", "conv_mix_w_2", "w_att_branch_2", "w_conv_branch_2", "w_out_2",
        "norm_mix_post_2", "norm_ffn_pre_2", "w_up_2", "conv_ffn_w_2", "w_down_2", "norm_ffn_post_2"]
_SCRATCH = {"mixed_f": (512, N_TOK), "a_gate": (512, N_TOK), "x1": (N_TOK, D), "merged": (2 * P, N_TOK), "x2": (N_TOK, D)}


def kernel(**inputs):
    import concourse.bacc as bacc
    from concourse.bass_utils import run_bass_kernel_spmd

    nc = bacc.Bacc("TRN2", target_bir_lowering=False, num_devices=1)
    arrays, a, const = {}, {}, {}
    for name in _INS:
        array = np.ascontiguousarray(inputs[name])
        arrays[f"in_{name}"] = array
        a[name] = nc.dram_tensor(f"in_{name}", array.shape, mybir.dt.from_np(array.dtype), kind="ExternalInput").ap()
    for name, array in constants().items():
        arrays[f"const_{name}"] = array
        const[name] = nc.dram_tensor(f"const_{name}", array.shape, F32, kind="ExternalInput").ap()
    scratch = {name: nc.dram_tensor(f"scratch_{name}", shape, F32, kind="Internal").ap()
               for name, shape in _SCRATCH.items()}
    out = nc.dram_tensor("out_0", (1, N_TOK, D), F32, kind="ExternalOutput").ap()
    two_block_kernel(nc, a, const, scratch, out)
    r = run_bass_kernel_spmd(nc, [arrays], core_ids=[0])
    return r.results[0]["out_0"]
```
